# Optimizing a Trainium2 kernel written in Bass

```python
import jax, jax.numpy as jnp
from jax import lax
import numpy as np

D_MODEL = 1024
BATCH = 1
SEQ = 256
DEPTH = 2
DEC_BATCH = 8
DEC_SEQ = 16
PAST_LEN = 256

CHUNK = 64
MIX_WIDTH = D_MODEL
CONV_CH = 512
CONV_K = 31
POOL_CH = MIX_WIDTH - CONV_CH
POOL_WINDOWS = (2, 4, 8, 16)
POOL_GROUPS = 4
POOL_GC = POOL_CH // POOL_GROUPS
POOL_HIST = 15
D_FF = 2816
N_EXPERTS = 8
TOP_K = 2
EXPERT_FF = 2816
N_DENSE = (DEPTH + 1) // 2
N_MOE = DEPTH // 2
EPS = 1e-6

kernel_name = 'hybrid_conv_pool_stream_step'

def rms_norm(x, g):
    xf = x.astype(jnp.float32)
    y = xf * lax.rsqrt(jnp.mean(xf * xf, axis=-1, keepdims=True) + EPS)
    return (y * g.astype(jnp.float32)).astype(x.dtype)

def layer_norm(x, g, b):
    xf = x.astype(jnp.float32)
    mu = jnp.mean(xf, axis=-1, keepdims=True)
    xc = xf - mu
    y = xc * lax.rsqrt(jnp.mean(xc * xc, axis=-1, keepdims=True) + EPS)
    return (y * g.astype(jnp.float32) + b.astype(jnp.float32)).astype(x.dtype)

def conv_group(a_hist, a_new, conv_w, conv_b, ln_g, ln_b):
    ext = jnp.concatenate([a_hist, a_new], axis=1)
    y = lax.conv_general_dilated(ext, conv_w[:, None, :], window_strides=(1,), padding='VALID',
                                 dimension_numbers=('NWC', 'WIO', 'NWC'),
                                 feature_group_count=CONV_CH)
    y = jax.nn.silu(layer_norm(y + conv_b, ln_g, ln_b))
    return y, ext[:, -(CONV_K - 1):]

def pool_group(p_hist, p_new, pos0, pool_w, pool_scale):
    b, l, _ = p_new.shape
    ext = jnp.concatenate([p_hist, p_new], axis=1)
    cs = jnp.cumsum(ext.astype(jnp.float32), axis=1)
    cs = jnp.concatenate([jnp.zeros((b, 1, POOL_CH), jnp.float32), cs], axis=1)
    pos1 = jnp.arange(l, dtype=jnp.float32) + jnp.float32(pos0 + 1)
    means = []
    for g, w in enumerate(POOL_WINDOWS):
        sl = slice(g * POOL_GC, (g + 1) * POOL_GC)
        s = cs[:, POOL_HIST + 1:POOL_HIST + 1 + l, sl] - cs[:, POOL_HIST + 1 - w:POOL_HIST + 1 - w + l, sl]
        cnt = jnp.minimum(pos1, jnp.float32(w))[None, :, None]
        means.append(s / cnt)
    d = (jnp.concatenate(means, axis=-1) - p_new.astype(jnp.float32)).astype(p_new.dtype)
    z = jnp.einsum('blgc,gcd->blgd', d.reshape(b, l, POOL_GROUPS, POOL_GC), pool_w)
    return z.reshape(b, l, POOL_CH) * pool_scale, ext[:, -POOL_HIST:]

def mixer_layer(x, conv_hist, pool_hist, pos0, norm_g, w_in, conv_w, conv_b, ln_g, ln_b, pool_w, pool_scale, w_out):
    h = rms_norm(x, norm_g)
    u = jnp.einsum('bld,de->ble', h, w_in)
    a = u[..., :CONV_CH] * jax.nn.sigmoid(u[..., CONV_CH:2 * CONV_CH])
    c, new_conv = conv_group(conv_hist, a, conv_w, conv_b, ln_g, ln_b)
    z, new_pool = pool_group(pool_hist, u[..., 2 * CONV_CH:], pos0, pool_w, pool_scale)
    mix = jnp.einsum('ble,ed->bld', jnp.concatenate([c, z], axis=-1), w_out)
    return x + mix, new_conv, new_pool

def swiglu(h, wg, wu, wd):
    return jnp.einsum('blf,fd->bld', jax.nn.silu(jnp.einsum('bld,df->blf', h, wg)) * jnp.einsum('bld,df->blf', h, wu), wd)

def moe_swiglu(h, router_w, router_b, wg, wu, wd):
    logits = jnp.einsum('bld,de->ble', h, router_w).astype(jnp.float32) + router_b.astype(jnp.float32)
    top_v, top_i = lax.top_k(logits, TOP_K)
    top_p = jax.nn.softmax(top_v, axis=-1)
    gates = jnp.sum(jax.nn.one_hot(top_i, N_EXPERTS, dtype=jnp.float32) * top_p[..., None], axis=-2)
    out = jnp.zeros_like(h)
    for e in range(N_EXPERTS):
        out = out + gates[..., e:e + 1].astype(h.dtype) * swiglu(h, wg[e], wu[e], wd[e])
    return out

def trunk(x, conv_hist, pool_hist, pos0, weights):
    (norm_mix, w_in, conv_w, conv_b, conv_ln_g, conv_ln_b, pool_w, pool_scale, w_out, norm_ffn,
     dense_w_gate, dense_w_up, dense_w_down, router_w, router_b, moe_w_gate, moe_w_up, moe_w_down, norm_final) = weights
    new_conv, new_pool = [], []
    for l in range(DEPTH):
        x, nc, npl = mixer_layer(x, conv_hist[l], pool_hist[l], pos0, norm_mix[l], w_in[l], conv_w[l], conv_b[l],
                                 conv_ln_g[l], conv_ln_b[l], pool_w[l], pool_scale[l], w_out[l])
        new_conv.append(nc)
        new_pool.append(npl)
        h = rms_norm(x, norm_ffn[l])
        j = l // 2
        if l % 2 == 0:
            x = x + swiglu(h, dense_w_gate[j], dense_w_up[j], dense_w_down[j])
        else:
            x = x + moe_swiglu(h, router_w[j], router_b[j], moe_w_gate[j], moe_w_up[j], moe_w_down[j])
    return rms_norm(x, norm_final), jnp.stack(new_conv), jnp.stack(new_pool)

def setup_inputs(seed: int = 0) -> dict:
    key = jax.random.key(seed)
    ks = jax.random.split(key, 24)
    f32 = jnp.float32

    def nrm(k, shape, s):
        return s * jax.random.normal(k, shape, f32)

    return {
        'x_prompt': nrm(ks[0], (BATCH, SEQ, D_MODEL), 1.0),
        'x_sample': nrm(ks[1], (DEC_BATCH, DEC_SEQ, D_MODEL), 1.0),
        'state_conv': nrm(ks[2], (DEPTH, DEC_BATCH, CONV_K - 1, CONV_CH), 0.5),
        'state_pool': nrm(ks[3], (DEPTH, DEC_BATCH, POOL_HIST, POOL_CH), 1.0),
        'norm_mix': 1.0 + nrm(ks[4], (DEPTH, D_MODEL), 0.05),
        'w_in': nrm(ks[5], (DEPTH, D_MODEL, 2 * CONV_CH + POOL_CH), D_MODEL ** -0.5),
        'conv_w': nrm(ks[6], (DEPTH, CONV_K, CONV_CH), CONV_K ** -0.5),
        'conv_b': nrm(ks[7], (DEPTH, CONV_CH), 0.02),
        'conv_ln_g': 1.0 + nrm(ks[8], (DEPTH, CONV_CH), 0.05),
        'conv_ln_b': nrm(ks[9], (DEPTH, CONV_CH), 0.02),
        'pool_w': nrm(ks[10], (DEPTH, POOL_GROUPS, POOL_GC, POOL_GC), POOL_GC ** -0.5),
        'pool_scale': 1.0 + nrm(ks[11], (DEPTH, POOL_CH), 0.1),
        'w_out': nrm(ks[12], (DEPTH, MIX_WIDTH, D_MODEL), MIX_WIDTH ** -0.5),
        'norm_ffn': 1.0 + nrm(ks[13], (DEPTH, D_MODEL), 0.05),
        'dense_w_gate': nrm(ks[14], (N_DENSE, D_MODEL, D_FF), D_MODEL ** -0.5),
        'dense_w_up': nrm(ks[15], (N_DENSE, D_MODEL, D_FF), D_MODEL ** -0.5),
        'dense_w_down': nrm(ks[16], (N_DENSE, D_FF, D_MODEL), D_FF ** -0.5),
        'router_w': nrm(ks[17], (N_MOE, D_MODEL, N_EXPERTS), D_MODEL ** -0.5),
        'router_b': nrm(ks[18], (N_MOE, N_EXPERTS), 0.01),
        'moe_w_gate': nrm(ks[19], (N_MOE, N_EXPERTS, D_MODEL, EXPERT_FF), D_MODEL ** -0.5),
        'moe_w_up': nrm(ks[20], (N_MOE, N_EXPERTS, D_MODEL, EXPERT_FF), D_MODEL ** -0.5),
        'moe_w_down': nrm(ks[21], (N_MOE, N_EXPERTS, EXPERT_FF, D_MODEL), EXPERT_FF ** -0.5),
        'norm_final': 1.0 + nrm(ks[22], (D_MODEL,), 0.05),
    }

def reference(x_prompt, x_sample, state_conv, state_pool, norm_mix, w_in, conv_w, conv_b, conv_ln_g, conv_ln_b,
              pool_w, pool_scale, w_out, norm_ffn, dense_w_gate, dense_w_up, dense_w_down, router_w, router_b,
              moe_w_gate, moe_w_up, moe_w_down, norm_final):
    weights = (norm_mix, w_in, conv_w, conv_b, conv_ln_g, conv_ln_b, pool_w, pool_scale, w_out, norm_ffn,
               dense_w_gate, dense_w_up, dense_w_down, router_w, router_b, moe_w_gate, moe_w_up, moe_w_down, norm_final)
    bp = x_prompt.shape[0]
    zero_conv = jnp.zeros((DEPTH, bp, CONV_K - 1, CONV_CH), x_prompt.dtype)
    zero_pool = jnp.zeros((DEPTH, bp, POOL_HIST, POOL_CH), x_prompt.dtype)
    y_prompt, conv_p, pool_p = trunk(x_prompt, zero_conv, zero_pool, 0, weights)
    y_sample, conv_s, pool_s = trunk(x_sample, state_conv, state_pool, PAST_LEN, weights)
    return (y_prompt, y_sample, conv_p, pool_p, conv_s, pool_s)


_drawn_inputs = setup_inputs


def setup_inputs(seed=0):
    import zlib

    import numpy as np

    out = dict(_drawn_inputs(seed))
    spreads = {}
    factors = {}
    for name, (base, spread) in spreads.items():
        noise = np.random.default_rng([zlib.crc32(name.encode()), seed]).standard_normal(out[name].shape)
        drawn = base * np.exp(spread * noise) if base else spread * noise
        out[name] = __import__('jax').numpy.asarray(drawn.astype(out[name].dtype))
    for name, factor in factors.items():
        out[name] = (out[name] * factor).astype(out[name].dtype)
    return out
```

```python
from contextlib import ExitStack

import numpy as np

import concourse.bass as bass
from concourse import mybir

F32 = mybir.dt.float32
F32R = mybir.dt.float32r
I32 = mybir.dt.int32
ALU = mybir.AluOpType
ACT = mybir.ActivationFunctionType
AXX = mybir.AxisListType.X

P = 128
D = 1024
KD = D // P
SEQ = 256
NSEQ, DSEQ = 8, 16
TOK = SEQ + NSEQ * DSEQ
NTB = TOK // P
CH = 512
NCB = CH // P
TAPS = 31
CHIST = TAPS - 1
PHIST = 15
FF = 2816
FT = 256
NF = FF // FT
NE = 8
EPS = 1e-6
LAYERS = 2
TILE = 2048
CSEG = CHIST + DSEQ
CEXT = CHIST + SEQ + NSEQ * CSEG
PSEG = PHIST + DSEQ
PEXT = PHIST + SEQ + NSEQ * PSEG
WIN = TOK

C_MIX, C_FFN, C_CB, C_LG, C_LB, C_PS, C_CW = 0, 16, 32, 40, 48, 56, 64
NPRM = C_CW + LAYERS * TAPS * NCB

WIN_TILES = [0, 2, 1, 3, 4, 5]
WIN_BANK = [0, 1, 6, 7] * 3
WOUT_TILES = [2, 3, 0, 1]
STATES = [(True, 0, 4), (True, 4, 4), (True, 0, 0), (False, 0, 3), (False, 3, 3), (False, 6, 2), (False, 0, 0)]
NST = len(STATES)
SIDE_BANK = [[0, 1, 6, 7][i % 4] for i in range(NST + 4)]


def stored_before(i):
    return sum(max(n, 1) for j, (_, _, n) in enumerate(STATES) if j < i and j % 2 == i % 2)


STORES = [stored_before(NST + (NST % 2)), stored_before(NST + 1 - (NST % 2))]

GEN_WIN = [[0] * 6, [8, 8, 8, 7, 6, 6]]
GEN_WOUT = [[1] * 4, [9, 9, 9, 8]]
GEN_DENSE = [2, 2, 2, 2, 1, 1]
GEN_MOE = [10, 10, 10, 9, 7, 7]

DENSE_UNITS = NF * NTB
PAIRS = NE // 2


def build(nc, a):
    ctx = ExitStack()
    with ctx:
        base = 16512
        at = {}

        def place(name, floats, dt=F32, offset=None, parts=P):
            o = at["next"] if offset is None else offset
            t = nc.alloc_sbuf_tensor_at(name, [parts, floats], dt, offset=base + o)
            if offset is None:
                at["next"] = (o + floats * 4 + 31) // 32 * 32
            at[name] = o
            return t

        def sem(name):
            return ctx.enter_context(nc.semaphore(name))

        at["next"] = 0
        raw = place("raw", 6 * TILE)
        w_hi = place("w_hi", 6 * TILE, F32R)
        w_lo = place("w_lo", 6 * TILE, F32R)
        x = place("x", NTB * D)
        a_hi = place("a_hi", KD * TOK, F32R)
        a_lo = place("a_lo", KD * TOK, F32R)
        e_floats = NCB * (CEXT + PEXT)
        ext = place("ext", e_floats)
        ident = place("ident", P)
        mean_w = place("mean_w", P)
        prm = place("prm", NPRM)
        rw_hi = place("rw_hi", KD * NE, F32R)
        rw_lo = place("rw_lo", KD * NE, F32R)
        cinv = place("cinv", 16)
        stat = place("stat", 12)
        s0 = (at["next"] + 31) // 32 * 32
        hist = place("hist", 3 * CH, offset=s0)
        prm_rows = place("prm_rows", 3 * P, offset=s0)
        pool_w = place("pool_w", NCB * P, offset=s0)
        sgm = place("sgm", WIN, offset=s0 + 2048)
        win_a = place("win_a", 271, offset=s0 + 2048)
        win_b = place("win_b", 271, offset=s0 + 3136 + 32)
        stage = place("stage", 2 * CH, offset=s0 + 2048)
        ft_hi = place("ft_hi", 2 * FT, F32R, offset=s0)
        ft_lo = place("ft_lo", 2 * FT, F32R, offset=s0 + 2048)
        silu = place("silu", FT, offset=s0 + 4096)
        act_b = place("act_b", FT, offset=s0 + 5120)
        rw_raw = place("rw_raw", KD * NE, offset=s0)
        assert base + s0 + 6144 <= 229344
        oh, ol = at["a_hi"], at["a_lo"]
        pt = place("pt", NTB * P, F32R, offset=oh + 4096)
        ye_hi = place("ye_hi", D, F32R, offset=oh + 5632)
        ye_lo = place("ye_lo", D, F32R, offset=ol + 5632)
        tri = place("tri", P, offset=oh + 9728)
        lg = place("lg", NTB * NE, offset=ol + 9728)
        cmp_gt = place("cmp_gt", NE * NE, offset=ol + 9856)
        cmp_eq = place("cmp_eq", NE * NE, offset=ol + 10112)
        low = place("low", NE * NE, offset=oh + 10240)
        rank = place("rank", NTB * NE, offset=ol + 10368)
        mask = place("mask", NTB * NE, offset=ol + 10496)
        gate = place("gate", NTB * NE, offset=ol + 10624)
        rmax = place("rmax", 2 * NTB, offset=ol + 10752)
        rsum = place("rsum", 2 * NTB, offset=ol + 10784)
        post = place("post", NTB * NE, offset=ol + 10816)
        posb = place("posb", 3 * NTB * NE, offset=ol + 10944)
        rb = place("rb", NE, offset=oh + 10496)
        cnt_f = place("cnt_f", NE, offset=ol + 11232)
        cnt_i = place("cnt_i", NE, I32, offset=ol + 11264)
        h = ext[:, 0:NTB * D]
        onehot = ext[:, NTB * D:NTB * D + NTB * P]
        iota = ext[:, NTB * D + NTB * P + D:NTB * D + NTB * P + D + P]
        gbc = ext[:, NTB * D + NTB * P:NTB * D + NTB * P + D]

        ps = ctx.enter_context(nc.psum_tensor("ps", [P, 8, 512], F32))

        def cext(c):
            return ext[:, c * CEXT:(c + 1) * CEXT]

        def pext(g):
            o = NCB * CEXT + g * PEXT
            return ext[:, o:o + PEXT]

        def c_sample(c, off, n):
            return cext(c)[:, CHIST + SEQ:].rearrange("p (s t) -> p s t", t=CSEG)[:, :, off:off + n]

        def p_sample(g, off, n):
            return pext(g)[:, PHIST + SEQ:].rearrange("p (s t) -> p s t", t=PSEG)[:, :, off:off + n]

        def streams(ap):
            return ap.rearrange("p (s t) -> p s t", t=DSEQ)

        def y_sb(c):
            return ext[:, c * WIN:(c + 1) * WIN]

        def y_sq(c):
            o = NCB * CEXT + c * WIN
            return ext[:, o:o + WIN]

        def state_rows(i):
            pooled, _, n = STATES[i]
            rows, seg = (PHIST, PSEG) if pooled else (CHIST, CSEG)
            return rows + seg * max(n - 1, 0)

        def state_cols(i, c):
            pooled, s, n = STATES[i]
            e = pext(c) if pooled else cext(c)
            hist_n, seg = (PHIST, PSEG) if pooled else (CHIST, CSEG)
            o = SEQ if n == 0 else hist_n + SEQ + s * seg + DSEQ
            return e[:, o:o + state_rows(i)]

        S = {n: sem(n) for n in (
            "x_loaded const_loaded prm_loaded prm_turned prm_ready ssq_done ms_ready std_ready h_ready ht_done "
            "hT_hi hT_lo hist_loaded hist_turned hist_ready ext_zeroed blk_done sig_done gated "
            "p_done poolw_loaded conv_step conv_done y_ready mean_done xc_done sq_done var_done ve_ready "
            "sd_ready xn_done c_done c_hi c_lo z_in z_done z_hi z_lo st_turned st_copied st_stored0 st_stored1 "
            "wout_used x_added gu_done silu_done act_done turned ft_hi_ready ft_lo_ready down_done "
            "gbc_loaded final_gain tri_loaded iota_loaded y_stored rw_loaded rw_hi_ready rw_lo_ready mean_w_ready rb_loaded low_loaded logits_done lg_ready "
            "exp_done mask_ready pos_done cnt_ready onehot_ready gathered pt_turned pt_ready xT_hi xT_lo "
            "ye_hi_ready ye_lo_ready scattered x_complete dve_chain act_chain pool_chain"
        ).split()}
        loaded = [sem(f"loaded{i}") for i in range(6)]
        hi_ready = [sem(f"hi_ready{i}") for i in range(6)]
        lo_ready = [sem(f"lo_ready{i}") for i in range(6)]

        def slot(t, i):
            return t[:, i * TILE:(i + 1) * TILE]

        def load(sp, s, uses, src, rows):
            if not isinstance(uses, int) or uses > 0:
                sp.wait_ge(lo_ready[s], uses)
            sp.dma_start(slot(raw, s).rearrange("p (k n) -> p k n", k=rows), src).then_inc(loaded[s], 16)

        def make_hi(act, s, uses):
            act.wait_ge(loaded[s], uses * 16 + 16)
            act.activation(slot(w_hi, s), slot(raw, s), ACT.Copy).then_inc(hi_ready[s], 1)

        def make_lo(dve, s, uses):
            dve.wait_ge(hi_ready[s], uses + 1)
            dve.tensor_tensor(slot(w_lo, s), slot(raw, s), slot(w_hi, s).bitcast(F32), ALU.subtract)\
               .then_inc(lo_ready[s], 1)

        def product(pe, out, lh, ll, rh, rl, start, stop):
            pe.matmul(out, lh, rh, start=start, stop=False)
            pe.matmul(out, lh, rl, start=False, stop=False)
            return pe.matmul(out, ll, rh, start=False, stop=stop)

        class Ffn:
            def __init__(self, nb, gens, units, off, K):
                self.nb, self.gens, self.units, self.off, self.K = nb, gens, units, off, K

            def at(self, k):
                return Ffn(self.nb, self.gens, self.units, self.off, self.K + k)

            def slot(self, kind, c):
                return 3 * ((self.off + c) % 2) + "gud".index(kind)

            def uses(self, kind, c):
                return self.gens[self.slot(kind, c)] + (self.off + c) // 2 + self.K

            def count(self, l):
                return self.units + self.nb * self.off + l + 2 * self.nb * self.K

            def bank(self, l):
                return 6 + (self.nb * self.off + l) % 2

            def buf(self, l):
                return (self.nb * self.off + l) % 2

            def tiles(self, l):
                c, tb = divmod(l, self.nb)
                if self.nb == 1:
                    t = [("g", c + 1), ("d", c - 1), ("u", c + 1)]
                else:
                    t = [[("d", c)], [("g", c + 1)], [("u", c + 1)]][tb]
                return [(k, n) for k, n in t if n >= 0 and (n < NF or k == "d") and not (k != "d" and n >= NF)]

            def units_of(self, first, n):
                return range(self.nb * first, self.nb * (first + n))

        moe_w = {"g": a["moe_w_gate"], "u": a["moe_w_up"], "d": a["moe_w_down"]}
        dense_w = {"g": a["dense_w_gate"], "u": a["dense_w_up"], "d": a["dense_w_down"]}

        def ffn_src(w, kind, e, c):
            m = w[kind][0]
            if len(m.shape) == 3:
                m = m[bass.ds(e, 1)] if not isinstance(e, int) else m[e:e + 1]
                m = m.rearrange("o a b -> (o a) b")
            if kind == "d":
                return m[bass.ds(c * FT, FT), :].rearrange("(k p) n -> p k n", p=P)
            return m.rearrange("(k p) n -> p k n", p=P)[:, :, bass.ds(c * FT, FT)]

        def sp_ffn(sp, f, w, e):
            def one(g, kind, c, c_expr):
                load(sp, g.slot(kind, c), g.uses(kind, c), ffn_src(w, kind, e, c_expr), 8 if kind != "d" else 2)

            for kind in "gu":
                one(f, kind, 0, 0)

            for l in f.units_of(0, 3):
                for kind, c in f.tiles(l):
                    one(f, kind, c, c)
            with sp.Fori(0, 3) as k:
                for l in f.units_of(3, 2):
                    for kind, c in f.tiles(l):
                        one(f.at(k), kind, c, 2 * k + c)
            for l in f.units_of(3, 2):
                for kind, c in f.tiles(l):
                    if kind == "d" or c + 6 < NF:
                        one(f.at(3), kind, c, 6 + c)
            if f.nb == 1:
                one(f, "d", NF - 1, NF - 1)

        def units_loop(eng, f, fn):
            for l in f.units_of(0, 3):
                fn(f, l, 0)
            with eng.Fori(0, 3) as k:
                for l in f.units_of(3, 2):
                    fn(f.at(k), l, 0)
            for l in f.units_of(3, 2):
                fn(f.at(3), l, 6)

        def pair_items(p):
            return [Ffn(1, GEN_MOE, DENSE_UNITS, NF * b, NF * p) for b in range(2)]

        dense = Ffn(NTB, GEN_DENSE, 0, 0, 0)

        def overflow(eng, body):
            done = eng.alloc_register("pairs_done")
            eng.reg_mov(done, PAIRS)
            eng.wait_ge(S["cnt_ready"], 1)
            with eng.Fori(0, NE) as e:
                n = eng.value_load(cnt_i[0:1, bass.ds(e, 1)], min_val=0, max_val=TOK)
                with eng.If(n > P):
                    body(eng.snap(done, min_val=PAIRS, max_val=PAIRS + NE), e)
                    eng.reg_add(done, done, 1)

        block = ctx.enter_context(nc.Block())

        @block.sync
        def _(sp):
            for l in range(LAYERS):
                w = a["w_in"][l].rearrange("(k p) n -> p k n", p=P)
                for s, t in enumerate(WIN_TILES):
                    load(sp, s, GEN_WIN[l][s], w[:, :, t * 256:(t + 1) * 256], KD)
                w = a["w_out"][l].rearrange("(t k p) n -> t p k n", p=P, k=2)
                for s, t in enumerate(WOUT_TILES):
                    load(sp, s, GEN_WOUT[l][s], w[t], 2)
                if l == 0:
                    sp_ffn(sp, dense, dense_w, 0)
            with sp.Fori(0, PAIRS) as p:
                for b, f in enumerate(pair_items(p)):
                    sp_ffn(sp, f, moe_w, 2 * p + b)

            def body(done, e):
                for f in pair_items(done):
                    sp_ffn(sp, f, moe_w, e)
            overflow(sp, body)

        def act_norm(act, n):
            if n == 0:
                act.wait_ge(S["x_loaded"], 16 * NTB)
            else:
                act.wait_ge(S["x_added"], 6 * n if n < 4 else 18)
            for tb in range(NTB):
                act.activation(ext[:, tb * D:(tb + 1) * D], x[:, tb * D:(tb + 1) * D], ACT.Square,
                               accum_out=stat[:, tb:tb + 1]).then_inc(S["ssq_done"], 1)
            act.wait_ge(S["ms_ready"], n + 1)
            act.activation(stat[:, 6:9], stat[:, 3:6], ACT.Sqrt).then_inc(S["std_ready"], 1)

        def act_hT(act, n, gcol):
            for k in range(KD):
                act.wait_ge(S["ht_done"], KD * n + k + 1)
                scale = 1.0 if gcol is None else prm[:, gcol + k:gcol + k + 1]
                act.activation(a_hi[:, k * TOK:(k + 1) * TOK], ps[:, 6 + k % 2, 0:TOK], ACT.Copy, scale=scale)\
                   .then_inc(S["hT_hi"], 1)

        def act_ffn_tile(act, f, kind, c):
            done = f.count(f.nb * (c - 1))
            if not isinstance(done, int) or done > 0:
                act.wait_ge(S["down_done" if kind == "d" else "gu_done"], done)
            make_hi(act, f.slot(kind, c), f.uses(kind, c))

        def act_silu(act, f, l):
            act.wait_ge(S["gu_done"], f.count(l + 1))
            if not isinstance(f.K, int) or f.count(l) > 0:
                act.wait_ge(S["act_done"], f.count(l))
            act.activation(silu[:, :], ps[:, f.bank(l), 0:FT], ACT.Silu).then_inc(S["silu_done"], 1)

        def act_ft(act, f, l):
            act.wait_ge(S["turned"], f.count(l + 1))
            if not isinstance(f.K, int) or f.count(l - 1) > 0:
                act.wait_ge(S["down_done"], f.count(l - 1))
            b = f.buf(l)
            act.activation(ft_hi[:, b * FT:(b + 1) * FT], ps[:, f.bank(l), 0:FT], ACT.Copy)\
               .then_inc(S["ft_hi_ready"], 1)

        def act_units(act, f):
            def unit(g, l, shift):
                if l:
                    act_silu(act, g, l - 1)
                t = g.tiles(l)
                for kind, c in t[:2]:
                    if kind == "d" or c + shift < NF:
                        act_ffn_tile(act, g, kind, c)
                if l:
                    act_ft(act, g, l - 1)
                for kind, c in t[2:]:
                    if c + shift < NF:
                        act_ffn_tile(act, g, kind, c)
            units_loop(act, f, unit)
            n = NF * f.nb
            act_silu(act, f, n - 1)
            if f.nb == 1:
                act_ffn_tile(act, f, "d", NF - 1)
            act_ft(act, f, n - 1)

        @block.scalar
        def _(act):
            chain = [0]

            def link(ins):
                chain[0] += 1
                ins.then_inc(S["act_chain"], 1)
                act.wait_ge(S["act_chain"], chain[0])

            act.dma_start(x[:, 0:2 * D].rearrange("p (t d) -> p t d", t=2),
                          a["x_prompt"][0].rearrange("(t p) d -> p t d", p=P)).then_inc(S["x_loaded"], 16 * 2)
            act.dma_start(x[:, 2 * D:3 * D], a["x_sample"].rearrange("s t d -> (s t) d")).then_inc(S["x_loaded"], 16)
            act.dma_start(ident[:, :], a["c_ident"]).then_inc(S["const_loaded"], 16)
            act.dma_start(cinv[:, :], a["c_inv"]).then_inc(S["const_loaded"], 16)
            r = 0
            for name in ("norm_mix", "norm_ffn", "conv_b", "conv_ln_g", "conv_ln_b", "pool_scale"):
                rows = a[name].rearrange("l (k p) -> (l k) p", p=P)
                n = rows.shape[0]
                act.dma_start(prm_rows[r:r + n, 0:P], rows).then_inc(S["prm_loaded"], 16)
                r += n
            for l in range(LAYERS):
                act.dma_start(prm_rows[0:TAPS * NCB, (1 + l) * P:(2 + l) * P],
                              a["conv_w"][l].rearrange("j (c p) -> (j c) p", p=P)).then_inc(S["prm_loaded"], 16)
            act_norm(act, 0)
            for s in range(2):
                make_hi(act, s, 0)
            act.wait_ge(S["prm_turned"], 1)
            act.activation(prm[:, :], ps[:, 0, 0:NPRM], ACT.Copy).then_inc(S["prm_ready"], 1)
            act.wait_ge(S["prm_ready"], 1)
            for l in range(LAYERS):
                if l:
                    act_norm(act, 2)
                    for s in range(2):
                        act.wait_ge(S["gu_done"], DENSE_UNITS)
                        act.wait_ge(S["down_done"], DENSE_UNITS)
                        make_hi(act, s, GEN_WIN[l][s])
                if l == 0:
                    act.wait_ge(S["prm_turned"], 1)
                act.dma_start(hist[0:120, 0:2 * CH].rearrange("p (g c) -> p g c", g=2),
                              a["state_conv"][l].rearrange("(g s) t c -> (s t) g c", g=2))\
                   .then_inc(S["hist_loaded"], 16)
                act.dma_start(hist[0:120, 2 * CH:3 * CH], a["state_pool"][l].rearrange("s t c -> (s t) c"))\
                   .then_inc(S["hist_loaded"], 16)
                act_hT(act, 2 * l, C_MIX + KD * l)
                for s in range(2, 6):
                    make_hi(act, s, GEN_WIN[l][s])
                for c in range(NCB):
                    act.wait_ge(S["hist_turned"], NCB * l + c + 1)
                    act.activation(c_sample(c, 0, CHIST), ps[:, 2 + c, 0:240].rearrange("p (s t) -> p s t", t=CHIST),
                                   ACT.Copy).then_inc(S["hist_ready"], 1)
                    act.activation(p_sample(c, 0, PHIST), ps[:, 2 + c, 240:360].rearrange("p (s t) -> p s t", t=PHIST),
                                   ACT.Copy).then_inc(S["hist_ready"], 1)
                act.dma_start(pool_w[:, :].rearrange("p (g d) -> p g d", g=NCB),
                              a["pool_w"][l].rearrange("g c d -> c g d")).then_inc(S["poolw_loaded"], 16)
                for c in range(NCB):
                    act.wait_ge(S["blk_done"], 12 * l + [3, 4, 7, 8][c])
                    if 4 * l + c:
                        act.wait_ge(S["gated"], 4 * l + c)
                    act.activation(sgm[:, :], ps[:, 6 + c % 2, 0:TOK], ACT.Sigmoid).then_inc(S["sig_done"], 1)
                act.wait_ge(S["ext_zeroed"], 2 * l + 2)
                for g in range(NCB):
                    bank = WIN_BANK[8 + g]
                    act.wait_ge(S["blk_done"], 12 * l + 9 + g)
                    act.activation(pext(g)[:, PHIST:PHIST + SEQ], ps[:, bank, 0:SEQ], ACT.Copy)\
                       .then_inc(S["p_done"], 1)
                    act.activation(p_sample(g, PHIST, DSEQ), streams(ps[:, bank, SEQ:TOK]), ACT.Copy)\
                       .then_inc(S["p_done"], 1)
                for s in range(4):
                    act.wait_ge(S["blk_done"], 12 * l + 2 * s + 2)
                    make_hi(act, s, GEN_WOUT[l][s])
                act.wait_ge(S["gated"], 4 * l + 4)
                for i in range(NST):
                    n, b = state_rows(i), i % 2
                    before = STORES[b] * l + stored_before(i)
                    act.wait_ge(S["st_turned"], NST * l + i + 1)
                    if before:
                        act.wait_ge(S[f"st_stored{b}"], 16 * before)
                    act.activation(stage[0:n, b * CH:(b + 1) * CH], ps[0:n, SIDE_BANK[i], 0:CH], ACT.Copy)\
                       .then_inc(S["st_copied"], 1)
                for g in range(NCB):
                    act.wait_ge(S["z_done"], 4 * l + g + 1)
                    act.activation(a_hi[:, (4 + g) * TOK:(5 + g) * TOK], ps[:, SIDE_BANK[NST + g], 0:TOK], ACT.Copy,
                                   scale=prm[:, C_PS + 4 * l + g:C_PS + 4 * l + g + 1]).then_inc(S["z_hi"], 1)
                act.wait_ge(S["conv_done"], 4 * l + 4)
                for c in range(NCB):
                    act.activation(y_sb(c), ps[:, 2 + c, 0:TOK], ACT.Identity,
                                   bias=prm[:, C_CB + 4 * l + c:C_CB + 4 * l + c + 1]).then_inc(S["y_ready"], 1)
                for c in range(NCB):
                    act.wait_ge(S["xc_done"], 4 * l + c + 1)
                    act.activation(y_sq(c), y_sb(c), ACT.Square).then_inc(S["sq_done"], 1)
                act.wait_ge(S["ve_ready"], l + 1)
                act.activation(sgm[:, :], sgm[:, :], ACT.Sqrt).then_inc(S["sd_ready"], 1)
                for c in range(NCB):
                    act.wait_ge(S["xn_done"], 4 * l + c + 1)
                    act.activation(y_sb(c), y_sb(c), ACT.Silu, scale=prm[:, C_LG + 4 * l + c:C_LG + 4 * l + c + 1],
                                   bias=prm[:, C_LB + 4 * l + c:C_LB + 4 * l + c + 1]).then_inc(S["c_done"], 1)
                    act.wait_ge(S["c_done"], 4 * l + c + 1)
                    act.activation(a_hi[:, c * TOK:(c + 1) * TOK], y_sb(c), ACT.Copy).then_inc(S["c_hi"], 1)
                act_norm(act, 2 * l + 1)
                if l == 0:
                    act.wait_ge(S["wout_used"], 4)
                    for kind in "gu":
                        act_ffn_tile(act, dense, kind, 0)
                    act_hT(act, 1, C_FFN)
                    act_units(act, dense)
            act.dma_start(rw_raw[:, :].rearrange("p (k e) -> p k e", k=KD),
                          a["router_w"][0].rearrange("(k p) e -> p k e", p=P)).then_inc(S["rw_loaded"], 16)
            act.wait_ge(S["rw_loaded"], 16)
            act.activation(rw_hi[:, :], rw_raw[:, :], ACT.Copy).then_inc(S["rw_hi_ready"], 1)
            act_hT(act, 3, None)
            act.wait_ge(S["logits_done"], 1)
            act.dma_start(tri[:, :], a["c_tri"]).then_inc(S["tri_loaded"], 16)
            act.dma_start(low[:, :], a["c_low"]).then_inc(S["low_loaded"], 16)
            act.dma_start(rb[:, :], a["router_b"].to_broadcast([P, NE])).then_inc(S["rb_loaded"], 16)
            act.wait_ge(S["lg_ready"], 1)
            for tb in range(NTB):
                act.activation(gate[:, tb * NE:(tb + 1) * NE], lg[:, tb * NE:(tb + 1) * NE], ACT.Exp,
                               bias=rmax[:, NTB + tb:NTB + tb + 1]).then_inc(S["exp_done"], 1)

            def act_item(f, item):
                if f.off == 0:
                    for kind in "gu":
                        act_ffn_tile(act, f, kind, 0)
                act.wait_ge(S["pt_turned"], item + 1)
                act.activation(pt[:, :], ps[:, 4, 0:NTB * P], ACT.Copy).then_inc(S["pt_ready"], 1)
                for i in range(2):
                    act.wait_ge(S["gathered"], 2 * item + i + 1)
                    act.activation(a_hi[:, i * 512:(i + 1) * 512], ps[:, 2 + i, :], ACT.Copy).then_inc(S["xT_hi"], 1)
                if f.off:
                    for kind in "gu":
                        act_ffn_tile(act, f, kind, 0)
                act_units(act, f)
                act.wait_ge(S["down_done"], f.count(NF))
                for i in range(2):
                    act.activation(ye_hi[:, i * 512:(i + 1) * 512], ps[:, i, :], ACT.Copy).then_inc(S["ye_hi_ready"], 1)

            act.wait_ge(S["wout_used"], 8)
            with act.Fori(0, PAIRS) as p:
                for b, f in enumerate(pair_items(p)):
                    act_item(f, 2 * p + b)

            def body(done, e):
                for b, f in enumerate(pair_items(done)):
                    act_item(f, 2 * done + b)
            overflow(act, body)
            act.wait_ge(S["x_complete"], 1)
            for tb in range(NTB):
                act.activation(ext[:, tb * D:(tb + 1) * D], x[:, tb * D:(tb + 1) * D], ACT.Square,
                               accum_out=stat[:, tb:tb + 1]).then_inc(S["ssq_done"], 1)
            act.dma_start(gbc, a["norm_final"].rearrange("(o d) -> o d", o=1).to_broadcast([P, D]))\
               .then_inc(S["final_gain"], 16)
            act.wait_ge(S["ms_ready"], 5)
            act.activation(stat[:, 6:9], stat[:, 3:6], ACT.Sqrt).then_inc(S["std_ready"], 1)
            yp = a["y_prompt"][0].rearrange("(t p) d -> t p d", p=P)
            dst = [yp[0], yp[1], a["y_sample"].rearrange("s t d -> (s t) d")]
            for tb in range(NTB):
                act.wait_ge(S["h_ready"], 4 * NTB + tb + 1)
                act.dma_start(dst[tb], h[:, tb * D:(tb + 1) * D]).then_inc(S["y_stored"], 16)
            act.wait_ge(S["y_stored"], 16 * NTB)
            act.wait_ge(S["st_stored0"], 16 * 2 * STORES[0])
            act.wait_ge(S["st_stored1"], 16 * 2 * STORES[1])

        @block.vector
        def _(dve):
            chain = [0]

            def link(ins):
                chain[0] += 1
                ins.then_inc(S["dve_chain"], 1)
                dve.wait_ge(S["dve_chain"], chain[0])

            def dve_norm(n, gain=None):
                dve.wait_ge(S["ssq_done"], NTB * (n + 1))
                ms, sd, r, t = stat[:, 3:6], stat[:, 6:9], stat[:, 9:12], stat[:, 0:3]
                ins = dve.tensor_scalar(ms, stat[:, 0:3], 1.0 / D, EPS, ALU.mult, ALU.add)
                ins.then_inc(S["ms_ready"], 1)
                dve.wait_ge(S["std_ready"], n + 1)
                link(dve.reciprocal(r, sd))
                link(dve.tensor_tensor(t, r, r, ALU.mult))
                link(dve.tensor_tensor(t, t, ms, ALU.mult))
                link(dve.tensor_scalar(t, t, -0.5, 1.5, ALU.mult, ALU.add))
                link(dve.tensor_tensor(r, r, t, ALU.mult))
                if gain is not None:
                    dve.wait_ge(S[gain], 16)
                for tb in range(NTB):
                    o, i = h[:, tb * D:(tb + 1) * D], x[:, tb * D:(tb + 1) * D]
                    if gain is None:
                        dve.tensor_scalar(o, i, r[:, tb:tb + 1], None, ALU.mult).then_inc(S["h_ready"], 1)
                    else:
                        dve.scalar_tensor_tensor(out=o, in0=i, scalar=r[:, tb:tb + 1], in1=gbc, op0=ALU.mult,
                                                 op1=ALU.mult).then_inc(S["h_ready"], 1)

            def dve_hT(n, gcol):
                for k in range(KD):
                    dve.wait_ge(S["hT_hi"], KD * n + k + 1)
                    o, hi, src = (a_lo[:, k * TOK:(k + 1) * TOK], a_hi[:, k * TOK:(k + 1) * TOK].bitcast(F32),
                                  ps[:, 6 + k % 2, 0:TOK])
                    if gcol is None:
                        ins = dve.tensor_tensor(o, src, hi, ALU.subtract)
                    else:
                        ins = dve.scalar_tensor_tensor(out=o, in0=src, scalar=prm[:, gcol + k:gcol + k + 1], in1=hi,
                                                       op0=ALU.mult, op1=ALU.subtract)
                    ins.then_inc(S["hT_lo"], 1)

            def gated(l, c):
                bank = c % 2
                dve.wait_ge(S["sig_done"], 4 * l + c + 1)
                if c == 0:
                    dve.wait_ge(S["ext_zeroed"], 2 * l + 2)
                dve.tensor_tensor(cext(c)[:, CHIST:CHIST + SEQ], ps[:, bank, 0:SEQ], sgm[:, 0:SEQ], ALU.mult)
                dve.tensor_tensor(c_sample(c, CHIST, DSEQ), streams(ps[:, bank, SEQ:TOK]), streams(sgm[:, SEQ:TOK]),
                                  ALU.mult).then_inc(S["gated"], 1)

            steps = [0]

            def conv(l, c):
                dve.wait_ge(S["gated"], 4 * l + c + 1)
                dve.wait_ge(S["hist_ready"], 2 * NCB * (l + 1))
                dst = ps[:, 2 + c, 0:SEQ], streams(ps[:, 2 + c, SEQ:TOK])
                for j in range(TAPS):
                    col = C_CW + (l * TAPS + j) * NCB + c
                    w = prm[:, col:col + 1]
                    for o, src in zip(dst, (cext(c)[:, j:j + SEQ], c_sample(c, j, DSEQ))):
                        if j == 0:
                            ins = dve.tensor_scalar(o, src, w, None, ALU.mult)
                        else:
                            dve.wait_ge(S["conv_step"], steps[0] - 1)
                            ins = dve.scalar_tensor_tensor(out=o, in0=src, scalar=w, in1=o, op0=ALU.mult, op1=ALU.add)
                        if j == TAPS - 1 and o is dst[1]:
                            dve.wait_ge(S["conv_step"], steps[0])
                            ins.then_inc(S["conv_done"], 1)
                        else:
                            ins.then_inc(S["conv_step"], 1)
                            steps[0] += 1

            def tile_lo(f, kind, c):
                make_lo(dve, f.slot(kind, c), f.uses(kind, c))

            def act_mul(f, l):
                dve.wait_ge(S["silu_done"], f.count(l + 1))
                if not isinstance(f.K, int) or f.count(l) > 0:
                    dve.wait_ge(S["turned"], f.count(l))
                dve.tensor_tensor(act_b[:, :], ps[:, f.bank(l), FT:2 * FT], silu[:, :], ALU.mult)\
                   .then_inc(S["act_done"], 1)

            def ft_low(f, l):
                dve.wait_ge(S["ft_hi_ready"], f.count(l + 1))
                b = f.buf(l)
                dve.tensor_tensor(ft_lo[:, b * FT:(b + 1) * FT], ps[:, f.bank(l), 0:FT],
                                  ft_hi[:, b * FT:(b + 1) * FT].bitcast(F32), ALU.subtract)\
                   .then_inc(S["ft_lo_ready"], 1)

            def dve_units(f):
                def unit(g, l, shift):
                    if l:
                        act_mul(g, l - 1)
                    t = g.tiles(l)
                    for kind, c in t[:2]:
                        if kind == "d" or c + shift < NF:
                            tile_lo(g, kind, c)
                    if l:
                        ft_low(g, l - 1)
                    for kind, c in t[2:]:
                        if c + shift < NF:
                            tile_lo(g, kind, c)
                units_loop(dve, f, unit)
                n = NF * f.nb
                act_mul(f, n - 1)
                if f.nb == 1:
                    tile_lo(f, "d", NF - 1)
                ft_low(f, n - 1)

            def add_y():
                for i in range(6):
                    tb, dh = divmod(i, 2)
                    o = x[:, tb * D + dh * 512:tb * D + dh * 512 + 512]
                    dve.tensor_tensor(o, o, ps[:, i, :], ALU.add).then_inc(S["x_added"], 1)

            dve.memset(mean_w[:, :], 1.0 / CH).then_inc(S["mean_w_ready"], 1)
            dve_norm(0)
            for l in range(LAYERS):
                if l:
                    dve_norm(2)
                for s in range(2):
                    make_lo(dve, s, GEN_WIN[l][s])
                dve.wait_ge(S["prm_ready"], 1)
                dve_hT(2 * l, C_MIX + KD * l)
                for s in range(2, 6):
                    make_lo(dve, s, GEN_WIN[l][s])
                gated(l, 0)
                gated(l, 1)
                conv(l, 0)
                gated(l, 2)
                gated(l, 3)
                conv(l, 1)
                make_lo(dve, 0, GEN_WOUT[l][0])
                make_lo(dve, 1, GEN_WOUT[l][1])
                conv(l, 2)
                make_lo(dve, 2, GEN_WOUT[l][2])
                make_lo(dve, 3, GEN_WOUT[l][3])
                conv(l, 3)
                for g in range(NCB):
                    dve.wait_ge(S["z_hi"], 4 * l + g + 1)
                    o = (4 + g) * TOK
                    dve.scalar_tensor_tensor(out=a_lo[:, o:o + TOK], in0=ps[:, SIDE_BANK[NST + g], 0:TOK],
                                             scalar=prm[:, C_PS + 4 * l + g:C_PS + 4 * l + g + 1],
                                             in1=a_hi[:, o:o + TOK].bitcast(F32), op0=ALU.mult,
                                             op1=ALU.subtract).then_inc(S["z_lo"], 1)
                dve.wait_ge(S["mean_done"], l + 1)
                for c in range(NCB):
                    dve.tensor_tensor(y_sb(c), y_sb(c), ps[:, 6, 0:TOK], ALU.subtract).then_inc(S["xc_done"], 1)
                dve.wait_ge(S["var_done"], l + 1)
                dve.wait_ge(S["st_stored0"], 16 * STORES[0] * (l + 1))
                dve.wait_ge(S["st_stored1"], 16 * STORES[1] * (l + 1))
                dve.tensor_scalar(sgm[:, :], ps[:, 7, 0:TOK], EPS, None, ALU.add).then_inc(S["ve_ready"], 1)
                dve.wait_ge(S["sd_ready"], l + 1)
                link(dve.reciprocal(sgm[:, :], sgm[:, :]))
                dve.wait_ge(S["sq_done"], 4 * l + 4)
                for c in range(NCB):
                    dve.tensor_tensor(y_sb(c), y_sb(c), sgm[:, :], ALU.mult).then_inc(S["xn_done"], 1)
                for c in range(NCB):
                    dve.wait_ge(S["c_hi"], 4 * l + c + 1)
                    dve.tensor_tensor(a_lo[:, c * TOK:(c + 1) * TOK], y_sb(c),
                                      a_hi[:, c * TOK:(c + 1) * TOK].bitcast(F32), ALU.subtract).then_inc(S["c_lo"], 1)
                dve.wait_ge(S["wout_used"], 4 * (l + 1))
                add_y()
                if l == 0:
                    dve_norm(1)
                    for kind in "gu":
                        tile_lo(dense, kind, 0)
                    dve_hT(1, C_FFN)
                    dve_units(dense)
                    dve.wait_ge(S["down_done"], DENSE_UNITS)
                    add_y()
            dve_norm(3, "gbc_loaded")
            dve.wait_ge(S["rw_hi_ready"], 1)
            dve.tensor_tensor(rw_lo[:, :], rw_raw[:, :], rw_hi[:, :].bitcast(F32), ALU.subtract)\
               .then_inc(S["rw_lo_ready"], 1)
            dve_hT(3, None)
            dve.wait_ge(S["logits_done"], 1)
            dve.wait_ge(S["rb_loaded"], 16)
            dve.wait_ge(S["low_loaded"], 16)
            for tb in range(NTB):
                ins = dve.tensor_tensor(lg[:, tb * NE:(tb + 1) * NE], ps[:, 2, tb * NE:(tb + 1) * NE], rb[:, :], ALU.add)
            link(ins)
            link(dve.tensor_reduce(rmax[:, 0:NTB], lg[:, :].rearrange("p (t e) -> p t e", e=NE), AXX, ALU.max))
            dve.tensor_scalar(rmax[:, NTB:2 * NTB], rmax[:, 0:NTB], -1.0, None, ALU.mult).then_inc(S["lg_ready"], 1)
            for tb in range(NTB):
                row = lg[:, tb * NE:(tb + 1) * NE]
                other = row.unsqueeze(1).to_broadcast([P, NE, NE])
                own = row.unsqueeze(2).to_broadcast([P, NE, NE])
                m3 = lambda t: t[:, :].rearrange("p (e j) -> p e j", j=NE)
                link(dve.tensor_tensor(m3(cmp_gt), other, own, ALU.is_gt))
                link(dve.tensor_tensor(m3(cmp_eq), other, own, ALU.is_equal))
                link(dve.tensor_tensor(cmp_eq[:, :], cmp_eq[:, :], low[:, :], ALU.mult))
                link(dve.tensor_tensor(cmp_gt[:, :], cmp_gt[:, :], cmp_eq[:, :], ALU.add))
                link(dve.tensor_reduce(rank[:, tb * NE:(tb + 1) * NE], m3(cmp_gt), AXX, ALU.add))
            dve.tensor_scalar(mask[:, :], rank[:, :], 2.0, None, ALU.is_lt).then_inc(S["mask_ready"], 1)
            dve.wait_ge(S["mask_ready"], 1)
            dve.wait_ge(S["exp_done"], NTB)
            link(dve.tensor_tensor(gate[:, :], gate[:, :], mask[:, :], ALU.mult))
            link(dve.tensor_reduce(rsum[:, 0:NTB], gate[:, :].rearrange("p (t e) -> p t e", e=NE), AXX, ALU.add))
            link(dve.reciprocal(rsum[:, NTB:2 * NTB], rsum[:, 0:NTB]))
            for tb in range(NTB):
                ins = dve.tensor_scalar(gate[:, tb * NE:(tb + 1) * NE], gate[:, tb * NE:(tb + 1) * NE],
                                        rsum[:, NTB + tb:NTB + tb + 1], None, ALU.mult)
            link(ins)
            dve.wait_ge(S["iota_loaded"], 16)
            dve.wait_ge(S["pos_done"], 1)
            link(dve.tensor_scalar(post[:, :], ps[:, 3, 0:NTB * NE], float(CH), 1.0, ALU.mult, ALU.add))
            link(dve.tensor_tensor(post[:, :], post[:, :], mask[:, :], ALU.mult))
            for b in range(3):
                ins = dve.tensor_scalar(posb[:, b * NTB * NE:(b + 1) * NTB * NE], post[:, :], 1.0, float(P * b),
                                        ALU.subtract, ALU.subtract)
            link(ins)
            link(dve.tensor_scalar(cnt_f[:, :], ps[:, 3, NTB * NE:(NTB + 1) * NE], float(CH), None, ALU.mult))
            dve.tensor_copy(cnt_i[:, :], cnt_f[:, :]).then_inc(S["cnt_ready"], 1)

            def dve_item(f, item, e, blk):
                for tb in range(NTB):
                    ins = dve.tensor_scalar(onehot[:, tb * P:(tb + 1) * P], iota,
                                            posb[:, bass.ds(e + (blk * NTB * NE + tb * NE), 1)], None, ALU.is_equal)
                ins.then_inc(S["onehot_ready"], 1)
                if f.off == 0:
                    for kind in "gu":
                        tile_lo(f, kind, 0)
                for i in range(2):
                    dve.wait_ge(S["xT_hi"], 2 * item + i + 1)
                    dve.tensor_tensor(a_lo[:, i * 512:(i + 1) * 512], ps[:, 2 + i, :],
                                      a_hi[:, i * 512:(i + 1) * 512].bitcast(F32), ALU.subtract).then_inc(S["xT_lo"], 1)
                if f.off:
                    for kind in "gu":
                        tile_lo(f, kind, 0)
                dve_units(f)
                for i in range(2):
                    dve.wait_ge(S["ye_hi_ready"], 2 * item + i + 1)
                    dve.tensor_tensor(ye_lo[:, i * 512:(i + 1) * 512], ps[:, i, :],
                                      ye_hi[:, i * 512:(i + 1) * 512].bitcast(F32), ALU.subtract)\
                       .then_inc(S["ye_lo_ready"], 1)
                for i in range(6):
                    tb, dh = divmod(i, 2)
                    o = x[:, tb * D + dh * 512:tb * D + dh * 512 + 512]
                    dve.wait_ge(S["scattered"], 6 * item + i + 1)
                    dve.scalar_tensor_tensor(out=o, in0=ps[:, 4 + i % 2, :],
                                             scalar=gate[:, bass.ds(e + tb * NE, 1)], in1=o,
                                             op0=ALU.mult, op1=ALU.add).then_inc(S["x_added"], 1)

            with dve.Fori(0, PAIRS) as p:
                for b, f in enumerate(pair_items(p)):
                    dve_item(f, 2 * p + b, 2 * p + b, 0)

            last = dve.alloc_register("items_done")
            dve.reg_mov(last, 18 + 6 * NE)

            def body(done, e):
                for b, f in enumerate(pair_items(done)):
                    dve_item(f, 2 * done + b, e, 1 + b)
                dve.reg_add(last, last, 12)
            overflow(dve, body)
            dve.wait_ge(S["x_added"], dve.snap(last, min_val=66, max_val=66 + 12 * NE))
            dve.memset(stat[:, 0:3], 0.0).then_inc(S["x_complete"], 1)
            dve_norm(4, "final_gain")

        @block.tensor
        def _(pe):
            def pe_hT(n):
                pe.wait_ge(S["h_ready"], NTB * (n + 1))
                for k in range(KD):
                    if k >= 2 or n:
                        pe.wait_ge(S["hT_lo"], KD * n + max(k - 1, 0))
                    for tb in range(NTB):
                        ins = pe.transpose(ps[:, 6 + k % 2, tb * P:(tb + 1) * P],
                                           h[:, tb * D + k * P:tb * D + (k + 1) * P], ident[:, :])
                    ins.then_inc(S["ht_done"], 1)

            def blk(ap, i, width=TOK):
                return ap[:, i * width:(i + 1) * width]

            pe.wait_ge(S["const_loaded"], 32)
            pe.wait_ge(S["prm_loaded"], 16 * 8)
            pe.transpose(ps[:, 0, 0:64], prm_rows[0:64, 0:P], ident[0:64, 0:64])
            for l in range(LAYERS):
                n = TAPS * NCB
                ins = pe.transpose(ps[:, 0, 64 + l * n:64 + (l + 1) * n], prm_rows[0:n, (1 + l) * P:(2 + l) * P],
                                   ident[0:n, 0:n])
            ins.then_inc(S["prm_turned"], 1)

            def unit_gu(f, l, shift):
                c, tb = divmod(l, f.nb)
                if tb == 0:
                    for kind in "gu":
                        pe.wait_ge(lo_ready[f.slot(kind, c)], f.uses(kind, c) + 1)
                if not isinstance(f.K, int) or f.count(l - 1) > 0:
                    pe.wait_ge(S["ft_lo_ready"], f.count(l - 1))
                s = f.slot("g", c)
                out = ps[:, f.bank(l), :].rearrange("p (g n) -> p g n", g=2)

                def moving(w, k):
                    return w[:, s * TILE:(s + 2) * TILE].rearrange("p (g k n) -> p g k n", g=2, k=KD)[:, :, k, :]
                for k in range(KD):
                    o = k * TOK + tb * P if f.nb > 1 else k * P
                    ins = product(pe, out, a_hi[:, o:o + P], a_lo[:, o:o + P], moving(w_hi, k), moving(w_lo, k),
                                  k == 0, k == KD - 1)
                ins.then_inc(S["gu_done"], 1)

            def unit_turn(f, l):
                pe.wait_ge(S["act_done"], f.count(l + 1))
                for i in range(2):
                    ins = pe.transpose(ps[:, f.bank(l), i * P:(i + 1) * P], act_b[:, i * P:(i + 1) * P], ident[:, :])
                ins.then_inc(S["turned"], 1)

            def unit_down(f, l, shift):
                c, tb = divmod(l, f.nb)
                if tb == 0:
                    pe.wait_ge(lo_ready[f.slot("d", c)], f.uses("d", c) + 1)
                pe.wait_ge(S["ft_lo_ready"], f.count(l + 1))
                s = f.slot("d", c)
                b = f.buf(l)
                for i in range(2):
                    o = b * FT + i * P
                    for dh in range(2):
                        m = s * TILE + i * D + dh * 512
                        ins = product(pe, ps[:, 2 * tb + dh, :], ft_hi[:, o:o + P], ft_lo[:, o:o + P],
                                      w_hi[:, m:m + 512], w_lo[:, m:m + 512],
                                      c + shift == 0 and i == 0, c + shift == NF - 1 and i == 1)
                ins.then_inc(S["down_done"], 1)

            def pe_units(f):
                def unit(g, l, shift):
                    unit_gu(g, l, shift)
                    if l:
                        unit_turn(g, l - 1)
                    if l >= 2:
                        unit_down(g, l - 2, shift)
                units_loop(pe, f, unit)
                n = NF * f.nb
                unit_turn(f, n - 1)
                unit_down(f, n - 2, 0)
                unit_down(f, n - 1, 0)

            for l in range(LAYERS):
                pe_hT(2 * l)
                if l:
                    pe.wait_ge(S["x_added"], 12)
                pe.wait_ge(S["hist_loaded"], 32 * (l + 1))
                for c in range(NCB):
                    for g in range(3):
                        ins = pe.transpose(ps[:, 2 + c, g * 120:(g + 1) * 120],
                                           hist[0:120, g * CH + c * P:g * CH + (c + 1) * P], ident[0:120, 0:120])
                    ins.then_inc(S["hist_turned"], 1)
                pe.wait_ge(S["hT_lo"], KD * (2 * l + 1))
                if l == 0:
                    pe.wait_ge(S["prm_ready"], 1)
                for j in range(12):
                    s, m = divmod(j, 2)
                    if m == 0:
                        pe.wait_ge(lo_ready[s], GEN_WIN[l][s] + 1)
                    if j in (4, 5, 8, 9):
                        pe.wait_ge(S["gated"], 4 * l + {4: 1, 5: 2, 8: 3, 9: 4}[j])
                    if j in (6, 7, 10, 11):
                        pe.wait_ge(S["sig_done"], 4 * l + {6: 1, 7: 2, 10: 3, 11: 4}[j])
                    for k in range(KD):
                        o = s * TILE + k * 256 + m * P
                        ins = product(pe, ps[:, WIN_BANK[j], 0:TOK], w_hi[:, o:o + P], w_lo[:, o:o + P],
                                      blk(a_hi, k), blk(a_lo, k), k == 0, k == KD - 1)
                    ins.then_inc(S["blk_done"], 1)
                pe.wait_ge(S["p_done"], 8 * (l + 1))
                pe.wait_ge(S["gated"], 4 * (l + 1))
                pe.wait_ge(S["hist_ready"], 2 * NCB * (l + 1))
                for i in range(NST):
                    if i >= 4:
                        pe.wait_ge(S["st_copied"], NST * l + i - 3)
                    for c in range(NCB):
                        ins = pe.transpose(ps[0:state_rows(i), SIDE_BANK[i], c * P:(c + 1) * P], state_cols(i, c),
                                           ident[:, :])
                    ins.then_inc(S["st_turned"], 1)
                pe.wait_ge(S["poolw_loaded"], 16 * (l + 1))
                for g in range(NCB):
                    pe.wait_ge(S["st_copied"], NST * l + g + 4)
                    pe.wait_ge(S["z_in"], 4 * l + g + 1)
                    pe.matmul(ps[:, SIDE_BANK[NST + g], 0:SEQ], pool_w[:, g * P:(g + 1) * P],
                              pext(g)[:, PHIST:PHIST + SEQ], start=True, stop=True)
                    pe.matmul(streams(ps[:, SIDE_BANK[NST + g], SEQ:TOK]), pool_w[:, g * P:(g + 1) * P],
                              p_sample(g, PHIST, DSEQ), start=True, stop=True).then_inc(S["z_done"], 1)
                pe.wait_ge(S["y_ready"], 4 * (l + 1))
                pe.wait_ge(S["z_lo"], 4 * (l + 1))
                pe.wait_ge(S["mean_w_ready"], 1)
                for c in range(NCB):
                    ins = pe.matmul(ps[:, 6, 0:TOK], mean_w[:, :], y_sb(c), start=c == 0, stop=c == NCB - 1)
                ins.then_inc(S["mean_done"], 1)
                pe.wait_ge(S["sq_done"], 4 * (l + 1))
                for c in range(NCB):
                    ins = pe.matmul(ps[:, 7, 0:TOK], mean_w[:, :], y_sq(c), start=c == 0, stop=c == NCB - 1)
                ins.then_inc(S["var_done"], 1)
                for s, t in enumerate(WOUT_TILES):
                    pe.wait_ge(lo_ready[s], GEN_WOUT[l][s] + 1)
                    if s == 2:
                        pe.wait_ge(S["c_lo"], 4 * (l + 1))
                    for i in range(2):
                        e = 2 * t + i
                        for tb in range(NTB):
                            for dh in range(2):
                                o, m = e * TOK + tb * P, s * TILE + i * D + dh * 512
                                ins = product(pe, ps[:, 2 * tb + dh, :], a_hi[:, o:o + P], a_lo[:, o:o + P],
                                              w_hi[:, m:m + 512], w_lo[:, m:m + 512],
                                              s == 0 and i == 0, s == 3 and i == 1)
                    ins.then_inc(S["wout_used"], 1)
                if l == 0:
                    pe_hT(1)
                    pe.wait_ge(S["x_added"], 6)
                    pe.wait_ge(S["hT_lo"], 2 * KD)
                    pe_units(dense)
            pe_hT(3)
            pe.wait_ge(S["x_added"], 18)
            pe.wait_ge(S["hT_lo"], 4 * KD)
            pe.wait_ge(S["rw_lo_ready"], 1)
            for tb in range(NTB):
                for k in range(KD):
                    o = k * TOK + tb * P
                    ins = product(pe, ps[:, 2, tb * NE:(tb + 1) * NE], a_hi[:, o:o + P], a_lo[:, o:o + P],
                                  rw_hi[:, k * NE:(k + 1) * NE], rw_lo[:, k * NE:(k + 1) * NE], k == 0, k == KD - 1)
            ins.then_inc(S["logits_done"], 1)
            pe.wait_ge(S["mask_ready"], 1)
            pe.wait_ge(S["tri_loaded"], 16)
            for tb in range(NTB + 1):
                terms = [(mean_w, t) for t in range(min(tb, NTB))] + ([(tri, tb)] if tb < NTB else [])
                for i, (w, t) in enumerate(terms):
                    ins = pe.matmul(ps[:, 3, tb * NE:(tb + 1) * NE], w[:, :], mask[:, t * NE:(t + 1) * NE],
                                    start=i == 0, stop=i == len(terms) - 1)
            ins.then_inc(S["pos_done"], 1)

            def pe_item(f, item):
                pe.wait_ge(S["onehot_ready"], item + 1)
                pe.wait_ge(S["x_added"], 6 * item + 18)
                for tb in range(NTB):
                    ins = pe.transpose(ps[:, 4, tb * P:(tb + 1) * P], onehot[:, tb * P:(tb + 1) * P], ident[:, :])
                ins.then_inc(S["pt_turned"], 1)
                for i in range(2):
                    for k in range(4 * i, 4 * i + 4):
                        for tb in range(NTB):
                            ins = pe.matmul(ps[:, 2 + i, (k % 4) * P:(k % 4 + 1) * P],
                                            h[:, tb * D + k * P:tb * D + (k + 1) * P],
                                            onehot[:, tb * P:(tb + 1) * P], start=tb == 0, stop=tb == NTB - 1)
                    ins.then_inc(S["gathered"], 1)
                pe.wait_ge(S["xT_lo"], 2 * item + 2)
                pe_units(f)
                pe.wait_ge(S["pt_ready"], item + 1)
                pe.wait_ge(S["ye_lo_ready"], 2 * item + 2)
                for i in range(6):
                    tb, dh = divmod(i, 2)
                    if i >= 2:
                        pe.wait_ge(S["x_added"], 6 * item + 18 + i - 1)
                    pe.matmul(ps[:, 4 + i % 2, :], pt[:, tb * P:(tb + 1) * P], ye_hi[:, dh * 512:dh * 512 + 512],
                              start=True, stop=False)
                    pe.matmul(ps[:, 4 + i % 2, :], pt[:, tb * P:(tb + 1) * P], ye_lo[:, dh * 512:dh * 512 + 512],
                              start=False, stop=True).then_inc(S["scattered"], 1)

            pe.wait_ge(S["cnt_ready"], 1)
            with pe.Fori(0, PAIRS) as p:
                for b, f in enumerate(pair_items(p)):
                    pe_item(f, 2 * p + b)

            def body(done, e):
                for b, f in enumerate(pair_items(done)):
                    pe_item(f, 2 * done + b)
            overflow(pe, body)

        @block.gpsimd
        def _(pool):
            chain = [0]

            def link(ins):
                chain[0] += 1
                ins.then_inc(S["pool_chain"], 1)
                pool.wait_ge(S["pool_chain"], chain[0])

            for l in range(LAYERS):
                pool.wait_ge(S["ht_done"], KD * (2 * l + 1))
                pool.memset(ext[:, 0:NCB * CEXT].rearrange("p (c t) -> p c t", t=CEXT)[:, :, 0:CHIST], 0.0)\
                    .then_inc(S["ext_zeroed"], 1)
                pool.memset(ext[:, NCB * CEXT:].rearrange("p (c t) -> p c t", t=PEXT)[:, :, 0:PHIST], 0.0)\
                    .then_inc(S["ext_zeroed"], 1)
                pool.wait_ge(S["ext_zeroed"], 2 * l + 2)
                pool.wait_ge(S["p_done"], 8 * (l + 1))
                pool.wait_ge(S["hist_ready"], 2 * NCB * (l + 1))
                pool.wait_ge(S["const_loaded"], 32)
                for i, (pooled, s0_, n) in enumerate(STATES):
                    pool.wait_ge(S["st_copied"], NST * l + i + 1)
                    rows, seg = (PHIST, PSEG) if pooled else (CHIST, CSEG)
                    kind = "pool" if pooled else "conv"
                    dst = a[f"new_{kind}_sample"][l] if n else a[f"new_{kind}_prompt"][l]
                    for j in range(max(n, 1)):
                        pool.dma_start(dst[s0_ + j], stage[j * seg:j * seg + rows, (i % 2) * CH:(i % 2 + 1) * CH])\
                            .then_inc(S[f"st_stored{i % 2}"], 16)
                pool.wait_ge(S["st_stored0"], 16 * STORES[0] * (l + 1))
                pool.wait_ge(S["st_stored1"], 16 * STORES[1] * (l + 1))
                for g in range(NCB):
                    w = 2 << g
                    for prompt in (True, False):
                        if prompt:
                            e = pext(g)[:, 0:PHIST + SEQ]
                            bufs = [win_a[:, 0:271], win_b[:, 0:271]]
                            sl = lambda ap, lo, hi: ap[:, lo:hi]
                            n = PHIST + SEQ
                        else:
                            e = pext(g)[:, PHIST + SEQ:].rearrange("p (s t) -> p s t", t=PSEG)
                            bufs = [b[:, 0:NSEQ * PSEG].rearrange("p (s t) -> p s t", t=PSEG) for b in (win_a, win_b)]
                            sl = lambda ap, lo, hi: ap[:, :, lo:hi]
                            n = PSEG
                        src, k = e, 1
                        for step in range(g + 1):
                            dst = bufs[step % 2]
                            link(pool.tensor_tensor(sl(dst, 2 * k - 1, n), sl(src, 2 * k - 1, n),
                                                    sl(src, k - 1, n - k), ALU.add))
                            src, k = dst, 2 * k
                        m = bufs[(g + 1) % 2]
                        link(pool.tensor_scalar(sl(m, PHIST, n), sl(src, PHIST, n), 1.0 / w, None, ALU.mult))
                        if prompt:
                            link(pool.tensor_tensor(m[:, PHIST:PHIST + w - 1], src[:, PHIST:PHIST + w - 1],
                                                    cinv[:, 0:w - 1], ALU.mult))
                        ins = pool.tensor_tensor(sl(e, PHIST, n), sl(m, PHIST, n), sl(e, PHIST, n), ALU.subtract)
                        if prompt:
                            link(ins)
                        else:
                            ins.then_inc(S["z_in"], 1)
                            pool.wait_ge(S["z_in"], 4 * l + g + 1)
                if l == 1:
                    pool.wait_ge(S["x_added"], 18)
                    pool.dma_start(gbc, a["norm_ffn"][1:2, :].to_broadcast([P, D])).then_inc(S["gbc_loaded"], 16)
                    pool.dma_start(iota, a["c_iota"]).then_inc(S["iota_loaded"], 16)


_INS = ["x_prompt", "x_sample", "state_conv", "state_pool", "norm_mix", "w_in", "conv_w", "conv_b", "conv_ln_g",
        "conv_ln_b", "pool_w", "pool_scale", "w_out", "norm_ffn", "dense_w_gate", "dense_w_up", "dense_w_down",
        "router_w", "router_b", "moe_w_gate", "moe_w_up", "moe_w_down", "norm_final"]
_OUTS = [("y_prompt", (1, SEQ, D)), ("y_sample", (NSEQ, DSEQ, D)), ("new_conv_prompt", (LAYERS, 1, CHIST, CH)),
         ("new_pool_prompt", (LAYERS, 1, PHIST, CH)), ("new_conv_sample", (LAYERS, NSEQ, CHIST, CH)),
         ("new_pool_sample", (LAYERS, NSEQ, PHIST, CH))]


def constants():
    i = np.arange(P)
    e = np.arange(NE)
    return {
        "c_ident": np.eye(P, dtype=np.float32),
        "c_tri": ((i[:, None] < i[None, :]) / float(CH)).astype(np.float32),
        "c_iota": np.broadcast_to(i, (P, P)).astype(np.float32),
        "c_inv": np.broadcast_to(1.0 / (np.arange(16) + 1.0), (P, 16)).astype(np.float32),
        "c_low": np.broadcast_to((e[None, :] < e[:, None]).reshape(1, -1), (P, NE * NE)).astype(np.float32),
    }


def kernel(**inputs):
    import numpy as _np
    import concourse.bacc as _bacc
    from concourse import mybir as _mybir
    from concourse.bass_utils import run_bass_kernel_spmd as _run

    nc = _bacc.Bacc("TRN2", target_bir_lowering=False, num_devices=1)
    arrays, args = {}, {}
    for name, value in list((n, inputs[n]) for n in _INS) + list(constants().items()):
        v = _np.ascontiguousarray(value)
        arrays[f"in_{name}"] = v
        args[name] = nc.dram_tensor(f"in_{name}", v.shape, _mybir.dt.from_np(v.dtype), kind="ExternalInput").ap()
    for name, shape in _OUTS:
        args[name] = nc.dram_tensor(f"out_{name}", shape, _mybir.dt.float32, kind="ExternalOutput").ap()
    build(nc, args)
    r = _run(nc, [arrays], core_ids=[0])
    return tuple(r.results[0][f"out_{name}"] for name, _ in _OUTS)
```

```python
from contextlib import ExitStack

import numpy as np

import concourse.bass as bass
from concourse import mybir

F32 = mybir.dt.float32
F32R = mybir.dt.float32r
I32 = mybir.dt.int32
ALU = mybir.AluOpType
ACT = mybir.ActivationFunctionType
AXX = mybir.AxisListType.X

P = 128
D = 1024
KD = D // P
SEQ = 256
NSEQ, DSEQ = 8, 16
TOK = SEQ + NSEQ * DSEQ
NTB = TOK // P
CH = 512
NCB = CH // P
TAPS = 31
CHIST = TAPS - 1
PHIST = 15
FF = 2816
FT = 256
NF = FF // FT
NE = 8
EPS = 1e-6
LAYERS = 2
TILE = 2048
CSEG = CHIST + DSEQ
CEXT = CHIST + SEQ + NSEQ * CSEG
PSEG = PHIST + DSEQ
PEXT = PHIST + SEQ + NSEQ * PSEG
WIN = TOK

C_MIX, C_FFN, C_CB, C_LG, C_LB, C_PS, C_CW = 0, 16, 32, 40, 48, 56, 64
NPRM = C_CW + LAYERS * TAPS * NCB

WIN_TILES = [4, 5, 0, 2, 1, 3]
WIN_BANK = [0, 1, 6, 7] * 3
P_BLK, A_BLK, B_BLK = [0, 1, 2, 3], [4, 5, 8, 9], [6, 7, 10, 11]
WOUT_TILES = [2, 3, 0, 1]
STATES = [(True, 0, 4), (True, 4, 4), (True, 0, 0), (False, 0, 3), (False, 3, 3), (False, 6, 2), (False, 0, 0)]
NST, NPST = len(STATES), 3
ST_BANK = [4, 5, 4, 0, 1, 6, 7]
Z_BANK = [0, 1, 6, 7]
PE_CONV = [2, 3]


def state_stores(i):
    return max(STATES[i][2], 1)


GEN_WIN = [[0] * 6, [8, 8, 8, 7, 6, 6]]
GEN_WOUT = [[1] * 4, [9, 9, 9, 8]]
GEN_DENSE = [2, 2, 2, 2, 1, 1]
GEN_MOE = [10, 10, 10, 9, 7, 7]

DENSE_UNITS = NF * NTB
PAIRS = NE // 2
SCATTER = {3: (0, 1), 4: (2, 3), 9: (4, 5)}


def build(nc, a):
    ctx = ExitStack()
    with ctx:
        base = 16512
        at = {}

        def place(name, floats, dt=F32, offset=None, parts=P):
            o = at["next"] if offset is None else offset
            t = nc.alloc_sbuf_tensor_at(name, [parts, floats], dt, offset=base + o)
            if offset is None:
                at["next"] = (o + floats * 4 + 31) // 32 * 32
            at[name] = o
            return t

        def sem(name):
            return ctx.enter_context(nc.semaphore(name))

        at["next"] = 0
        raw = place("raw", 6 * TILE)
        w_hi = place("w_hi", 6 * TILE, F32R)
        w_lo = place("w_lo", 6 * TILE, F32R)
        x = place("x", NTB * D)
        a_hi = place("a_hi", KD * TOK, F32R)
        a_lo = place("a_lo", KD * TOK, F32R)
        e_floats = NCB * (CEXT + PEXT)
        ext = place("ext", e_floats)
        ident = place("ident", P)
        mean_w = place("mean_w", P)
        prm = place("prm", NPRM)
        rw_hi = place("rw_hi", KD * NE, F32R)
        rw_lo = place("rw_lo", KD * NE, F32R)
        cinv = place("cinv", 16)
        stat = place("stat", 12)
        mhalf = place("mhalf", 1)
        eps = place("eps", 1)
        s0 = (at["next"] + 31) // 32 * 32
        hist = place("hist", 3 * CH, offset=s0)
        prm_rows = place("prm_rows", 3 * P, offset=s0)
        pool_w = place("pool_w", NCB * P, offset=s0)
        sgm = place("sgm", WIN, offset=s0 + 2048)
        win_a = place("win_a", 271, offset=s0 + 3584)
        win_b = place("win_b", 271, offset=s0 + 4704)
        stage_p = place("stage_p", CH, offset=s0)
        stage_c = place("stage_c", 2 * CH, offset=s0 + 2048)
        diag = [place("diag2", 32 * P, offset=at["w_hi"] + 4 * TILE * 4),
                place("diag3", 32 * P, offset=at["w_lo"] + 4 * TILE * 4)]
        ft_hi = place("ft_hi", 2 * FT, F32R, offset=s0)
        ft_lo = place("ft_lo", 2 * FT, F32R, offset=s0 + 2048)
        silu = place("silu", FT, offset=s0 + 4096)
        act_b = place("act_b", FT, offset=s0 + 5120)
        assert base + s0 + 6144 <= 229344
        oh, ol = at["a_hi"], at["a_lo"]
        pt = [place("pt0", NTB * P, F32R, offset=oh + 4096), place("pt1", NTB * P, F32R, offset=oh + 9728)]
        ye_hi = place("ye_hi", D, F32R, offset=oh + 5632)
        ye_lo = place("ye_lo", D, F32R, offset=ol + 5632)
        tri = place("tri", P, offset=s0)
        low = place("low", NE * NE, offset=s0 + 512)
        rb = place("rb", NE, offset=s0 + 768)
        cmp_gt = place("cmp_gt", NTB * NE * NE, offset=s0 + 1024)
        cmp_eq = place("cmp_eq", NTB * NE * NE, offset=s0 + 1792)
        rw_raw = place("rw_raw", KD * NE, offset=s0 + 2560)
        lg = place("lg", NTB * NE, offset=s0 + 2816)
        rank = place("rank", NTB * NE, offset=s0 + 2944)
        rmax = place("rmax", 2 * NTB, offset=s0 + 3072)
        rsum = place("rsum", 2 * NTB, offset=s0 + 3104)
        post = place("post", NTB * NE, offset=s0 + 3136)
        cnt_f = place("cnt_f", NE, offset=s0 + 3264)
        mask = place("mask", NTB * NE, offset=ol + 9728)
        gate = place("gate", NTB * NE, offset=ol + 9856)
        posb = place("posb", 3 * NTB * NE, offset=ol + 9984)
        cnt_i = place("cnt_i", NE, I32, offset=ol + 10272)
        h = ext[:, 0:NTB * D]
        onehot = ext[:, NTB * D:NTB * D + NTB * P]
        iota = ext[:, NTB * D + NTB * P + D:NTB * D + NTB * P + D + P]
        gbc = ext[:, NTB * D + NTB * P:NTB * D + NTB * P + D]

        def gate_e(tb):
            return gate[:, tb * NE:(tb + 1) * NE]

        ps = ctx.enter_context(nc.psum_tensor("ps", [P, 8, 512], F32))

        def cext(c):
            return ext[:, c * CEXT:(c + 1) * CEXT]

        def pext(g):
            o = NCB * CEXT + g * PEXT
            return ext[:, o:o + PEXT]

        def c_sample(c, off, n):
            return cext(c)[:, CHIST + SEQ:].rearrange("p (s t) -> p s t", t=CSEG)[:, :, off:off + n]

        def p_sample(g, off, n):
            return pext(g)[:, PHIST + SEQ:].rearrange("p (s t) -> p s t", t=PSEG)[:, :, off:off + n]

        def streams(ap):
            return ap.rearrange("p (s t) -> p s t", t=DSEQ)

        def y_sb(c):
            return ext[:, c * WIN:(c + 1) * WIN]

        def y_sq(c):
            o = NCB * CEXT + c * WIN
            return ext[:, o:o + WIN]

        def state_rows(i):
            pooled, _, n = STATES[i]
            rows, seg = (PHIST, PSEG) if pooled else (CHIST, CSEG)
            return rows + seg * max(n - 1, 0)

        def state_cols(i, c):
            pooled, s, n = STATES[i]
            e = pext(c) if pooled else cext(c)
            hist_n, seg = (PHIST, PSEG) if pooled else (CHIST, CSEG)
            o = SEQ if n == 0 else hist_n + SEQ + s * seg + DSEQ
            return e[:, o:o + state_rows(i)]

        S = {n: sem(n) for n in (
            "x_loaded const_loaded prm_loaded prm_turned prm_ready ssq_done ms_ready rstd_ready h_ready ht_done "
            "hT_hi hT_lo hist_loaded hist_turned hist_ready ext_zeroed blk_done sig_done gated "
            "p_done poolw_loaded conv_step conv_done pe_conv_done y_ready mean_done xc_done sq_done var_done "
            "sd_ready xn_done diag_ready c_done c_hi c_lo z_in z_done z_hi z_lo st_turned st_copied stp_stored stc_stored0 stc_stored1 y_blk mhalf_ready "
            "wout_used x_added gu_done silu_done act_done turned ft_hi_ready ft_lo_ready down_done "
            "gbc_loaded final_gain tri_loaded iota_loaded y_stored rw_loaded rw_hi_ready rw_lo_ready mean_w_ready rb_loaded low_loaded logits_done lg_ready "
            "exp_done mask_ready pos_done cnt_ready onehot_ready gathered pt_turned pt_ready xT_hi xT_lo "
            "ye_hi_ready ye_lo_ready scattered x_complete dve_chain act_chain pool_chain"
        ).split()}
        loaded = [sem(f"loaded{i}") for i in range(6)]
        hi_ready = [sem(f"hi_ready{i}") for i in range(6)]
        lo_ready = [sem(f"lo_ready{i}") for i in range(6)]

        def slot(t, i):
            return t[:, i * TILE:(i + 1) * TILE]

        def load(sp, s, uses, src, rows):
            if not isinstance(uses, int) or uses > 0:
                sp.wait_ge(lo_ready[s], uses)
            sp.dma_start(slot(raw, s).rearrange("p (k n) -> p k n", k=rows), src).then_inc(loaded[s], 16)

        def make_hi(act, s, uses):
            act.wait_ge(loaded[s], uses * 16 + 16)
            act.activation(slot(w_hi, s), slot(raw, s), ACT.Copy).then_inc(hi_ready[s], 1)

        def make_lo(dve, s, uses):
            dve.wait_ge(hi_ready[s], uses + 1)
            dve.tensor_tensor(slot(w_lo, s), slot(raw, s), slot(w_hi, s).bitcast(F32), ALU.subtract)\
               .then_inc(lo_ready[s], 1)

        def product(pe, out, lh, ll, rh, rl, start, stop):
            pe.matmul(out, lh, rh, start=start, stop=False)
            pe.matmul(out, lh, rl, start=False, stop=False)
            return pe.matmul(out, ll, rh, start=False, stop=stop)

        class Ffn:
            def __init__(self, nb, gens, units, off, K):
                self.nb, self.gens, self.units, self.off, self.K = nb, gens, units, off, K
                self.step = 0

            def at(self, k):
                return Ffn(self.nb, self.gens, self.units, self.off, self.K + k)

            def slot(self, kind, c):
                return 3 * ((self.off + c) % 2) + "gud".index(kind)

            def uses(self, kind, c):
                return self.gens[self.slot(kind, c)] + (self.off + c) // 2 + self.K

            def count(self, l):
                return self.units + self.nb * self.off + l + 2 * self.nb * self.K

            def bank(self, l):
                return 6 + (self.nb * self.off + l) % 2

            def buf(self, l):
                return (self.nb * self.off + l) % 2

            def tiles(self, l):
                c, tb = divmod(l, self.nb)
                if self.nb == 1:
                    return [("g", c + 1), ("u", c + 1), ("d", c - 1)]
                return [[("d", c)], [("g", c + 1)], [("u", c + 1)]][tb]

            def units_of(self, first, n):
                return range(self.nb * first, self.nb * (first + n))

        moe_w = {"g": a["moe_w_gate"], "u": a["moe_w_up"], "d": a["moe_w_down"]}
        dense_w = {"g": a["dense_w_gate"], "u": a["dense_w_up"], "d": a["dense_w_down"]}

        def ffn_src(w, kind, e, c):
            m = w[kind][0]
            if len(m.shape) == 3:
                if kind == "d":
                    rows = m.rearrange("e (c k p) n -> (e c) p k n", p=P, k=2)
                    return rows[bass.ds(e * NF + c, 1)].rearrange("o p k n -> (o p) k n")
                m = m[bass.ds(e, 1)].rearrange("o a b -> (o a) b")
            if kind == "d":
                return m[bass.ds(c * FT, FT), :].rearrange("(k p) n -> p k n", p=P)
            return m.rearrange("(k p) n -> p k n", p=P)[:, :, bass.ds(c * FT, FT)]

        def sp_tile(sp, f, w, e, kind, c, c_expr):
            load(sp, f.slot(kind, c), f.uses(kind, c), ffn_src(w, kind, e, c_expr), 2 if kind == "d" else KD)

        def sp_dense(sp, f):
            for kind in "gu":
                sp_tile(sp, f, dense_w, 0, kind, 0, 0)

            def tiles(g, l, shift, k):
                for kind, c in g.tiles(l):
                    if c + shift < NF:
                        sp_tile(sp, g, dense_w, 0, kind, c, k + c)
            for l in f.units_of(0, 3):
                tiles(f, l, 0, 0)
            with sp.Fori(0, 3) as k:
                for l in f.units_of(3, 2):
                    tiles(f.at(k), l, 0, 2 * k)
            for l in f.units_of(3, 2):
                tiles(f.at(3), l, 6, 6)

        def units_loop(eng, f, fn):
            head = 3 if f.nb > 1 else 5
            rounds = (NF - head - 2) // 2
            for l in f.units_of(0, head):
                fn(f, l, 0)
            with eng.Fori(0, rounds) as k:
                for l in f.units_of(head, 2):
                    g = f.at(k)
                    g.step = 2 * k
                    fn(g, l, 0)
            for l in f.units_of(head, 2):
                fn(f.at(rounds), l, 2 * rounds)

        class Item:
            def __init__(self, n, e, blk, parity, prev, nxt):
                self.n, self.e, self.blk, self.parity, self.prev, self.nxt = n, e, blk, parity, prev, nxt

        def run_pair(eng, unit, p, spec, first, more):
            for b in range(2):
                prev = None if first and b == 0 else spec(b - 1)
                nxt = spec(b + 1) if more or b == 0 else None
                item = Item(*spec(b), b, prev, nxt)
                units_loop(eng, Ffn(1, GEN_MOE, DENSE_UNITS, NF * b, NF * p),
                           lambda f, l, shift: unit(f, l, shift, item))

        def wanted(f, kind, c, shift, item):
            if c + shift < 0:
                return item is not None and item.prev is not None
            if c + shift >= NF:
                return item is not None and item.nxt is not None
            return True

        def mixture(eng, start, unit, finish):
            def pair(p, first, more):
                spec = lambda j: (2 * p + j, 2 * p + j, 0)
                if first:
                    start(p, spec(0))
                run_pair(eng, unit, p, spec, first, more)
                if not more:
                    finish(Ffn(1, GEN_MOE, DENSE_UNITS, NF, NF * p), Item(*spec(1), 1, None, None))
            pair(0, True, True)
            with eng.Fori(1, PAIRS - 1) as p:
                pair(p, False, True)
            pair(PAIRS - 1, False, False)

            def body(done, e):
                spec = lambda j: (2 * done + j, e, 1 + j)
                start(done, spec(0))
                run_pair(eng, unit, done, spec, True, False)
                finish(Ffn(1, GEN_MOE, DENSE_UNITS, NF, NF * done), Item(*spec(1), 1, None, None))
            overflow(eng, body)

        dense = Ffn(NTB, GEN_DENSE, 0, 0, 0)

        def overflow(eng, body):
            done = eng.alloc_register("pairs_done")
            eng.reg_mov(done, PAIRS)
            eng.wait_ge(S["cnt_ready"], 1)
            with eng.Fori(0, NE) as e:
                n = eng.value_load(cnt_i[0:1, bass.ds(e, 1)], min_val=0, max_val=TOK)
                with eng.If(n > P):
                    body(eng.snap(done, min_val=PAIRS, max_val=PAIRS + NE), e)
                    eng.reg_add(done, done, 1)

        block = ctx.enter_context(nc.Block())

        @block.sync
        def _(sp):
            xp = a["x_prompt"][0].rearrange("(t p) d -> t p d", p=P)
            for tb, src in enumerate((xp[0], xp[1], a["x_sample"].rearrange("s t d -> (s t) d"))):
                sp.dma_start(x[:, tb * D:(tb + 1) * D], src).then_inc(S["x_loaded"], 16)
            for l in range(LAYERS):
                w = a["w_in"][l].rearrange("(k p) n -> p k n", p=P)
                for s, t in enumerate(WIN_TILES):
                    load(sp, s, GEN_WIN[l][s], w[:, :, t * 256:(t + 1) * 256], KD)
                w = a["w_out"][l].rearrange("(t k p) n -> t p k n", p=P, k=2)
                for s, t in enumerate(WOUT_TILES):
                    load(sp, s, GEN_WOUT[l][s], w[t], 2)
                if l == 0:
                    sp_dense(sp, dense)

            def start(p, spec):
                f = Ffn(1, GEN_MOE, DENSE_UNITS, 0, NF * p)
                for kind in "gu":
                    sp_tile(sp, f, moe_w, spec[1], kind, 0, 0)

            def unit(f, l, shift, item):
                for kind, c in f.tiles(l):
                    if wanted(f, kind, c, shift, item):
                        t = c + shift
                        e = item.prev[1] if t < 0 else item.nxt[1] if t >= NF else item.e
                        sp_tile(sp, f, moe_w, e, kind, c, f.step + t % NF if t != t % NF else f.step + t)

            def finish(f, item):
                sp_tile(sp, f, moe_w, item.e, "d", NF - 1, NF - 1)
            mixture(sp, start, unit, finish)

        def act_norm(act, n):
            for tb in range(NTB):
                if n == 0:
                    act.wait_ge(S["x_loaded"], 16 * NTB)
                elif n < 4:
                    act.wait_ge(S["x_added"], 6 * (n - 1) + 2 * tb + 2)
                act.activation(ext[:, tb * D:(tb + 1) * D], x[:, tb * D:(tb + 1) * D], ACT.Square,
                               accum_out=stat[:, tb:tb + 1]).then_inc(S["ssq_done"], 1)

        def act_hT(act, n, gcol):
            for k in range(KD):
                act.wait_ge(S["ht_done"], KD * n + k + 1)
                scale = 1.0 if gcol is None else prm[:, gcol + k:gcol + k + 1]
                act.activation(a_hi[:, k * TOK:(k + 1) * TOK], ps[:, 6 + k % 2, 0:TOK], ACT.Copy, scale=scale)\
                   .then_inc(S["hT_hi"], 1)

        def act_ffn_tile(act, f, kind, c):
            done = f.count(f.nb * (c - 1))
            if not isinstance(done, int) or done > 0:
                act.wait_ge(S["down_done" if kind == "d" else "gu_done"], done)
            make_hi(act, f.slot(kind, c), f.uses(kind, c))

        def act_silu(act, f, l):
            act.wait_ge(S["gu_done"], f.count(l + 1))
            if not isinstance(f.K, int) or f.count(l) > 0:
                act.wait_ge(S["act_done"], f.count(l))
            act.activation(silu[:, :], ps[:, f.bank(l), 0:FT], ACT.Silu).then_inc(S["silu_done"], 1)

        def act_ft(act, f, l):
            act.wait_ge(S["turned"], f.count(l + 1))
            if not isinstance(f.K, int) or f.count(l - 1) > 0:
                act.wait_ge(S["down_done"], f.count(l - 1))
            b = f.buf(l)
            act.activation(ft_hi[:, b * FT:(b + 1) * FT], ps[:, f.bank(l), 0:FT], ACT.Copy)\
               .then_inc(S["ft_hi_ready"], 1)

        def act_unit(act, f, l, shift, item):
            true = l + shift if item is not None and isinstance(f.step, int) else None
            prev = item is not None and item.prev is not None
            before = l > 0 or prev
            if true == 1:
                act.wait_ge(S["pt_turned"], item.n + 1)
                act.activation(pt[item.parity][:, :], ps[:, 4, 0:NTB * P], ACT.Copy).then_inc(S["pt_ready"], 1)
            if before:
                act_silu(act, f, l - 1)
            if true == 2 and prev:
                act_ye(act, f.count(0), item.prev[0])
            t = f.tiles(l)
            for i, (kind, c) in enumerate(t):
                if i == 2 and true == NF - 1 and item.nxt is not None:
                    act_xT(act, f.count(l + 1), item.nxt[0])
                if i == 2 and before:
                    act_ft(act, f, l - 1)
                if wanted(f, kind, c, shift, item):
                    act_ffn_tile(act, f, kind, c)
            if len(t) == 1 and before:
                act_ft(act, f, l - 1)

        def act_xT(act, done, n):
            act.wait_ge(S["gu_done"], done)
            for i in range(2):
                act.wait_ge(S["gathered"], 2 * n + i + 1)
                act.activation(a_hi[:, i * 512:(i + 1) * 512], ps[:, 2 + i, :], ACT.Copy).then_inc(S["xT_hi"], 1)

        def act_ye(act, done, n):
            act.wait_ge(S["down_done"], done)
            if not isinstance(n, int) or n > 0:
                act.wait_ge(S["scattered"], 6 * n)
            for i in range(2):
                act.activation(ye_hi[:, i * 512:(i + 1) * 512], ps[:, i, :], ACT.Copy).then_inc(S["ye_hi_ready"], 1)

        @block.scalar
        def _(act):
            chain = [0]

            def link(ins):
                chain[0] += 1
                ins.then_inc(S["act_chain"], 1)
                act.wait_ge(S["act_chain"], chain[0])

            act.dma_start(ident[:, :], a["c_ident"]).then_inc(S["const_loaded"], 16)
            act.dma_start(cinv[:, :], a["c_inv"]).then_inc(S["const_loaded"], 16)
            r = 0
            for name in ("norm_mix", "norm_ffn", "conv_b", "conv_ln_g", "conv_ln_b", "pool_scale"):
                rows = a[name].rearrange("l (k p) -> (l k) p", p=P)
                n = rows.shape[0]
                act.dma_start(prm_rows[r:r + n, 0:P], rows).then_inc(S["prm_loaded"], 16)
                r += n
            for l in range(LAYERS):
                act.dma_start(prm_rows[0:TAPS * NCB, (1 + l) * P:(2 + l) * P],
                              a["conv_w"][l].rearrange("j (c p) -> (j c) p", p=P)).then_inc(S["prm_loaded"], 16)
            for l in range(LAYERS):
                if l:
                    act.wait_ge(S["gu_done"], DENSE_UNITS)
                    act.wait_ge(S["down_done"], DENSE_UNITS)
                else:
                    act_norm(act, 0)
                for s in range(2):
                    make_hi(act, s, GEN_WIN[l][s])
                if l == 0:
                    act.wait_ge(S["prm_turned"], 1)
                    act.activation(prm[:, :], ps[:, 0, 0:NPRM], ACT.Copy).then_inc(S["prm_ready"], 1)
                    act.wait_ge(S["prm_ready"], 1)
                else:
                    act_norm(act, 2)
                act.dma_start(hist[0:120, 0:2 * CH].rearrange("p (g c) -> p g c", g=2),
                              a["state_conv"][l].rearrange("(g s) t c -> (s t) g c", g=2))\
                   .then_inc(S["hist_loaded"], 16)
                act.dma_start(hist[0:120, 2 * CH:3 * CH], a["state_pool"][l].rearrange("s t c -> (s t) c"))\
                   .then_inc(S["hist_loaded"], 16)
                act_hT(act, 2 * l, C_MIX + KD * l)
                for s in range(2, 4):
                    make_hi(act, s, GEN_WIN[l][s])
                for c in range(NCB):
                    act.wait_ge(S["hist_turned"], NCB * l + c + 1)
                    act.activation(c_sample(c, 0, CHIST), ps[:, 2 + c, 0:240].rearrange("p (s t) -> p s t", t=CHIST),
                                   ACT.Copy).then_inc(S["hist_ready"], 1)
                    act.activation(p_sample(c, 0, PHIST), ps[:, 2 + c, 240:360].rearrange("p (s t) -> p s t", t=PHIST),
                                   ACT.Copy).then_inc(S["hist_ready"], 1)
                for s in range(4, 6):
                    make_hi(act, s, GEN_WIN[l][s])
                act.wait_ge(S["ext_zeroed"], 2 * l + 2)
                for g in range(NCB):
                    bank = WIN_BANK[P_BLK[g]]
                    act.wait_ge(S["blk_done"], 12 * l + P_BLK[g] + 1)
                    act.activation(pext(g)[:, PHIST:PHIST + SEQ], ps[:, bank, 0:SEQ], ACT.Copy)\
                       .then_inc(S["p_done"], 1)
                    act.activation(p_sample(g, PHIST, DSEQ), streams(ps[:, bank, SEQ:TOK]), ACT.Copy)\
                       .then_inc(S["p_done"], 1)
                for s in range(2):
                    act.wait_ge(S["blk_done"], 12 * l + 2 * s + 2)
                    make_hi(act, s, GEN_WOUT[l][s])
                stored = l * sum(state_stores(i) for i in range(NPST))
                for i in range(NPST):
                    act.wait_ge(S["st_turned"], NST * l + i + 1)
                    if stored:
                        act.wait_ge(S["stp_stored"], 16 * stored)
                    act.activation(stage_p[0:state_rows(i), :], ps[0:state_rows(i), ST_BANK[i], 0:CH], ACT.Copy)\
                       .then_inc(S["st_copied"], 1)
                    stored += state_stores(i)

                def sigmoid(c):
                    act.wait_ge(S["blk_done"], 12 * l + B_BLK[c] + 1)
                    if 4 * l + c:
                        act.wait_ge(S["gated"], 4 * l + c)
                    act.activation(sgm[:, :], ps[:, WIN_BANK[B_BLK[c]], 0:TOK], ACT.Sigmoid)\
                       .then_inc(S["sig_done"], 1)
                sigmoid(0)
                sigmoid(1)
                act.wait_ge(S["stp_stored"], 16 * stored)
                act.dma_start(pool_w[:, :].rearrange("p (g d) -> p g d", g=NCB),
                              a["pool_w"][l].rearrange("g c d -> c g d")).then_inc(S["poolw_loaded"], 16)
                for s in range(2, 4):
                    act.wait_ge(S["blk_done"], 12 * l + 2 * s + 2)
                    make_hi(act, s, GEN_WOUT[l][s])
                sigmoid(2)
                sigmoid(3)
                act.wait_ge(S["blk_done"], 12 * (l + 1))
                for i, c in enumerate(PE_CONV):
                    for j in range(TAPS):
                        col = C_CW + (l * TAPS + j) * NCB + c
                        act.activation(diag[i][:, j * P:(j + 1) * P], ident[:, :], ACT.Copy,
                                       scale=prm[:, col:col + 1]).then_inc(S["diag_ready"], 1)
                act.wait_ge(S["gated"], 4 * l + 4)
                act.wait_ge(S["z_in"], 4 * l + 4)
                count = [l * sum(state_stores(i) for i in range(NPST + b, NST, 2)) for b in range(2)]
                for i in range(NPST, NST):
                    n, b = state_rows(i), (i - NPST) % 2
                    act.wait_ge(S["st_turned"], NST * l + i + 1)
                    if count[b]:
                        act.wait_ge(S[f"stc_stored{b}"], 16 * count[b])
                    act.activation(stage_c[0:n, b * CH:(b + 1) * CH], ps[0:n, ST_BANK[i], 0:CH], ACT.Copy)\
                       .then_inc(S["st_copied"], 1)
                    count[b] += state_stores(i)
                for g in range(NCB):
                    act.wait_ge(S["z_done"], 4 * l + g + 1)
                    act.activation(a_hi[:, (4 + g) * TOK:(5 + g) * TOK], ps[:, Z_BANK[g], 0:TOK], ACT.Copy,
                                   scale=prm[:, C_PS + 4 * l + g:C_PS + 4 * l + g + 1]).then_inc(S["z_hi"], 1)
                act.wait_ge(S["conv_done"], 2 * l + 2)
                act.wait_ge(S["pe_conv_done"], 2 * l + 2)
                for c in range(NCB):
                    act.activation(y_sb(c), ps[:, 2 + c, 0:TOK], ACT.Identity,
                                   bias=prm[:, C_CB + 4 * l + c:C_CB + 4 * l + c + 1]).then_inc(S["y_ready"], 1)
                for c in range(NCB):
                    act.wait_ge(S["xc_done"], 4 * l + c + 1)
                    act.activation(y_sq(c), y_sb(c), ACT.Square).then_inc(S["sq_done"], 1)
                act.wait_ge(S["var_done"], l + 1)
                for b in range(2):
                    act.wait_ge(S[f"stc_stored{b}"], 16 * count[b])
                act.activation(sgm[:, :], ps[:, 7, 0:TOK], ACT.Sqrt, bias=eps[:, 0:1]).then_inc(S["sd_ready"], 1)
                for c in range(NCB):
                    act.wait_ge(S["xn_done"], 4 * l + c + 1)
                    act.activation(y_sb(c), y_sb(c), ACT.Silu, scale=prm[:, C_LG + 4 * l + c:C_LG + 4 * l + c + 1],
                                   bias=prm[:, C_LB + 4 * l + c:C_LB + 4 * l + c + 1]).then_inc(S["c_done"], 1)
                for c in range(NCB):
                    act.wait_ge(S["c_done"], 4 * l + c + 1)
                    act.activation(a_hi[:, c * TOK:(c + 1) * TOK], y_sb(c), ACT.Copy).then_inc(S["c_hi"], 1)
                if l == 0:
                    act.wait_ge(S["wout_used"], 2)
                    for kind in "gu":
                        act_ffn_tile(act, dense, kind, 0)
                    act_norm(act, 1)
                    act_hT(act, 1, C_FFN)
                    act.wait_ge(S["wout_used"], 3)
                    units_loop(act, dense, lambda f, l, shift: act_unit(act, f, l, shift, None))
                    act_silu(act, dense, DENSE_UNITS - 1)
                    act_ft(act, dense, DENSE_UNITS - 1)
            act.wait_ge(S["wout_used"], 5)
            for kind in "gu":
                act_ffn_tile(act, Ffn(1, GEN_MOE, DENSE_UNITS, 0, 0), kind, 0)
            act.wait_ge(S["x_added"], 14)
            act.dma_start(rw_raw[:, :].rearrange("p (k e) -> p k e", k=KD),
                          a["router_w"][0].rearrange("(k p) e -> p k e", p=P)).then_inc(S["rw_loaded"], 16)
            act.dma_start(tri[:, :], a["c_tri"]).then_inc(S["tri_loaded"], 16)
            act.dma_start(low[:, :], a["c_low"]).then_inc(S["low_loaded"], 16)
            act.dma_start(rb[:, :], a["router_b"].to_broadcast([P, NE])).then_inc(S["rb_loaded"], 16)
            act_norm(act, 3)
            act.wait_ge(S["rw_loaded"], 16)
            act.activation(rw_hi[:, :], rw_raw[:, :], ACT.Copy).then_inc(S["rw_hi_ready"], 1)
            act_hT(act, 3, None)
            act.wait_ge(S["lg_ready"], 1)
            for tb in range(NTB):
                act.activation(gate_e(tb), lg[:, tb * NE:(tb + 1) * NE], ACT.Exp,
                               bias=rmax[:, NTB + tb:NTB + tb + 1]).then_inc(S["exp_done"], 1)
            act.wait_ge(S["wout_used"], 6)

            def start(p, spec):
                f = Ffn(1, GEN_MOE, DENSE_UNITS, 0, NF * p)
                if not (isinstance(p, int) and p == 0):
                    for kind in "gu":
                        act_ffn_tile(act, f, kind, 0)
                act_xT(act, f.count(0), spec[0])

            def finish(f, item):
                act_silu(act, f, NF - 1)
                act_ffn_tile(act, f, "d", NF - 1)
                act_ft(act, f, NF - 1)
                act_ye(act, f.count(NF), item.n)
            mixture(act, start, lambda f, l, shift, item: act_unit(act, f, l, shift, item), finish)
            act.wait_ge(S["x_complete"], 1)
            for tb in range(NTB):
                act.activation(ext[:, tb * D:(tb + 1) * D], x[:, tb * D:(tb + 1) * D], ACT.Square,
                               accum_out=stat[:, tb:tb + 1]).then_inc(S["ssq_done"], 1)
            act.dma_start(gbc, a["norm_final"].rearrange("(o d) -> o d", o=1).to_broadcast([P, D]))\
               .then_inc(S["final_gain"], 16)
            yp = a["y_prompt"][0].rearrange("(t p) d -> t p d", p=P)
            dst = [yp[0], yp[1], a["y_sample"].rearrange("s t d -> (s t) d")]
            for tb in range(NTB):
                act.wait_ge(S["h_ready"], 4 * NTB + tb + 1)
                act.dma_start(dst[tb], h[:, tb * D:(tb + 1) * D]).then_inc(S["y_stored"], 16)
            act.wait_ge(S["y_stored"], 16 * NTB)
            act.wait_ge(S["stp_stored"], 16 * LAYERS * sum(state_stores(i) for i in range(NPST)))
            for b in range(2):
                act.wait_ge(S[f"stc_stored{b}"], 16 * LAYERS * sum(state_stores(i) for i in range(NPST + b, NST, 2)))

        @block.vector
        def _(dve):
            chain = [0]

            def link(ins):
                chain[0] += 1
                ins.then_inc(S["dve_chain"], 1)
                dve.wait_ge(S["dve_chain"], chain[0])

            def dve_norm(n, gain=None):
                dve.wait_ge(S["ssq_done"], NTB * (n + 1))
                ms, r = stat[:, 3:6], stat[:, 6:9]
                dve.tensor_scalar(ms, stat[:, 0:3], 1.0 / D, EPS, ALU.mult, ALU.add).then_inc(S["ms_ready"], 1)
                dve.wait_ge(S["rstd_ready"], n + 1)
                if gain is not None:
                    dve.wait_ge(S[gain], 16)
                for tb in range(NTB):
                    o, i = h[:, tb * D:(tb + 1) * D], x[:, tb * D:(tb + 1) * D]
                    if gain is None:
                        dve.tensor_scalar(o, i, r[:, tb:tb + 1], None, ALU.mult).then_inc(S["h_ready"], 1)
                    else:
                        dve.scalar_tensor_tensor(out=o, in0=i, scalar=r[:, tb:tb + 1], in1=gbc, op0=ALU.mult,
                                                 op1=ALU.mult).then_inc(S["h_ready"], 1)

            def dve_hT(n, gcol):
                for k in range(KD):
                    dve.wait_ge(S["hT_hi"], KD * n + k + 1)
                    o, hi, src = (a_lo[:, k * TOK:(k + 1) * TOK], a_hi[:, k * TOK:(k + 1) * TOK].bitcast(F32),
                                  ps[:, 6 + k % 2, 0:TOK])
                    if gcol is None:
                        ins = dve.tensor_tensor(o, src, hi, ALU.subtract)
                    else:
                        ins = dve.scalar_tensor_tensor(out=o, in0=src, scalar=prm[:, gcol + k:gcol + k + 1], in1=hi,
                                                       op0=ALU.mult, op1=ALU.subtract)
                    ins.then_inc(S["hT_lo"], 1)

            def gated(l, c):
                bank = WIN_BANK[A_BLK[c]]
                dve.wait_ge(S["sig_done"], 4 * l + c + 1)
                if c == 0:
                    dve.wait_ge(S["ext_zeroed"], 2 * l + 2)
                dve.tensor_tensor(cext(c)[:, CHIST:CHIST + SEQ], ps[:, bank, 0:SEQ], sgm[:, 0:SEQ], ALU.mult)
                dve.tensor_tensor(c_sample(c, CHIST, DSEQ), streams(ps[:, bank, SEQ:TOK]), streams(sgm[:, SEQ:TOK]),
                                  ALU.mult).then_inc(S["gated"], 1)

            steps = [0]

            def conv(l, c, first, end):
                if first == 0:
                    dve.wait_ge(S["gated"], 4 * l + c + 1)
                    dve.wait_ge(S["hist_ready"], 2 * NCB * (l + 1))
                dst = ps[:, 2 + c, 0:SEQ], streams(ps[:, 2 + c, SEQ:TOK])
                for j in range(first, end):
                    col = C_CW + (l * TAPS + j) * NCB + c
                    w = prm[:, col:col + 1]
                    for o, src in zip(dst, (cext(c)[:, j:j + SEQ], c_sample(c, j, DSEQ))):
                        if j == 0:
                            ins = dve.tensor_scalar(o, src, w, None, ALU.mult)
                        else:
                            dve.wait_ge(S["conv_step"], steps[0] - 1)
                            ins = dve.scalar_tensor_tensor(out=o, in0=src, scalar=w, in1=o, op0=ALU.mult, op1=ALU.add)
                        ins.then_inc(S["conv_step"], 1)
                        steps[0] += 1
                if end == TAPS:
                    dve.wait_ge(S["conv_step"], steps[0])
                    dve.sem_inc(S["conv_done"], 1)

            def tile_lo(f, kind, c):
                make_lo(dve, f.slot(kind, c), f.uses(kind, c))

            def act_mul(f, l):
                dve.wait_ge(S["silu_done"], f.count(l + 1))
                if not isinstance(f.K, int) or f.count(l) > 0:
                    dve.wait_ge(S["turned"], f.count(l))
                dve.tensor_tensor(act_b[:, :], ps[:, f.bank(l), FT:2 * FT], silu[:, :], ALU.mult)\
                   .then_inc(S["act_done"], 1)

            def ft_low(f, l):
                dve.wait_ge(S["ft_hi_ready"], f.count(l + 1))
                b = f.buf(l)
                dve.tensor_tensor(ft_lo[:, b * FT:(b + 1) * FT], ps[:, f.bank(l), 0:FT],
                                  ft_hi[:, b * FT:(b + 1) * FT].bitcast(F32), ALU.subtract)\
                   .then_inc(S["ft_lo_ready"], 1)

            def dve_unit(f, l, shift, item):
                true = l + shift if item is not None and isinstance(f.step, int) else None
                prev = item is not None and item.prev is not None
                before = l > 0 or prev
                if before:
                    act_mul(f, l - 1)
                if true == 2 and prev:
                    dve_ye(item.prev[0])
                if true == 2 and item.nxt is not None:
                    dve.wait_ge(S["pt_turned"], item.n + 1)
                    one_hot(*item.nxt)
                t = f.tiles(l)
                for i, (kind, c) in enumerate(t):
                    if i == 2 and true == NF - 1 and item.nxt is not None:
                        dve_xT(item.nxt[0])
                    if i == 2 and before:
                        ft_low(f, l - 1)
                    if wanted(f, kind, c, shift, item):
                        tile_lo(f, kind, c)
                if len(t) == 1 and before:
                    ft_low(f, l - 1)
                if prev and true in SCATTER:
                    add_expert(item.prev, SCATTER[true])

            def one_hot(n, e, blk):
                for tb in range(NTB):
                    ins = dve.tensor_scalar(onehot[:, tb * P:(tb + 1) * P], iota,
                                            posb[:, bass.ds(e + (blk * NTB * NE + tb * NE), 1)], None, ALU.is_equal)
                ins.then_inc(S["onehot_ready"], 1)

            def dve_xT(n):
                for i in range(2):
                    dve.wait_ge(S["xT_hi"], 2 * n + i + 1)
                    dve.tensor_tensor(a_lo[:, i * 512:(i + 1) * 512], ps[:, 2 + i, :],
                                      a_hi[:, i * 512:(i + 1) * 512].bitcast(F32), ALU.subtract).then_inc(S["xT_lo"], 1)

            def dve_ye(n):
                for i in range(2):
                    dve.wait_ge(S["ye_hi_ready"], 2 * n + i + 1)
                    dve.tensor_tensor(ye_lo[:, i * 512:(i + 1) * 512], ps[:, i, :],
                                      ye_hi[:, i * 512:(i + 1) * 512].bitcast(F32), ALU.subtract)\
                       .then_inc(S["ye_lo_ready"], 1)

            def add_expert(spec, pieces):
                n, e, _ = spec
                for i in pieces:
                    tb, dh = divmod(i, 2)
                    o = x[:, tb * D + dh * 512:tb * D + dh * 512 + 512]
                    dve.wait_ge(S["scattered"], 6 * n + i + 1)
                    dve.scalar_tensor_tensor(out=o, in0=ps[:, 4 + i % 2, :],
                                             scalar=gate[:, bass.ds(e + tb * NE, 1)], in1=o,
                                             op0=ALU.mult, op1=ALU.add).then_inc(S["x_added"], 1)

            def add_y(tb):
                for dh in range(2):
                    o = x[:, tb * D + dh * 512:tb * D + dh * 512 + 512]
                    dve.tensor_tensor(o, o, ps[:, 2 * tb + dh, :], ALU.add).then_inc(S["x_added"], 1)

            dve.memset(mean_w[:, :], 1.0 / CH).then_inc(S["mean_w_ready"], 1)
            dve.memset(eps[:, :], EPS).then_inc(S["mean_w_ready"], 1)
            dve.memset(mhalf[:, :], -0.5).then_inc(S["mhalf_ready"], 1)
            for l in range(LAYERS):
                if l == 0:
                    dve_norm(0)
                for s in range(2):
                    make_lo(dve, s, GEN_WIN[l][s])
                if l:
                    dve_norm(2)
                dve.wait_ge(S["prm_ready"], 1)
                dve_hT(2 * l, C_MIX + KD * l)
                for s in range(2, 6):
                    make_lo(dve, s, GEN_WIN[l][s])
                for s in range(2):
                    make_lo(dve, s, GEN_WOUT[l][s])
                gated(l, 0)
                gated(l, 1)
                conv(l, 0, 0, 14)
                gated(l, 2)
                gated(l, 3)
                for s in range(2, 4):
                    make_lo(dve, s, GEN_WOUT[l][s])
                conv(l, 0, 14, TAPS)
                conv(l, 1, 0, TAPS)
                for g in range(NCB):
                    dve.wait_ge(S["z_hi"], 4 * l + g + 1)
                    o = (4 + g) * TOK
                    dve.scalar_tensor_tensor(out=a_lo[:, o:o + TOK], in0=ps[:, Z_BANK[g], 0:TOK],
                                             scalar=prm[:, C_PS + 4 * l + g:C_PS + 4 * l + g + 1],
                                             in1=a_hi[:, o:o + TOK].bitcast(F32), op0=ALU.mult,
                                             op1=ALU.subtract).then_inc(S["z_lo"], 1)
                dve.wait_ge(S["mean_done"], l + 1)
                for c in range(NCB):
                    dve.tensor_tensor(y_sb(c), y_sb(c), ps[:, 6, 0:TOK], ALU.subtract).then_inc(S["xc_done"], 1)
                dve.wait_ge(S["sd_ready"], l + 1)
                link(dve.reciprocal(sgm[:, :], sgm[:, :]))
                dve.wait_ge(S["sq_done"], 4 * l + 4)
                for c in range(NCB):
                    dve.tensor_tensor(y_sb(c), y_sb(c), sgm[:, :], ALU.mult).then_inc(S["xn_done"], 1)
                for c in range(NCB):
                    dve.wait_ge(S["c_hi"], 4 * l + c + 1)
                    dve.tensor_tensor(a_lo[:, c * TOK:(c + 1) * TOK], y_sb(c),
                                      a_hi[:, c * TOK:(c + 1) * TOK].bitcast(F32), ALU.subtract).then_inc(S["c_lo"], 1)
                if l == 0:
                    for kind in "gu":
                        tile_lo(dense, kind, 0)
                for tb in range(NTB):
                    dve.wait_ge(S["y_blk"], NTB * l + tb + 1)
                    add_y(tb)
                if l == 0:
                    dve_norm(1)
                    dve_hT(1, C_FFN)
                    units_loop(dve, dense, lambda f, l, shift: dve_unit(f, l, shift, None))
                    act_mul(dense, DENSE_UNITS - 1)
                    ft_low(dense, DENSE_UNITS - 1)
                    for tb in range(NTB):
                        dve.wait_ge(S["down_done"], DENSE_UNITS - NTB + tb + 1)
                        add_y(tb)
            for kind in "gu":
                tile_lo(Ffn(1, GEN_MOE, DENSE_UNITS, 0, 0), kind, 0)
            dve_norm(3, "gbc_loaded")
            dve.wait_ge(S["rw_hi_ready"], 1)
            dve.tensor_tensor(rw_lo[:, :], rw_raw[:, :], rw_hi[:, :].bitcast(F32), ALU.subtract)\
               .then_inc(S["rw_lo_ready"], 1)
            dve_hT(3, None)
            dve.wait_ge(S["logits_done"], 1)
            dve.wait_ge(S["rb_loaded"], 16)
            dve.wait_ge(S["low_loaded"], 16)
            for tb in range(NTB):
                ins = dve.tensor_tensor(lg[:, tb * NE:(tb + 1) * NE], ps[:, 2, tb * NE:(tb + 1) * NE], rb[:, :], ALU.add)
            link(ins)
            link(dve.tensor_reduce(rmax[:, 0:NTB], lg[:, :].rearrange("p (t e) -> p t e", e=NE), AXX, ALU.max))
            dve.tensor_scalar(rmax[:, NTB:2 * NTB], rmax[:, 0:NTB], -1.0, None, ALU.mult).then_inc(S["lg_ready"], 1)
            m4 = lambda t: t[:, :].rearrange("p (t e j) -> p t e j", e=NE, j=NE)
            l3 = lg[:, :].rearrange("p (t e) -> p t e", e=NE)
            for tb in range(NTB):
                other = l3[:, tb].unsqueeze(1).to_broadcast([P, NE, NE])
                own = l3[:, tb].unsqueeze(2).to_broadcast([P, NE, NE])
                dve.tensor_tensor(m4(cmp_gt)[:, tb], other, own, ALU.is_gt)
                ins = dve.tensor_tensor(m4(cmp_eq)[:, tb], other, own, ALU.is_equal)
            link(ins)
            for tb in range(NTB):
                ins = dve.tensor_tensor(cmp_eq[:, tb * NE * NE:(tb + 1) * NE * NE],
                                        cmp_eq[:, tb * NE * NE:(tb + 1) * NE * NE], low[:, :], ALU.mult)
            link(ins)
            link(dve.tensor_tensor(cmp_gt[:, :], cmp_gt[:, :], cmp_eq[:, :], ALU.add))
            link(dve.tensor_reduce(rank[:, :], cmp_gt[:, :].rearrange("p (t j) -> p t j", j=NE), AXX, ALU.add))
            dve.tensor_scalar(mask[:, :], rank[:, :], 2.0, None, ALU.is_lt).then_inc(S["mask_ready"], 1)
            dve.wait_ge(S["mask_ready"], 1)
            dve.wait_ge(S["exp_done"], NTB)
            link(dve.tensor_tensor(gate[:, :], gate[:, :], mask[:, :], ALU.mult))
            link(dve.tensor_reduce(rsum[:, 0:NTB], gate[:, :].rearrange("p (t e) -> p t e", e=NE), AXX, ALU.add))
            link(dve.reciprocal(rsum[:, NTB:2 * NTB], rsum[:, 0:NTB]))
            for tb in range(NTB):
                ins = dve.tensor_scalar(gate[:, tb * NE:(tb + 1) * NE], gate[:, tb * NE:(tb + 1) * NE],
                                        rsum[:, NTB + tb:NTB + tb + 1], None, ALU.mult)
            link(ins)
            dve.wait_ge(S["iota_loaded"], 16)
            dve.wait_ge(S["pos_done"], 1)
            link(dve.tensor_scalar(post[:, :], ps[:, 3, 0:NTB * NE], float(CH), 1.0, ALU.mult, ALU.add))
            link(dve.tensor_tensor(post[:, :], post[:, :], mask[:, :], ALU.mult))
            for b in range(3):
                ins = dve.tensor_scalar(posb[:, b * NTB * NE:(b + 1) * NTB * NE], post[:, :], 1.0, float(P * b),
                                        ALU.subtract, ALU.subtract)
            link(ins)
            link(dve.tensor_scalar(cnt_f[:, :], ps[:, 3, NTB * NE:(NTB + 1) * NE], float(CH), None, ALU.mult))
            dve.tensor_copy(cnt_i[:, :], cnt_f[:, :]).then_inc(S["cnt_ready"], 1)

            last = dve.alloc_register("residual_adds")
            dve.reg_mov(last, 18 + 6 * NE)

            def start(p, spec):
                f = Ffn(1, GEN_MOE, DENSE_UNITS, 0, NF * p)
                one_hot(*spec)
                if not (isinstance(p, int) and p == 0):
                    for kind in "gu":
                        tile_lo(f, kind, 0)
                dve_xT(spec[0])

            def finish(f, item):
                act_mul(f, NF - 1)
                tile_lo(f, "d", NF - 1)
                ft_low(f, NF - 1)
                dve_ye(item.n)
                add_expert((item.n, item.e, item.blk), range(6))
                if not isinstance(item.n, int):
                    dve.reg_add(last, last, 12)
            mixture(dve, start, dve_unit, finish)
            dve.wait_ge(S["x_added"], dve.snap(last, min_val=66, max_val=66 + 12 * NE))
            dve.memset(stat[:, 0:3], 0.0).then_inc(S["x_complete"], 1)
            dve_norm(4, "final_gain")

        @block.tensor
        def _(pe):
            def pe_hT(n):
                pe.wait_ge(S["h_ready"], NTB * (n + 1))
                for k in range(KD):
                    if k >= 2 or n:
                        pe.wait_ge(S["hT_lo"], KD * n + max(k - 1, 0))
                    for tb in range(NTB):
                        ins = pe.transpose(ps[:, 6 + k % 2, tb * P:(tb + 1) * P],
                                           h[:, tb * D + k * P:tb * D + (k + 1) * P], ident[:, :])
                    ins.then_inc(S["ht_done"], 1)

            def blk(ap, i, width=TOK):
                return ap[:, i * width:(i + 1) * width]

            pe.wait_ge(S["const_loaded"], 32)
            pe.wait_ge(S["prm_loaded"], 16 * 8)
            pe.transpose(ps[:, 0, 0:64], prm_rows[0:64, 0:P], ident[0:64, 0:64])
            for l in range(LAYERS):
                n = TAPS * NCB
                ins = pe.transpose(ps[:, 0, 64 + l * n:64 + (l + 1) * n], prm_rows[0:n, (1 + l) * P:(2 + l) * P],
                                   ident[0:n, 0:n])
            ins.then_inc(S["prm_turned"], 1)

            def unit_gu(f, l):
                c, tb = divmod(l, f.nb)
                if tb == 0:
                    for kind in "gu":
                        pe.wait_ge(lo_ready[f.slot(kind, c)], f.uses(kind, c) + 1)
                if not isinstance(f.K, int) or f.count(l - 1) > 0:
                    pe.wait_ge(S["ft_lo_ready"], f.count(l - 1))
                s = f.slot("g", c)
                out = ps[:, f.bank(l), :].rearrange("p (g n) -> p g n", g=2)

                def moving(w, k):
                    return w[:, s * TILE:(s + 2) * TILE].rearrange("p (g k n) -> p g k n", g=2, k=KD)[:, :, k, :]
                for k in range(KD):
                    o = k * TOK + tb * P if f.nb > 1 else k * P
                    ins = product(pe, out, a_hi[:, o:o + P], a_lo[:, o:o + P], moving(w_hi, k), moving(w_lo, k),
                                  k == 0, k == KD - 1)
                ins.then_inc(S["gu_done"], 1)

            def unit_turn(f, l):
                pe.wait_ge(S["act_done"], f.count(l + 1))
                for i in range(2):
                    ins = pe.transpose(ps[:, f.bank(l), i * P:(i + 1) * P], act_b[:, i * P:(i + 1) * P], ident[:, :])
                ins.then_inc(S["turned"], 1)

            def unit_down(f, l, shift):
                c, tb = divmod(l, f.nb)
                if tb == 0:
                    pe.wait_ge(lo_ready[f.slot("d", c)], f.uses("d", c) + 1)
                pe.wait_ge(S["ft_lo_ready"], f.count(l + 1))
                s = f.slot("d", c)
                b = f.buf(l)
                step = (c + shift) % NF
                for i in range(2):
                    o = b * FT + i * P
                    for dh in range(2):
                        m = s * TILE + i * D + dh * 512
                        ins = product(pe, ps[:, 2 * tb + dh, :], ft_hi[:, o:o + P], ft_lo[:, o:o + P],
                                      w_hi[:, m:m + 512], w_lo[:, m:m + 512],
                                      step == 0 and i == 0, step == NF - 1 and i == 1)
                ins.then_inc(S["down_done"], 1)

            def pe_unit(f, l, shift, item):
                static = isinstance(f.step, int)
                true = l + shift if item is not None and static else None
                prev = item is not None and item.prev is not None
                if true == 0:
                    pe.wait_ge(S["xT_lo"], 2 * item.n + 2)
                unit_gu(f, l)
                if true == 0:
                    turn_one_hot(item)
                if prev and true in SCATTER:
                    scatter(item.prev[0], 1 - item.parity, SCATTER[true])
                if l > 0 or prev:
                    unit_turn(f, l - 1)
                if l > 1 or prev:
                    if true == 2 and prev:
                        pe.wait_ge(S["ye_lo_ready"], 2 * item.prev[0] + 2)
                    unit_down(f, l - 2, shift)
                if true == 9 and item.nxt is not None:
                    gather(item.nxt[0])

            def turn_one_hot(item):
                pe.wait_ge(S["x_added"], 6 * item.n + (12 if item.prev is not None else 18))
                for tb in range(NTB):
                    ins = pe.transpose(ps[:, 4, tb * P:(tb + 1) * P], onehot[:, tb * P:(tb + 1) * P], ident[:, :])
                ins.then_inc(S["pt_turned"], 1)

            def gather(n):
                pe.wait_ge(S["onehot_ready"], n + 1)
                for i in range(2):
                    for k in range(4 * i, 4 * i + 4):
                        for tb in range(NTB):
                            ins = pe.matmul(ps[:, 2 + i, (k % 4) * P:(k % 4 + 1) * P],
                                            h[:, tb * D + k * P:tb * D + (k + 1) * P],
                                            onehot[:, tb * P:(tb + 1) * P], start=tb == 0, stop=tb == NTB - 1)
                    ins.then_inc(S["gathered"], 1)

            def scatter(n, parity, pieces):
                for i in pieces:
                    tb, dh = divmod(i, 2)
                    if i >= 2:
                        pe.wait_ge(S["x_added"], 6 * n + 18 + i - 1)
                    pe.matmul(ps[:, 4 + i % 2, :], pt[parity][:, tb * P:(tb + 1) * P],
                              ye_hi[:, dh * 512:dh * 512 + 512], start=True, stop=False)
                    pe.matmul(ps[:, 4 + i % 2, :], pt[parity][:, tb * P:(tb + 1) * P],
                              ye_lo[:, dh * 512:dh * 512 + 512], start=False, stop=True).then_inc(S["scattered"], 1)

            for l in range(LAYERS):
                pe_hT(2 * l)
                if l:
                    pe.wait_ge(S["x_added"], 12)
                pe.wait_ge(S["hist_loaded"], 32 * (l + 1))
                for c in range(NCB):
                    for g in range(3):
                        ins = pe.transpose(ps[:, 2 + c, g * 120:(g + 1) * 120],
                                           hist[0:120, g * CH + c * P:g * CH + (c + 1) * P], ident[0:120, 0:120])
                    ins.then_inc(S["hist_turned"], 1)
                pe.wait_ge(S["hT_lo"], KD * (2 * l + 1))
                if l == 0:
                    pe.wait_ge(S["prm_ready"], 1)

                def states(i):
                    for c in range(NCB):
                        ins = pe.transpose(ps[0:state_rows(i), ST_BANK[i], c * P:(c + 1) * P], state_cols(i, c),
                                           ident[:, :])
                    ins.then_inc(S["st_turned"], 1)
                for j in range(12):
                    s, m = divmod(j, 2)
                    if m == 0:
                        pe.wait_ge(lo_ready[s], GEN_WIN[l][s] + 1)
                    if j in (4, 5, 6, 7):
                        pe.wait_ge(S["p_done"], 8 * l + 2 * (j - 4) + 2)
                    if j in (8, 9):
                        pe.wait_ge(S["gated"], 4 * l + j - 7)
                    if j in (10, 11):
                        pe.wait_ge(S["sig_done"], 4 * l + j - 9)
                    for k in range(KD):
                        o = s * TILE + k * 256 + m * P
                        ins = product(pe, ps[:, WIN_BANK[j], 0:TOK], w_hi[:, o:o + P], w_lo[:, o:o + P],
                                      blk(a_hi, k), blk(a_lo, k), k == 0, k == KD - 1)
                    ins.then_inc(S["blk_done"], 1)
                    if j == 7:
                        pe.wait_ge(S["p_done"], 8 * (l + 1))
                        pe.wait_ge(S["hist_ready"], 2 * NCB * (l + 1))
                        for i in range(NPST):
                            if i == 2:
                                pe.wait_ge(S["st_copied"], NST * l + 1)
                            states(i)
                pe.wait_ge(S["gated"], 4 * (l + 1))
                pe.wait_ge(S["st_copied"], NST * l + NPST)
                for i, c in enumerate(PE_CONV):
                    for half in range(2):
                        for j in range(TAPS):
                            if half == 0:
                                pe.wait_ge(S["diag_ready"], (2 * l + i) * TAPS + j + 1)
                                out, src = ps[:, 2 + c, 0:SEQ], cext(c)[:, j:j + SEQ]
                            else:
                                out, src = streams(ps[:, 2 + c, SEQ:TOK]), c_sample(c, j, DSEQ)
                            ins = pe.matmul(out, diag[i][:, j * P:(j + 1) * P], src, start=j == 0, stop=j == TAPS - 1)
                    ins.then_inc(S["pe_conv_done"], 1)
                    if i == 0:
                        for n in range(NPST, NST):
                            states(n)
                pe.wait_ge(S["poolw_loaded"], 16 * (l + 1))
                for g in range(NCB):
                    pe.wait_ge(S["st_copied"], NST * l + NPST + g + 1)
                    pe.wait_ge(S["z_in"], 4 * l + g + 1)
                    pe.matmul(ps[:, Z_BANK[g], 0:SEQ], pool_w[:, g * P:(g + 1) * P],
                              pext(g)[:, PHIST:PHIST + SEQ], start=True, stop=True)
                    pe.matmul(streams(ps[:, Z_BANK[g], SEQ:TOK]), pool_w[:, g * P:(g + 1) * P],
                              p_sample(g, PHIST, DSEQ), start=True, stop=True).then_inc(S["z_done"], 1)

                def w_out(s, tb):
                    for i in range(2):
                        e = 2 * WOUT_TILES[s] + i
                        for dh in range(2):
                            o, m = e * TOK + tb * P, s * TILE + i * D + dh * 512
                            ins = product(pe, ps[:, 2 * tb + dh, :], a_hi[:, o:o + P], a_lo[:, o:o + P],
                                          w_hi[:, m:m + 512], w_lo[:, m:m + 512], s == 0 and i == 0, s == 3 and i == 1)
                    return ins

                pe.wait_ge(S["y_ready"], 4 * (l + 1))
                pe.wait_ge(S["z_lo"], 4 * (l + 1))
                pe.wait_ge(S["mean_w_ready"], 2)
                for c in range(NCB):
                    ins = pe.matmul(ps[:, 6, 0:TOK], mean_w[:, :], y_sb(c), start=c == 0, stop=c == NCB - 1)
                ins.then_inc(S["mean_done"], 1)
                pe.wait_ge(lo_ready[0], GEN_WOUT[l][0] + 1)
                for tb in range(NTB):
                    ins = w_out(0, tb)
                ins.then_inc(S["wout_used"], 1)
                pe.wait_ge(S["sq_done"], 4 * (l + 1))
                for c in range(NCB):
                    ins = pe.matmul(ps[:, 7, 0:TOK], mean_w[:, :], y_sq(c), start=c == 0, stop=c == NCB - 1)
                ins.then_inc(S["var_done"], 1)
                pe.wait_ge(lo_ready[1], GEN_WOUT[l][1] + 1)
                for tb in range(NTB):
                    ins = w_out(1, tb)
                ins.then_inc(S["wout_used"], 1)
                pe.wait_ge(S["c_lo"], 4 * (l + 1))
                for s in (2, 3):
                    pe.wait_ge(lo_ready[s], GEN_WOUT[l][s] + 1)
                for tb in range(NTB):
                    w_out(2, tb)
                    w_out(3, tb).then_inc(S["y_blk"], 1)
                pe.wait_ge(S["y_blk"], NTB * (l + 1))
                pe.sem_inc(S["wout_used"], 1)
                if l == 0:
                    pe_hT(1)
                    pe.wait_ge(S["x_added"], 6)
                    pe.wait_ge(S["hT_lo"], 2 * KD)
                    units_loop(pe, dense, lambda f, l, shift: pe_unit(f, l, shift, None))
                    unit_turn(dense, DENSE_UNITS - 1)
                    unit_down(dense, DENSE_UNITS - 2, 0)
                    unit_down(dense, DENSE_UNITS - 1, 0)
            pe_hT(3)
            pe.wait_ge(S["x_added"], 18)
            pe.wait_ge(S["hT_lo"], 4 * KD)
            pe.wait_ge(S["rw_lo_ready"], 1)
            for tb in range(NTB):
                for k in range(KD):
                    o = k * TOK + tb * P
                    ins = product(pe, ps[:, 2, tb * NE:(tb + 1) * NE], a_hi[:, o:o + P], a_lo[:, o:o + P],
                                  rw_hi[:, k * NE:(k + 1) * NE], rw_lo[:, k * NE:(k + 1) * NE], k == 0, k == KD - 1)
            ins.then_inc(S["logits_done"], 1)
            pe.wait_ge(S["mask_ready"], 1)
            pe.wait_ge(S["tri_loaded"], 16)
            for tb in range(NTB + 1):
                terms = [(mean_w, t) for t in range(min(tb, NTB))] + ([(tri, tb)] if tb < NTB else [])
                for i, (w, t) in enumerate(terms):
                    ins = pe.matmul(ps[:, 3, tb * NE:(tb + 1) * NE], w[:, :], mask[:, t * NE:(t + 1) * NE],
                                    start=i == 0, stop=i == len(terms) - 1)
            ins.then_inc(S["pos_done"], 1)
            pe.wait_ge(S["cnt_ready"], 1)

            def start(p, spec):
                gather(spec[0])

            def finish(f, item):
                unit_turn(f, NF - 1)
                unit_down(f, NF - 2, 0)
                unit_down(f, NF - 1, 0)
                pe.wait_ge(S["ye_lo_ready"], 2 * item.n + 2)
                scatter(item.n, item.parity, range(6))
            mixture(pe, start, pe_unit, finish)

        @block.gpsimd
        def _(pool):
            chain = [0]

            def link(ins):
                chain[0] += 1
                ins.then_inc(S["pool_chain"], 1)
                pool.wait_ge(S["pool_chain"], chain[0])

            def rsqrt(out, src, width, ready, n, done):
                pool.wait_ge(S[ready], n)
                pool.tensor_tensor(out, src, mhalf[:, 0:1].to_broadcast([P, width]), ALU.pow).then_inc(S[done], 1)

            def store(l, i):
                pooled, s0_, n = STATES[i]
                pool.wait_ge(S["st_copied"], NST * l + i + 1)
                rows, seg = (PHIST, PSEG) if pooled else (CHIST, CSEG)
                kind = "pool" if pooled else "conv"
                dst = a[f"new_{kind}_sample"][l] if n else a[f"new_{kind}_prompt"][l]
                b = (i - NPST) % 2
                src, done = (stage_p, "stp_stored") if pooled else (stage_c[:, b * CH:(b + 1) * CH], f"stc_stored{b}")
                for j in range(max(n, 1)):
                    pool.dma_start(dst[s0_ + j], src[j * seg:j * seg + rows, :]).then_inc(S[done], 16)

            pool.wait_ge(S["mhalf_ready"], 1)
            for l in range(LAYERS):
                rsqrt(stat[:, 6:9], stat[:, 3:6], 3, "ms_ready", 2 * l + 1, "rstd_ready")
                pool.wait_ge(S["ht_done"], KD * (2 * l + 1))
                pool.memset(ext[:, 0:NCB * CEXT].rearrange("p (c t) -> p c t", t=CEXT)[:, :, 0:CHIST], 0.0)\
                    .then_inc(S["ext_zeroed"], 1)
                pool.memset(ext[:, NCB * CEXT:].rearrange("p (c t) -> p c t", t=PEXT)[:, :, 0:PHIST], 0.0)\
                    .then_inc(S["ext_zeroed"], 1)
                pool.wait_ge(S["ext_zeroed"], 2 * l + 2)
                pool.wait_ge(S["p_done"], 8 * (l + 1))
                pool.wait_ge(S["hist_ready"], 2 * NCB * (l + 1))
                pool.wait_ge(S["const_loaded"], 32)
                pool.wait_ge(S["st_turned"], NST * l + NPST)
                for i in range(NPST):
                    store(l, i)
                for g in range(NCB):
                    w = 2 << g
                    for prompt in (True, False):
                        if prompt:
                            e = pext(g)[:, 0:PHIST + SEQ]
                            bufs = [win_a[:, 0:271], win_b[:, 0:271]]
                            sl = lambda ap, lo, hi: ap[:, lo:hi]
                            n = PHIST + SEQ
                        else:
                            e = pext(g)[:, PHIST + SEQ:].rearrange("p (s t) -> p s t", t=PSEG)
                            bufs = [b[:, 0:NSEQ * PSEG].rearrange("p (s t) -> p s t", t=PSEG) for b in (win_a, win_b)]
                            sl = lambda ap, lo, hi: ap[:, :, lo:hi]
                            n = PSEG
                        src, k = e, 1
                        for step in range(g + 1):
                            dst = bufs[step % 2]
                            link(pool.tensor_tensor(sl(dst, 2 * k - 1, n), sl(src, 2 * k - 1, n),
                                                    sl(src, k - 1, n - k), ALU.add))
                            src, k = dst, 2 * k
                        m = bufs[(g + 1) % 2]
                        link(pool.tensor_scalar(sl(m, PHIST, n), sl(src, PHIST, n), 1.0 / w, None, ALU.mult))
                        if prompt:
                            link(pool.tensor_tensor(m[:, PHIST:PHIST + w - 1], src[:, PHIST:PHIST + w - 1],
                                                    cinv[:, 0:w - 1], ALU.mult))
                        ins = pool.tensor_tensor(sl(e, PHIST, n), sl(m, PHIST, n), sl(e, PHIST, n), ALU.subtract)
                        if prompt:
                            link(ins)
                        else:
                            ins.then_inc(S["z_in"], 1)
                            pool.wait_ge(S["z_in"], 4 * l + g + 1)
                for i in range(NPST, NST):
                    store(l, i)
                if l == 0:
                    rsqrt(stat[:, 6:9], stat[:, 3:6], 3, "ms_ready", 2, "rstd_ready")
            pool.wait_ge(S["c_lo"], 4 * LAYERS)
            pool.dma_start(gbc, a["norm_ffn"][1:2, :].to_broadcast([P, D])).then_inc(S["gbc_loaded"], 16)
            pool.dma_start(iota, a["c_iota"]).then_inc(S["iota_loaded"], 16)
            for n in (4, 5):
                rsqrt(stat[:, 6:9], stat[:, 3:6], 3, "ms_ready", n, "rstd_ready")


_INS = ["x_prompt", "x_sample", "state_conv", "state_pool", "norm_mix", "w_in", "conv_w", "conv_b", "conv_ln_g",
        "conv_ln_b", "pool_w", "pool_scale", "w_out", "norm_ffn", "dense_w_gate", "dense_w_up", "dense_w_down",
        "router_w", "router_b", "moe_w_gate", "moe_w_up", "moe_w_down", "norm_final"]
_OUTS = [("y_prompt", (1, SEQ, D)), ("y_sample", (NSEQ, DSEQ, D)), ("new_conv_prompt", (LAYERS, 1, CHIST, CH)),
         ("new_pool_prompt", (LAYERS, 1, PHIST, CH)), ("new_conv_sample", (LAYERS, NSEQ, CHIST, CH)),
         ("new_pool_sample", (LAYERS, NSEQ, PHIST, CH))]


def constants():
    i = np.arange(P)
    e = np.arange(NE)
    return {
        "c_ident": np.eye(P, dtype=np.float32),
        "c_tri": ((i[:, None] < i[None, :]) / float(CH)).astype(np.float32),
        "c_iota": np.broadcast_to(i, (P, P)).astype(np.float32),
        "c_inv": np.broadcast_to(1.0 / (np.arange(16) + 1.0), (P, 16)).astype(np.float32),
        "c_low": np.broadcast_to((e[None, :] < e[:, None]).reshape(1, -1), (P, NE * NE)).astype(np.float32),
    }


def kernel(**inputs):
    import numpy as _np
    import concourse.bacc as _bacc
    from concourse import mybir as _mybir
    from concourse.bass_utils import run_bass_kernel_spmd as _run

    nc = _bacc.Bacc("TRN2", target_bir_lowering=False, num_devices=1)
    arrays, args = {}, {}
    for name, value in list((n, inputs[n]) for n in _INS) + list(constants().items()):
        v = _np.ascontiguousarray(value)
        arrays[f"in_{name}"] = v
        args[name] = nc.dram_tensor(f"in_{name}", v.shape, _mybir.dt.from_np(v.dtype), kind="ExternalInput").ap()
    for name, shape in _OUTS:
        args[name] = nc.dram_tensor(f"out_{name}", shape, _mybir.dt.float32, kind="ExternalOutput").ap()
    build(nc, args)
    r = _run(nc, [arrays], core_ids=[0])
    return tuple(r.results[0][f"out_{name}"] for name, _ in _OUTS)
```

```python
from contextlib import ExitStack

import numpy as np

import concourse.bass as bass
from concourse import mybir

F32 = mybir.dt.float32
F32R = mybir.dt.float32r
I32 = mybir.dt.int32
ALU = mybir.AluOpType
ACT = mybir.ActivationFunctionType
AXX = mybir.AxisListType.X

P = 128
D = 1024
KD = D // P
SEQ = 256
NSEQ, DSEQ = 8, 16
TOK = SEQ + NSEQ * DSEQ
NTB = TOK // P
CH = 512
NCB = CH // P
TAPS = 31
CHIST = TAPS - 1
PHIST = 15
FF = 2816
FT = 256
NF = FF // FT
NE = 8
EPS = 1e-6
LAYERS = 2
TILE = 2048
CSEG = CHIST + DSEQ
CEXT = CHIST + SEQ + NSEQ * CSEG
PSEG = PHIST + DSEQ
PEXT = PHIST + SEQ + NSEQ * PSEG
WIN = TOK

C_CB, C_LG, C_LB, C_PS, C_CW = 0, 8, 16, 24, 32
NPRM = C_CW + LAYERS * TAPS * NCB

WIN_TILES = [0, 2, 4, 5, 1, 3]
WIN_BANK = [0, 1, 6, 7] * 3
A_BLK, B_BLK, P_BLK = [0, 1, 8, 9], [2, 3, 10, 11], [4, 5, 6, 7]
WOUT_TILES = [2, 3, 0, 1]
WOUT_SLOT = [0, 1, 4, 5]
STATES = [(True, 0, 4), (True, 4, 4), (True, 0, 0), (False, 0, 3), (False, 3, 3), (False, 6, 2), (False, 0, 0)]
NST, NPST = len(STATES), 3
ST_BANK = [4, 5, 4, 6, 7, 0, 1]
PST_BUF = [0, 1, 1]
Z_BANK = [6, 7, 0, 1]
PE_CONV = [2, 3]


def state_stores(i):
    return max(STATES[i][2], 1)


def pst_stores(b):
    return sum(state_stores(i) for i in range(NPST) if PST_BUF[i] == b)


GEN_WIN = [[0] * 6, [8, 8, 7, 6, 7, 7]]
GEN_WOUT = [[1] * 4, [9, 9, 8, 8]]
GEN_DENSE = [2, 2, 1, 1, 2, 2]
GEN_MOE = [10, 10, 8, 7, 9, 9]

DENSE_UNITS = NF * NTB
PAIRS = NE // 2
SCATTER = {3: (0, 1), 4: (2, 3), 9: (4, 5)}


def build(nc, a):
    ctx = ExitStack()
    with ctx:
        base = 16512
        at = {}

        def place(name, floats, dt=F32, offset=None, parts=P):
            o = at["next"] if offset is None else offset
            t = nc.alloc_sbuf_tensor_at(name, [parts, floats], dt, offset=base + o)
            if offset is None:
                at["next"] = (o + floats * 4 + 31) // 32 * 32
            at[name] = o
            return t

        def sem(name):
            return ctx.enter_context(nc.semaphore(name))

        at["next"] = 0
        raw = place("raw", 6 * TILE)
        w_hi = place("w_hi", 6 * TILE, F32R)
        w_lo = place("w_lo", 6 * TILE, F32R)
        x = place("x", NTB * D)
        a_hi = place("a_hi", KD * TOK, F32R)
        a_lo = place("a_lo", KD * TOK, F32R)
        e_floats = NCB * (CEXT + PEXT)
        ext = place("ext", e_floats)
        ident = place("ident", P)
        mean_w = place("mean_w", P)
        prm = place("prm", NPRM)
        rw_hi = place("rw_hi", KD * NE, F32R)
        rw_lo = place("rw_lo", KD * NE, F32R)
        cinv = place("cinv", 16)
        stat = place("stat", 12)
        mhalf = place("mhalf", 1)
        eps = place("eps", 1)
        s0 = (at["next"] + 31) // 32 * 32
        hist = place("hist", 3 * CH, offset=s0)
        pool_w = place("pool_w", NCB * P, offset=s0)
        sgm = place("sgm", WIN, offset=s0 + 2048)
        win_a = place("win_a", 271, offset=s0 + 3584)
        win_b = place("win_b", 271, offset=s0 + 4704)
        stage_p = [place("stage_p0", CH, offset=s0 + 3584), place("stage_p1", CH, offset=s0)]
        stage_c = place("stage_c", 2 * CH, offset=s0 + 2048)
        prm_rows = place("prm_rows", 3 * P, offset=at["w_lo"] + 5 * TILE * 4)
        diag = [place("diag2", 32 * P, offset=at["w_hi"] + 2 * TILE * 4),
                place("diag3", 32 * P, offset=at["w_lo"] + 2 * TILE * 4)]
        ft_hi = place("ft_hi", 2 * FT, F32R, offset=s0)
        ft_lo = place("ft_lo", 2 * FT, F32R, offset=s0 + 2048)
        silu = place("silu", FT, offset=s0 + 4096)
        act_b = place("act_b", FT, offset=s0 + 5120)
        assert base + s0 + 6144 <= 229344
        oh, ol = at["a_hi"], at["a_lo"]
        pt = [place("pt0", NTB * P, F32R, offset=oh + 4096), place("pt1", NTB * P, F32R, offset=oh + 9728)]
        ye_hi = place("ye_hi", D, F32R, offset=oh + 5632)
        ye_lo = place("ye_lo", D, F32R, offset=ol + 5632)
        tri = place("tri", P, offset=s0)
        low = place("low", NE * NE, offset=s0 + 512)
        rb = place("rb", NE, offset=s0 + 768)
        cmp_gt = place("cmp_gt", NTB * NE * NE, offset=s0 + 1024)
        cmp_eq = place("cmp_eq", NTB * NE * NE, offset=s0 + 1792)
        rw_raw = place("rw_raw", KD * NE, offset=s0 + 2560)
        lg = place("lg", NTB * NE, offset=s0 + 2816)
        rank = place("rank", NTB * NE, offset=s0 + 2944)
        rmax = place("rmax", 2 * NTB, offset=s0 + 3072)
        rsum = place("rsum", 2 * NTB, offset=s0 + 3104)
        post = place("post", NTB * NE, offset=s0 + 3136)
        cnt_f = place("cnt_f", NE + 1, offset=s0 + 3264)
        lgt = place("lgt", TOK, offset=s0 + 4096)
        mask = place("mask", (NTB + 1) * NE, offset=ol + 9728)
        gate = place("gate", NTB * NE, offset=ol + 9856)
        posb = place("posb", 3 * NTB * NE, offset=ol + 9984)
        cnt_i = place("cnt_i", NE + 1, I32, offset=ol + 10272)
        h = ext[:, 0:NTB * D]
        onehot = ext[:, NTB * D:NTB * D + NTB * P]
        iota = ext[:, NTB * D + NTB * P + D:NTB * D + NTB * P + D + P]
        gbc = ext[:, NTB * D + NTB * P:NTB * D + NTB * P + D]

        ps = ctx.enter_context(nc.psum_tensor("ps", [P, 8, 512], F32))

        def cext(c):
            return ext[:, c * CEXT:(c + 1) * CEXT]

        def pext(g):
            o = NCB * CEXT + g * PEXT
            return ext[:, o:o + PEXT]

        def c_sample(c, off, n):
            return cext(c)[:, CHIST + SEQ:].rearrange("p (s t) -> p s t", t=CSEG)[:, :, off:off + n]

        def p_sample(g, off, n):
            return pext(g)[:, PHIST + SEQ:].rearrange("p (s t) -> p s t", t=PSEG)[:, :, off:off + n]

        def streams(ap):
            return ap.rearrange("p (s t) -> p s t", t=DSEQ)

        def y_sb(c):
            return ext[:, c * WIN:(c + 1) * WIN]

        def y_sq(c):
            o = NCB * CEXT + c * WIN
            return ext[:, o:o + WIN]

        def state_rows(i):
            pooled, _, n = STATES[i]
            rows, seg = (PHIST, PSEG) if pooled else (CHIST, CSEG)
            return rows + seg * max(n - 1, 0)

        def state_cols(i, c):
            pooled, s, n = STATES[i]
            e = pext(c) if pooled else cext(c)
            hist_n, seg = (PHIST, PSEG) if pooled else (CHIST, CSEG)
            o = SEQ if n == 0 else hist_n + SEQ + s * seg + DSEQ
            return e[:, o:o + state_rows(i)]

        S = {n: sem(n) for n in (
            "x_loaded0 x_loaded1 x_loaded2 const_loaded prm_loaded_sp prm_loaded_act prm_loaded_pool "
            "prm_turned prm_ready mean_w_ready mhalf_ready "
            "ssq_done ms_ready rstd_ready gbc_loaded h_ready ht_done hT_hi hT_lo "
            "blk_done sig_done gated p_done "
            "hist_loaded hist_turned hist_ready ext_zeroed "
            "st_turned st_copied stp_stored0 stp_stored1 stc_stored0 stc_stored1 "
            "conv_step conv_done diag_ready pe_conv_done y_ready "
            "mean_done xc_done sq_done var_done sd_ready xn_done c_done c_hi c_lo "
            "poolw_loaded z_in z_done z_hi z_lo "
            "wout_used y_blk x_added "
            "gu_done silu_done act_done turned ft_hi_ready ft_lo_ready down_done "
            "rw_loaded rw_hi_ready rw_lo_ready tri_loaded iota_loaded rb_loaded low_loaded "
            "logits_done lgt_ready lg_turned lg_ready exp_done mask_ready pos_done cnt_ready "
            "onehot_ready gathered xT_hi xT_lo pt_turned pt_ready ye_hi_ready ye_lo_ready scattered "
            "x_complete y_stored "
            "dve_chain pool_chain"
        ).split()}
        loaded = [sem(f"loaded{i}") for i in range(6)]
        hi_ready = [sem(f"hi_ready{i}") for i in range(6)]
        lo_ready = [sem(f"lo_ready{i}") for i in range(6)]

        def slot(t, i):
            return t[:, i * TILE:(i + 1) * TILE]

        def load(sp, s, uses, src, rows):
            if not isinstance(uses, int) or uses > 0:
                sp.wait_ge(lo_ready[s], uses)
            sp.dma_start(slot(raw, s).rearrange("p (k n) -> p k n", k=rows), src).then_inc(loaded[s], 16)

        def make_hi(act, s, uses):
            act.wait_ge(loaded[s], uses * 16 + 16)
            act.activation(slot(w_hi, s), slot(raw, s), ACT.Copy).then_inc(hi_ready[s], 1)

        def make_lo(dve, s, uses):
            dve.wait_ge(hi_ready[s], uses + 1)
            dve.tensor_tensor(slot(w_lo, s), slot(raw, s), slot(w_hi, s).bitcast(F32), ALU.subtract)\
               .then_inc(lo_ready[s], 1)

        def ht_bank(tb, half):
            return 2 * tb + half

        def ht_view(t, tb, half):
            four = t[:, half * 4 * TOK:(half + 1) * 4 * TOK].rearrange("p (k t) -> p k t", t=TOK)
            return four[:, :, tb * P:(tb + 1) * P]

        def ht_psum(tb, half):
            return ps[:, ht_bank(tb, half), :].rearrange("p (k t) -> p k t", t=P)

        def ht_count(n, tb, half):
            return 2 * (NTB * n + tb) + half + 1

        def product(pe, out, lh, ll, rh, rl, start, stop):
            pe.matmul(out, lh, rh, start=start, stop=False)
            pe.matmul(out, lh, rl, start=False, stop=False)
            return pe.matmul(out, ll, rh, start=False, stop=stop)

        class Ffn:
            def __init__(self, nb, gens, units, off, K):
                self.nb, self.gens, self.units, self.off, self.K = nb, gens, units, off, K
                self.step = 0

            def at(self, k):
                return Ffn(self.nb, self.gens, self.units, self.off, self.K + k)

            def slot(self, kind, c):
                return 3 * ((self.off + c) % 2) + "gud".index(kind)

            def uses(self, kind, c):
                return self.gens[self.slot(kind, c)] + (self.off + c) // 2 + self.K

            def count(self, l):
                return self.units + self.nb * self.off + l + 2 * self.nb * self.K

            def bank(self, l):
                return 6 + (self.nb * self.off + l) % 2

            def buf(self, l):
                return (self.nb * self.off + l) % 2

            def tiles(self, l):
                c, tb = divmod(l, self.nb)
                if self.nb == 1:
                    return [("g", c + 1), ("u", c + 1), ("d", c - 1)]
                return [[("d", c)], [("g", c + 1)], [("u", c + 1)]][tb]

            def units_of(self, first, n):
                return range(self.nb * first, self.nb * (first + n))

        moe_w = {"g": a["moe_w_gate"], "u": a["moe_w_up"], "d": a["moe_w_down"]}
        dense_w = {"g": a["dense_w_gate"], "u": a["dense_w_up"], "d": a["dense_w_down"]}

        def ffn_src(w, kind, e, c):
            m = w[kind][0]
            if len(m.shape) == 3:
                if kind == "d":
                    rows = m.rearrange("e (c k p) n -> (e c) p k n", p=P, k=2)
                    return rows[bass.ds(e * NF + c, 1)].rearrange("o p k n -> (o p) k n")
                m = m[bass.ds(e, 1)].rearrange("o a b -> (o a) b")
            if kind == "d":
                return m[bass.ds(c * FT, FT), :].rearrange("(k p) n -> p k n", p=P)
            return m.rearrange("(k p) n -> p k n", p=P)[:, :, bass.ds(c * FT, FT)]

        PRM_ROWS = [(c, a[name].rearrange("l (k p) -> (l k) p", p=P)) for c, name in (
            (C_CB, "conv_b"), (C_LG, "conv_ln_g"), (C_LB, "conv_ln_b"), (C_PS, "pool_scale"))]
        PRM_ACT = 1
        GAINS = [a["norm_mix"][0:1, :], a["norm_ffn"][0:1, :], a["norm_mix"][1:2, :], a["norm_ffn"][1:2, :],
                 a["norm_final"].rearrange("(o d) -> o d", o=1)]

        def sp_tile(sp, f, w, e, kind, c, c_expr):
            load(sp, f.slot(kind, c), f.uses(kind, c), ffn_src(w, kind, e, c_expr), 2 if kind == "d" else KD)

        def sp_dense(sp, f):
            for kind in "gu":
                sp_tile(sp, f, dense_w, 0, kind, 0, 0)

            def tiles(g, l, shift, k):
                for kind, c in g.tiles(l):
                    if c + shift < NF:
                        sp_tile(sp, g, dense_w, 0, kind, c, k + c)
            for l in f.units_of(0, 3):
                tiles(f, l, 0, 0)
            with sp.Fori(0, 3) as k:
                for l in f.units_of(3, 2):
                    tiles(f.at(k), l, 0, 2 * k)
            for l in f.units_of(3, 2):
                tiles(f.at(3), l, 6, 6)

        def units_loop(eng, f, fn):
            head = 3 if f.nb > 1 else 5
            rounds = (NF - head - 2) // 2
            for l in f.units_of(0, head):
                fn(f, l, 0)
            with eng.Fori(0, rounds) as k:
                for l in f.units_of(head, 2):
                    g = f.at(k)
                    g.step = 2 * k
                    fn(g, l, 0)
            for l in f.units_of(head, 2):
                fn(f.at(rounds), l, 2 * rounds)

        class Item:
            def __init__(self, n, e, blk, parity, prev, nxt):
                self.n, self.e, self.blk, self.parity, self.prev, self.nxt = n, e, blk, parity, prev, nxt

        def run_pair(eng, unit, p, spec, first, more):
            for b in range(2):
                prev = None if first and b == 0 else spec(b - 1)
                nxt = spec(b + 1) if more or b == 0 else None
                item = Item(*spec(b), b, prev, nxt)
                units_loop(eng, Ffn(1, GEN_MOE, DENSE_UNITS, NF * b, NF * p),
                           lambda f, l, shift: unit(f, l, shift, item))

        def wanted(f, kind, c, shift, item):
            if c + shift < 0:
                return item is not None and item.prev is not None
            if c + shift >= NF:
                return item is not None and item.nxt is not None
            return True

        def made_ahead(item, true):
            return item is not None and true == 0 and isinstance(item.n, int) and item.n == 0

        def mixture(eng, start, unit, finish):
            def pair(p, first, more):
                spec = lambda j: (2 * p + j, 2 * p + j, 0)
                if first:
                    start(p, spec(0))
                run_pair(eng, unit, p, spec, first, more)
                if not more:
                    finish(Ffn(1, GEN_MOE, DENSE_UNITS, NF, NF * p), Item(*spec(1), 1, None, None))
            pair(0, True, True)
            with eng.Fori(1, PAIRS - 1) as p:
                pair(p, False, True)
            pair(PAIRS - 1, False, False)

            def body(done, e):
                spec = lambda j: (2 * done + j, e, 1 + j)
                start(done, spec(0))
                run_pair(eng, unit, done, spec, True, False)
                finish(Ffn(1, GEN_MOE, DENSE_UNITS, NF, NF * done), Item(*spec(1), 1, None, None))
            overflow(eng, body)

        dense = Ffn(NTB, GEN_DENSE, 0, 0, 0)

        def overflow(eng, body):
            done = eng.alloc_register("pairs_done")
            eng.reg_mov(done, PAIRS)
            eng.wait_ge(S["cnt_ready"], 1)
            largest = eng.value_load(cnt_i[0:1, NE:NE + 1], min_val=0, max_val=TOK)
            with eng.If(largest > P):
                with eng.Fori(0, NE) as e:
                    n = eng.value_load(cnt_i[0:1, bass.ds(e, 1)], min_val=0, max_val=TOK)
                    with eng.If(n > P):
                        body(eng.snap(done, min_val=PAIRS, max_val=PAIRS + NE), e)
                        eng.reg_add(done, done, 1)

        block = ctx.enter_context(nc.Block())

        @block.sync
        def _(sp):
            def store(l, i):
                pooled, s0_, n = STATES[i]
                sp.wait_ge(S["st_copied"], NST * l + i + 1)
                rows, seg = (PHIST, PSEG) if pooled else (CHIST, CSEG)
                kind = "pool" if pooled else "conv"
                dst = a[f"new_{kind}_sample"][l] if n else a[f"new_{kind}_prompt"][l]
                b = PST_BUF[i] if pooled else (i - NPST) % 2
                src = stage_p[b] if pooled else stage_c[:, b * CH:(b + 1) * CH]
                done = f"stp_stored{b}" if pooled else f"stc_stored{b}"
                for j in range(max(n, 1)):
                    sp.dma_start(dst[s0_ + j], src[j * seg:j * seg + rows, :]).then_inc(S[done], 16)

            xp = a["x_prompt"][0].rearrange("(t p) d -> t p d", p=P)
            for tb, src in enumerate((xp[0], xp[1], a["x_sample"].rearrange("s t d -> (s t) d"))):
                sp.dma_start(x[:, tb * D:(tb + 1) * D], src).then_inc(S[f"x_loaded{tb}"], 16)
            for l in range(LAYERS):
                sp.dma_start(prm_rows[0:TAPS * NCB, (1 + l) * P:(2 + l) * P],
                             a["conv_w"][l].rearrange("j (c p) -> (j c) p", p=P)).then_inc(S["prm_loaded_sp"], 16)
            for l in range(LAYERS):
                w = a["w_in"][l].rearrange("(k p) n -> p k n", p=P)
                for s, t in enumerate(WIN_TILES):
                    load(sp, s, GEN_WIN[l][s], w[:, :, t * 256:(t + 1) * 256], KD)
                w = a["w_out"][l].rearrange("(t k p) n -> t p k n", p=P, k=2)
                for s, t in enumerate(WOUT_TILES):
                    load(sp, WOUT_SLOT[s], GEN_WOUT[l][s], w[t], 2)
                for i in range(NST):
                    store(l, i)
                if l == 0:
                    sp_dense(sp, dense)

            def start(p, spec):
                f = Ffn(1, GEN_MOE, DENSE_UNITS, 0, NF * p)
                for kind in "gu":
                    sp_tile(sp, f, moe_w, spec[1], kind, 0, 0)

            def unit(f, l, shift, item):
                for kind, c in f.tiles(l):
                    if wanted(f, kind, c, shift, item):
                        t = c + shift
                        e = item.prev[1] if t < 0 else item.nxt[1] if t >= NF else item.e
                        sp_tile(sp, f, moe_w, e, kind, c, f.step + t % NF if t != t % NF else f.step + t)

            def finish(f, item):
                sp_tile(sp, f, moe_w, item.e, "d", NF - 1, NF - 1)
            mixture(sp, start, unit, finish)

        def act_square(act, n, tb):
            if n == 0:
                act.wait_ge(S[f"x_loaded{tb}"], 16)
            elif n < 4:
                act.wait_ge(S["x_added"], 6 * (n - 1) + 2 * tb + 2)
            act.activation(ext[:, tb * D:(tb + 1) * D], x[:, tb * D:(tb + 1) * D], ACT.Square,
                           accum_out=stat[:, tb:tb + 1]).then_inc(S["ssq_done"], 1)

        def act_hT(act, n, tb):
            for half in range(2):
                act.wait_ge(S["ht_done"], ht_count(n, tb, half))
                act.activation(ht_view(a_hi, tb, half), ht_psum(tb, half), ACT.Copy).then_inc(S["hT_hi"], 1)

        def act_between(act, n):
            act_square(act, n, 0)
            act_square(act, n, 1)
            act_hT(act, n, 0)
            if n == 3:
                act.wait_ge(S["rw_loaded"], 16)
                act.activation(rw_hi[:, :], rw_raw[:, :], ACT.Copy).then_inc(S["rw_hi_ready"], 1)
            act_square(act, n, 2)
            act_hT(act, n, 1)
            act_hT(act, n, 2)

        def act_ffn_tile(act, f, kind, c):
            done = f.count(f.nb * (c - 1))
            if not isinstance(done, int) or done > 0:
                act.wait_ge(S["down_done" if kind == "d" else "gu_done"], done)
            make_hi(act, f.slot(kind, c), f.uses(kind, c))

        def act_silu(act, f, l):
            act.wait_ge(S["gu_done"], f.count(l + 1))
            if not isinstance(f.K, int) or f.count(l) > 0:
                act.wait_ge(S["act_done"], f.count(l))
            act.activation(silu[:, :], ps[:, f.bank(l), 0:FT], ACT.Silu).then_inc(S["silu_done"], 1)

        def act_ft(act, f, l):
            act.wait_ge(S["turned"], f.count(l + 1))
            if not isinstance(f.K, int) or f.count(l - 1) > 0:
                act.wait_ge(S["down_done"], f.count(l - 1))
            b = f.buf(l)
            act.activation(ft_hi[:, b * FT:(b + 1) * FT], ps[:, f.bank(l), 0:FT], ACT.Copy)\
               .then_inc(S["ft_hi_ready"], 1)

        def act_unit(act, f, l, shift, item):
            true = l + shift if item is not None and isinstance(f.step, int) else None
            prev = item is not None and item.prev is not None
            before = l > 0 or prev
            if true == 1:
                act.wait_ge(S["pt_turned"], item.n + 1)
                act.activation(pt[item.parity][:, :], ps[:, 4, 0:NTB * P], ACT.Copy).then_inc(S["pt_ready"], 1)
            if before:
                act_silu(act, f, l - 1)
            if true == 2 and prev:
                act_ye(act, f.count(0), item.prev[0])
            t = f.tiles(l)
            for i, (kind, c) in enumerate(t):
                if i == 2 and true == NF - 1 and item.nxt is not None:
                    act_xT(act, f.count(l + 1), item.nxt[0])
                if i == 2 and before:
                    act_ft(act, f, l - 1)
                if wanted(f, kind, c, shift, item) and not made_ahead(item, true):
                    act_ffn_tile(act, f, kind, c)
            if len(t) == 1 and before:
                act_ft(act, f, l - 1)

        def act_xT(act, done, n):
            act.wait_ge(S["gu_done"], done)
            for i in range(2):
                act.wait_ge(S["gathered"], 2 * n + i + 1)
                act.activation(a_hi[:, i * 512:(i + 1) * 512], ps[:, 2 + i, :], ACT.Copy).then_inc(S["xT_hi"], 1)

        def act_ye(act, done, n):
            act.wait_ge(S["down_done"], done)
            if not isinstance(n, int) or n > 0:
                act.wait_ge(S["scattered"], 6 * n)
            for i in range(2):
                act.activation(ye_hi[:, i * 512:(i + 1) * 512], ps[:, i, :], ACT.Copy).then_inc(S["ye_hi_ready"], 1)

        @block.scalar
        def _(act):
            act.dma_start(ident[:, :], a["c_ident"]).then_inc(S["const_loaded"], 16)
            act.dma_start(cinv[:, :], a["c_inv"]).then_inc(S["const_loaded"], 16)
            for r, rows in PRM_ROWS[:PRM_ACT]:
                act.dma_start(prm_rows[r:r + rows.shape[0], 0:P], rows).then_inc(S["prm_loaded_act"], 16)
            for l in range(LAYERS):
                if l:
                    act.wait_ge(S["gu_done"], DENSE_UNITS)
                    make_hi(act, 0, GEN_WIN[l][0])
                for tb in range(NTB):
                    act_square(act, 2 * l, tb)
                act_hT(act, 2 * l, 0)
                act_hT(act, 2 * l, 1)
                if l == 0:
                    make_hi(act, 0, GEN_WIN[l][0])
                act_hT(act, 2 * l, 2)
                if l == 0:
                    act.wait_ge(S["prm_turned"], 1)
                    act.activation(prm[:, :], ps[:, 6, 0:NPRM], ACT.Copy).then_inc(S["prm_ready"], 1)
                    act.wait_ge(S["prm_ready"], 1)
                for s in range(1, 4):
                    make_hi(act, s, GEN_WIN[l][s])
                for c in range(NCB):
                    act.wait_ge(S["hist_turned"], NCB * l + c + 1)
                    act.activation(c_sample(c, 0, CHIST), ps[:, 2 + c, 0:240].rearrange("p (s t) -> p s t", t=CHIST),
                                   ACT.Copy).then_inc(S["hist_ready"], 1)
                    act.activation(p_sample(c, 0, PHIST), ps[:, 2 + c, 240:360].rearrange("p (s t) -> p s t", t=PHIST),
                                   ACT.Copy).then_inc(S["hist_ready"], 1)
                for s in range(4, 6):
                    make_hi(act, s, GEN_WIN[l][s])

                def sigmoid(c):
                    act.wait_ge(S["blk_done"], 12 * l + B_BLK[c] + 1)
                    if 4 * l + c:
                        act.wait_ge(S["gated"], 4 * l + c)
                    act.activation(sgm[:, :], ps[:, WIN_BANK[B_BLK[c]], 0:TOK], ACT.Sigmoid)\
                       .then_inc(S["sig_done"], 1)

                def copy_state(i):
                    act.wait_ge(S["st_turned"], NST * l + i + 1)
                    b = PST_BUF[i]
                    stored = l * pst_stores(b) + sum(state_stores(n) for n in range(i) if PST_BUF[n] == b)
                    if stored:
                        act.wait_ge(S[f"stp_stored{b}"], 16 * stored)
                    act.activation(stage_p[b][0:state_rows(i), :], ps[0:state_rows(i), ST_BANK[i], 0:CH], ACT.Copy)\
                       .then_inc(S["st_copied"], 1)

                def diagonals(i, first, end):
                    c = PE_CONV[i]
                    for j in range(first, end):
                        col = C_CW + (l * TAPS + j) * NCB + c
                        act.activation(diag[i][:, j * P:(j + 1) * P], ident[:, :], ACT.Copy,
                                       scale=prm[:, col:col + 1]).then_inc(S["diag_ready"], 1)
                sigmoid(0)
                sigmoid(1)
                for s in range(2):
                    make_hi(act, WOUT_SLOT[s], GEN_WOUT[l][s])
                act.wait_ge(S["ext_zeroed"], 2 * l + 2)
                for g in range(NCB):
                    bank = WIN_BANK[P_BLK[g]]
                    act.wait_ge(S["blk_done"], 12 * l + P_BLK[g] + 1)
                    act.activation(pext(g)[:, PHIST:PHIST + SEQ], ps[:, bank, 0:SEQ], ACT.Copy)\
                       .then_inc(S["p_done"], 1)
                    act.activation(p_sample(g, PHIST, DSEQ), streams(ps[:, bank, SEQ:TOK]), ACT.Copy)\
                       .then_inc(S["p_done"], 1)
                diagonals(0, 0, 10)
                copy_state(0)
                copy_state(1)
                diagonals(0, 10, TAPS)
                sigmoid(2)
                copy_state(2)
                sigmoid(3)
                diagonals(1, 0, TAPS)
                act.wait_ge(S["stp_stored1"], 16 * (l + 1) * pst_stores(1))
                act.dma_start(pool_w[:, :].rearrange("p (g d) -> p g d", g=NCB),
                              a["pool_w"][l].rearrange("g c d -> c g d")).then_inc(S["poolw_loaded"], 16)
                for s in range(2, 4):
                    make_hi(act, WOUT_SLOT[s], GEN_WOUT[l][s])
                act.wait_ge(S["gated"], 4 * l + 4)
                act.wait_ge(S["z_in"], 4 * l + 4)
                count = [l * sum(state_stores(i) for i in range(NPST + b, NST, 2)) for b in range(2)]
                for i in range(NPST, NST):
                    n, b = state_rows(i), (i - NPST) % 2
                    act.wait_ge(S["st_turned"], NST * l + i + 1)
                    if count[b]:
                        act.wait_ge(S[f"stc_stored{b}"], 16 * count[b])
                    act.activation(stage_c[0:n, b * CH:(b + 1) * CH], ps[0:n, ST_BANK[i], 0:CH], ACT.Copy)\
                       .then_inc(S["st_copied"], 1)
                    count[b] += state_stores(i)
                for g in range(NCB):
                    act.wait_ge(S["z_done"], 4 * l + g + 1)
                    act.activation(a_hi[:, (4 + g) * TOK:(5 + g) * TOK], ps[:, Z_BANK[g], 0:TOK], ACT.Copy,
                                   scale=prm[:, C_PS + 4 * l + g:C_PS + 4 * l + g + 1]).then_inc(S["z_hi"], 1)
                act.wait_ge(S["conv_done"], 3 * (l + 1))
                for c in range(NCB):
                    if c in PE_CONV:
                        act.wait_ge(S["pe_conv_done"], 2 * l + PE_CONV.index(c) + 1)
                    bias = prm[:, C_CB + 4 * l + c:C_CB + 4 * l + c + 1]
                    if c in PE_CONV:
                        act.activation(y_sb(c)[:, 0:SEQ], ps[:, 2 + c, 0:SEQ], ACT.Identity, bias=bias)
                        act.activation(y_sb(c)[:, SEQ:TOK], ps[:, c, TOK:TOK + P], ACT.Identity, bias=bias)\
                           .then_inc(S["y_ready"], 1)
                    else:
                        act.activation(y_sb(c), ps[:, 2 + c, 0:TOK], ACT.Identity, bias=bias)\
                           .then_inc(S["y_ready"], 1)
                for c in range(NCB):
                    act.wait_ge(S["xc_done"], 4 * l + c + 1)
                    act.activation(y_sq(c), y_sb(c), ACT.Square).then_inc(S["sq_done"], 1)
                act.wait_ge(S["var_done"], l + 1)
                for b in range(2):
                    act.wait_ge(S[f"stc_stored{b}"], 16 * count[b])
                act.activation(sgm[:, :], ps[:, 7, 0:TOK], ACT.Sqrt, bias=eps[:, 0:1]).then_inc(S["sd_ready"], 1)
                for c in range(NCB):
                    act.wait_ge(S["xn_done"], 4 * l + c + 1)
                    act.activation(y_sb(c), y_sb(c), ACT.Silu, scale=prm[:, C_LG + 4 * l + c:C_LG + 4 * l + c + 1],
                                   bias=prm[:, C_LB + 4 * l + c:C_LB + 4 * l + c + 1]).then_inc(S["c_done"], 1)
                for c in range(NCB):
                    act.wait_ge(S["c_done"], 4 * l + c + 1)
                    act.activation(a_hi[:, c * TOK:(c + 1) * TOK], y_sb(c), ACT.Copy).then_inc(S["c_hi"], 1)
                if l == 0:
                    act.wait_ge(S["wout_used"], 2)
                    for kind in "gu":
                        act_ffn_tile(act, dense, kind, 0)
                    act_between(act, 1)
                    act.wait_ge(S["wout_used"], 3)
                    units_loop(act, dense, lambda f, l, shift: act_unit(act, f, l, shift, None))
                    act_silu(act, dense, DENSE_UNITS - 1)
                    act_ft(act, dense, DENSE_UNITS - 1)
            act.wait_ge(S["wout_used"], 5)
            for kind in "gu":
                act_ffn_tile(act, Ffn(1, GEN_MOE, DENSE_UNITS, 0, 0), kind, 0)
            act_between(act, 3)
            act.wait_ge(S["wout_used"], 6)
            for kind in "gu":
                act_ffn_tile(act, Ffn(1, GEN_MOE, DENSE_UNITS, 0, 0), kind, 1)
            act.wait_ge(S["lg_ready"], 1)
            for tb in range(NTB):
                act.activation(gate[:, tb * NE:(tb + 1) * NE], lg[:, tb * NE:(tb + 1) * NE], ACT.Exp,
                               bias=rmax[:, NTB + tb:NTB + tb + 1]).then_inc(S["exp_done"], 1)

            def start(p, spec):
                f = Ffn(1, GEN_MOE, DENSE_UNITS, 0, NF * p)
                if not (isinstance(p, int) and p == 0):
                    for kind in "gu":
                        act_ffn_tile(act, f, kind, 0)
                act_xT(act, f.count(0), spec[0])

            def finish(f, item):
                act_silu(act, f, NF - 1)
                act_ffn_tile(act, f, "d", NF - 1)
                act_ft(act, f, NF - 1)
                act_ye(act, f.count(NF), item.n)
            mixture(act, start, lambda f, l, shift, item: act_unit(act, f, l, shift, item), finish)
            act.wait_ge(S["x_complete"], 1)
            for tb in range(NTB):
                act_square(act, 4, tb)
            yp = a["y_prompt"][0].rearrange("(t p) d -> t p d", p=P)
            dst = [yp[0], yp[1], a["y_sample"].rearrange("s t d -> (s t) d")]
            for tb in range(NTB):
                act.wait_ge(S["h_ready"], 4 * NTB + tb + 1)
                act.dma_start(dst[tb], h[:, tb * D:(tb + 1) * D]).then_inc(S["y_stored"], 16)
            act.wait_ge(S["y_stored"], 16 * NTB)
            for b in range(2):
                act.wait_ge(S[f"stp_stored{b}"], 16 * LAYERS * pst_stores(b))
                act.wait_ge(S[f"stc_stored{b}"], 16 * LAYERS * sum(state_stores(i) for i in range(NPST + b, NST, 2)))

        @block.vector
        def _(dve):
            chain = [0]

            def link(ins):
                chain[0] += 1
                ins.then_inc(S["dve_chain"], 1)
                dve.wait_ge(S["dve_chain"], chain[0])

            def mean_square(n, tb):
                dve.wait_ge(S["ssq_done"], NTB * n + tb + 1)
                dve.tensor_scalar(stat[:, 3 + tb:4 + tb], stat[:, tb:tb + 1], 1.0 / D, EPS, ALU.mult, ALU.add)\
                   .then_inc(S["ms_ready"], 1)

            def norm_row(n, tb):
                dve.wait_ge(S["rstd_ready"], NTB * n + tb + 1)
                dve.wait_ge(S["gbc_loaded"], 16 * (n + 1))
                dve.scalar_tensor_tensor(out=h[:, tb * D:(tb + 1) * D], in0=x[:, tb * D:(tb + 1) * D],
                                         scalar=stat[:, 6 + tb:7 + tb], in1=gbc, op0=ALU.mult, op1=ALU.mult)\
                   .then_inc(S["h_ready"], 1)

            def dve_hT(n, tb):
                for half in range(2):
                    dve.wait_ge(S["hT_hi"], ht_count(n, tb, half))
                    dve.tensor_tensor(ht_view(a_lo, tb, half), ht_psum(tb, half), ht_view(a_hi, tb, half).bitcast(F32),
                                      ALU.subtract).then_inc(S["hT_lo"], 1)

            def gated(l, c):
                bank = WIN_BANK[A_BLK[c]]
                dve.wait_ge(S["sig_done"], 4 * l + c + 1)
                if c == 0:
                    dve.wait_ge(S["ext_zeroed"], 2 * l + 2)
                dve.tensor_tensor(cext(c)[:, CHIST:CHIST + SEQ], ps[:, bank, 0:SEQ], sgm[:, 0:SEQ], ALU.mult)
                dve.tensor_tensor(c_sample(c, CHIST, DSEQ), streams(ps[:, bank, SEQ:TOK]), streams(sgm[:, SEQ:TOK]),
                                  ALU.mult).then_inc(S["gated"], 1)

            steps = [0]

            def conv(l, jobs, first, end):
                if first == 0:
                    dve.wait_ge(S["gated"], 4 * l + max(c for c, _ in jobs) + 1)
                    dve.wait_ge(S["hist_ready"], 2 * NCB * (l + 1))
                for j in range(first, end):
                    for c, sample in jobs:
                        if not sample:
                            o, src = ps[:, 2 + c, 0:SEQ], cext(c)[:, j:j + SEQ]
                        else:
                            o = streams(ps[:, c, TOK:TOK + P] if c in PE_CONV else ps[:, 2 + c, SEQ:TOK])
                            src = c_sample(c, j, DSEQ)
                        col = C_CW + (l * TAPS + j) * NCB + c
                        w = prm[:, col:col + 1]
                        if j == 0:
                            ins = dve.tensor_scalar(o, src, w, None, ALU.mult)
                        else:
                            dve.wait_ge(S["conv_step"], steps[0] - len(jobs) + 1)
                            ins = dve.scalar_tensor_tensor(out=o, in0=src, scalar=w, in1=o, op0=ALU.mult, op1=ALU.add)
                        ins.then_inc(S["conv_step"], 1)
                        steps[0] += 1
                if end == TAPS:
                    dve.wait_ge(S["conv_step"], steps[0])
                    dve.sem_inc(S["conv_done"], 1)

            def tile_lo(f, kind, c):
                make_lo(dve, f.slot(kind, c), f.uses(kind, c))

            def act_mul(f, l):
                dve.wait_ge(S["silu_done"], f.count(l + 1))
                if not isinstance(f.K, int) or f.count(l) > 0:
                    dve.wait_ge(S["turned"], f.count(l))
                dve.tensor_tensor(act_b[:, :], ps[:, f.bank(l), FT:2 * FT], silu[:, :], ALU.mult)\
                   .then_inc(S["act_done"], 1)

            def ft_low(f, l):
                dve.wait_ge(S["ft_hi_ready"], f.count(l + 1))
                b = f.buf(l)
                dve.tensor_tensor(ft_lo[:, b * FT:(b + 1) * FT], ps[:, f.bank(l), 0:FT],
                                  ft_hi[:, b * FT:(b + 1) * FT].bitcast(F32), ALU.subtract)\
                   .then_inc(S["ft_lo_ready"], 1)

            def dve_unit(f, l, shift, item):
                true = l + shift if item is not None and isinstance(f.step, int) else None
                prev = item is not None and item.prev is not None
                before = l > 0 or prev
                if before:
                    act_mul(f, l - 1)
                if true == 2 and prev:
                    dve_ye(item.prev[0])
                if true == 1 and item.nxt is not None:
                    dve.wait_ge(S["pt_turned"], item.n + 1)
                    one_hot(*item.nxt)
                t = f.tiles(l)
                for i, (kind, c) in enumerate(t):
                    if i == 2 and true == NF - 1 and item.nxt is not None:
                        dve_xT(item.nxt[0])
                    if i == 2 and before:
                        ft_low(f, l - 1)
                    if wanted(f, kind, c, shift, item) and not made_ahead(item, true):
                        tile_lo(f, kind, c)
                if len(t) == 1 and before:
                    ft_low(f, l - 1)
                if prev and true in SCATTER:
                    add_expert(item.prev, SCATTER[true])

            def one_hot(n, e, blk):
                for tb in range(NTB):
                    ins = dve.tensor_scalar(onehot[:, tb * P:(tb + 1) * P], iota,
                                            posb[:, bass.ds(e + (blk * NTB * NE + tb * NE), 1)], None, ALU.is_equal)
                ins.then_inc(S["onehot_ready"], 1)

            def dve_xT(n):
                for i in range(2):
                    dve.wait_ge(S["xT_hi"], 2 * n + i + 1)
                    dve.tensor_tensor(a_lo[:, i * 512:(i + 1) * 512], ps[:, 2 + i, :],
                                      a_hi[:, i * 512:(i + 1) * 512].bitcast(F32), ALU.subtract).then_inc(S["xT_lo"], 1)

            def dve_ye(n):
                for i in range(2):
                    dve.wait_ge(S["ye_hi_ready"], 2 * n + i + 1)
                    dve.tensor_tensor(ye_lo[:, i * 512:(i + 1) * 512], ps[:, i, :],
                                      ye_hi[:, i * 512:(i + 1) * 512].bitcast(F32), ALU.subtract)\
                       .then_inc(S["ye_lo_ready"], 1)

            def add_expert(spec, pieces):
                n, e, _ = spec
                for i in pieces:
                    tb, dh = divmod(i, 2)
                    o = x[:, tb * D + dh * 512:tb * D + dh * 512 + 512]
                    dve.wait_ge(S["scattered"], 6 * n + i + 1)
                    dve.scalar_tensor_tensor(out=o, in0=ps[:, 4 + i % 2, :],
                                             scalar=gate[:, bass.ds(e + tb * NE, 1)], in1=o,
                                             op0=ALU.mult, op1=ALU.add).then_inc(S["x_added"], 1)

            def add_y(tb):
                for dh in range(2):
                    o = x[:, tb * D + dh * 512:tb * D + dh * 512 + 512]
                    dve.tensor_tensor(o, o, ps[:, 2 * tb + dh, :], ALU.add).then_inc(S["x_added"], 1)

            dve.memset(mean_w[:, :], 1.0 / CH).then_inc(S["mean_w_ready"], 1)
            dve.memset(eps[:, :], EPS).then_inc(S["mean_w_ready"], 1)
            dve.memset(mhalf[:, :], -0.5).then_inc(S["mhalf_ready"], 1)
            for l in range(LAYERS):
                n = 2 * l
                if l == 0:
                    for tb in range(NTB):
                        mean_square(n, tb)
                        norm_row(n, tb)
                        if tb == 1:
                            dve_hT(n, 0)
                    dve_hT(n, 1)
                    make_lo(dve, 0, GEN_WIN[l][0])
                    dve_hT(n, 2)
                    dve.wait_ge(S["prm_ready"], 1)
                else:
                    def add(tb):
                        dve.wait_ge(S["down_done"], DENSE_UNITS - NTB + tb + 1)
                        add_y(tb)
                    add(0)
                    add(1)
                    mean_square(n, 0)
                    norm_row(n, 0)
                    add(2)
                    mean_square(n, 1)
                    norm_row(n, 1)
                    mean_square(n, 2)
                    dve_hT(n, 0)
                    norm_row(n, 2)
                    dve_hT(n, 1)
                    make_lo(dve, 0, GEN_WIN[l][0])
                    dve_hT(n, 2)
                for s in range(1, 6):
                    make_lo(dve, s, GEN_WIN[l][s])
                gated(l, 0)
                gated(l, 1)
                conv(l, [(0, False), (0, True)], 0, 6)
                make_lo(dve, WOUT_SLOT[0], GEN_WOUT[l][0])
                conv(l, [(0, False), (0, True)], 6, TAPS)
                gated(l, 2)
                conv(l, [(1, False), (1, True)], 0, 7)
                gated(l, 3)
                conv(l, [(1, False), (1, True)], 7, TAPS)
                conv(l, [(2, True), (3, True)], 0, TAPS)
                for g in range(NCB):
                    dve.wait_ge(S["z_hi"], 4 * l + g + 1)
                    o = (4 + g) * TOK
                    dve.scalar_tensor_tensor(out=a_lo[:, o:o + TOK], in0=ps[:, Z_BANK[g], 0:TOK],
                                             scalar=prm[:, C_PS + 4 * l + g:C_PS + 4 * l + g + 1],
                                             in1=a_hi[:, o:o + TOK].bitcast(F32), op0=ALU.mult,
                                             op1=ALU.subtract).then_inc(S["z_lo"], 1)
                dve.wait_ge(S["mean_done"], l + 1)
                for c in range(NCB):
                    dve.tensor_tensor(y_sb(c), y_sb(c), ps[:, 6, 0:TOK], ALU.subtract).then_inc(S["xc_done"], 1)
                for s in range(1, 4):
                    make_lo(dve, WOUT_SLOT[s], GEN_WOUT[l][s])
                dve.wait_ge(S["sd_ready"], l + 1)
                link(dve.reciprocal(sgm[:, :], sgm[:, :]))
                dve.wait_ge(S["sq_done"], 4 * l + 4)
                for c in range(NCB):
                    dve.tensor_tensor(y_sb(c), y_sb(c), sgm[:, :], ALU.mult).then_inc(S["xn_done"], 1)
                for c in range(NCB):
                    dve.wait_ge(S["c_hi"], 4 * l + c + 1)
                    dve.tensor_tensor(a_lo[:, c * TOK:(c + 1) * TOK], y_sb(c),
                                      a_hi[:, c * TOK:(c + 1) * TOK].bitcast(F32), ALU.subtract).then_inc(S["c_lo"], 1)

                def add(tb):
                    dve.wait_ge(S["y_blk"], NTB * l + tb + 1)
                    add_y(tb)
                f = dense if l == 0 else Ffn(1, GEN_MOE, DENSE_UNITS, 0, 0)
                n = 2 * l + 1
                add(0)
                mean_square(n, 0)
                tile_lo(f, "g", 0)
                norm_row(n, 0)
                tile_lo(f, "u", 0)
                add(1)
                mean_square(n, 1)
                dve_hT(n, 0)
                norm_row(n, 1)
                add(2)
                mean_square(n, 2)
                dve_hT(n, 1)
                if l:
                    dve.wait_ge(S["rw_hi_ready"], 1)
                    dve.tensor_tensor(rw_lo[:, :], rw_raw[:, :], rw_hi[:, :].bitcast(F32), ALU.subtract)\
                       .then_inc(S["rw_lo_ready"], 1)
                norm_row(n, 2)
                dve_hT(n, 2)
                if l == 0:
                    units_loop(dve, dense, lambda f, l, shift: dve_unit(f, l, shift, None))
                    act_mul(dense, DENSE_UNITS - 1)
                    ft_low(dense, DENSE_UNITS - 1)
            first = Ffn(1, GEN_MOE, DENSE_UNITS, 0, 0)
            dve.wait_ge(S["logits_done"], 1)
            dve.tensor_copy(lgt[0:NE, :], ps[0:NE, 2, 0:TOK]).then_inc(S["lgt_ready"], 1)
            dve.memset(mask[:, NTB * NE:(NTB + 1) * NE], 0.0)
            dve.wait_ge(S["lg_turned"], 1)
            dve.wait_ge(S["rb_loaded"], 16)
            dve.wait_ge(S["low_loaded"], 16)
            for tb in range(NTB):
                cols = slice(tb * NE, (tb + 1) * NE)
                ins = dve.tensor_tensor(lg[:, cols], ps[:, 4, cols], rb[:, :], ALU.add)
            link(ins)
            link(dve.tensor_reduce(rmax[:, 0:NTB], lg[:, :].rearrange("p (t e) -> p t e", e=NE), AXX, ALU.max))
            dve.tensor_scalar(rmax[:, NTB:2 * NTB], rmax[:, 0:NTB], -1.0, None, ALU.mult).then_inc(S["lg_ready"], 1)
            m4 = lambda t: t[:, :].rearrange("p (t e j) -> p t e j", e=NE, j=NE)
            l3 = lg[:, :].rearrange("p (t e) -> p t e", e=NE)
            for tb in range(NTB):
                other = l3[:, tb].unsqueeze(1).to_broadcast([P, NE, NE])
                own = l3[:, tb].unsqueeze(2).to_broadcast([P, NE, NE])
                dve.tensor_tensor(m4(cmp_gt)[:, tb], other, own, ALU.is_gt)
                ins = dve.tensor_tensor(m4(cmp_eq)[:, tb], other, own, ALU.is_equal)
            link(ins)
            for tb in range(NTB):
                ins = dve.tensor_tensor(cmp_eq[:, tb * NE * NE:(tb + 1) * NE * NE],
                                        cmp_eq[:, tb * NE * NE:(tb + 1) * NE * NE], low[:, :], ALU.mult)
            link(ins)
            link(dve.tensor_tensor(cmp_gt[:, :], cmp_gt[:, :], cmp_eq[:, :], ALU.add))
            link(dve.tensor_reduce(rank[:, :], cmp_gt[:, :].rearrange("p (t j) -> p t j", j=NE), AXX, ALU.add))
            dve.tensor_scalar(mask[:, 0:NTB * NE], rank[:, :], 2.0, None, ALU.is_lt).then_inc(S["mask_ready"], 1)
            dve.wait_ge(S["mask_ready"], 1)
            dve.wait_ge(S["iota_loaded"], 16)
            dve.wait_ge(S["pos_done"], 1)
            link(dve.tensor_scalar(post[:, :], ps[:, 3, 0:NTB * NE], float(CH), 1.0, ALU.mult, ALU.add))
            link(dve.tensor_tensor(post[:, :], post[:, :], mask[:, 0:NTB * NE], ALU.mult))
            for b in range(3):
                ins = dve.tensor_scalar(posb[:, b * NTB * NE:(b + 1) * NTB * NE], post[:, :], 1.0, float(P * b),
                                        ALU.subtract, ALU.subtract)
            link(ins)
            link(dve.tensor_scalar(cnt_f[:, 0:NE], ps[:, 3, NTB * NE:(NTB + 1) * NE], float(CH), None, ALU.mult))
            link(dve.tensor_reduce(cnt_f[:, NE:NE + 1], cnt_f[:, 0:NE], AXX, ALU.max))
            dve.tensor_copy(cnt_i[:, :], cnt_f[:, :]).then_inc(S["cnt_ready"], 1)

            one_hot(0, 0, 0)
            dve.wait_ge(S["exp_done"], NTB)
            link(dve.tensor_tensor(gate[:, :], gate[:, :], mask[:, 0:NTB * NE], ALU.mult))
            link(dve.tensor_reduce(rsum[:, 0:NTB], gate[:, :].rearrange("p (t e) -> p t e", e=NE), AXX, ALU.add))
            link(dve.reciprocal(rsum[:, NTB:2 * NTB], rsum[:, 0:NTB]))
            for tb in range(NTB):
                ins = dve.tensor_scalar(gate[:, tb * NE:(tb + 1) * NE], gate[:, tb * NE:(tb + 1) * NE],
                                        rsum[:, NTB + tb:NTB + tb + 1], None, ALU.mult)
            link(ins)
            for kind in "gu":
                tile_lo(first, kind, 1)
            last = dve.alloc_register("residual_adds")
            dve.reg_mov(last, 18 + 6 * NE)

            def start(p, spec):
                f = Ffn(1, GEN_MOE, DENSE_UNITS, 0, NF * p)
                if not (isinstance(p, int) and p == 0):
                    one_hot(*spec)
                    for kind in "gu":
                        tile_lo(f, kind, 0)
                dve_xT(spec[0])

            def finish(f, item):
                act_mul(f, NF - 1)
                tile_lo(f, "d", NF - 1)
                ft_low(f, NF - 1)
                dve_ye(item.n)
                add_expert((item.n, item.e, item.blk), range(6))
                if not isinstance(item.n, int):
                    dve.reg_add(last, last, 12)
            mixture(dve, start, dve_unit, finish)
            dve.wait_ge(S["x_added"], dve.snap(last, min_val=66, max_val=66 + 12 * NE))
            dve.memset(stat[:, 0:3], 0.0).then_inc(S["x_complete"], 1)
            for tb in range(NTB):
                mean_square(4, tb)
                norm_row(4, tb)

        @block.tensor
        def _(pe):
            def pe_hT(n, blocks):
                for tb in blocks:
                    pe.wait_ge(S["h_ready"], NTB * n + tb + 1)
                    for half in range(2):
                        for k in range(4 * half, 4 * half + 4):
                            ins = pe.transpose(ps[:, ht_bank(tb, half), (k % 4) * P:(k % 4 + 1) * P],
                                               h[:, tb * D + k * P:tb * D + (k + 1) * P], ident[:, :])
                        ins.then_inc(S["ht_done"], 1)

            def blk(ap, i, width=TOK):
                return ap[:, i * width:(i + 1) * width]

            pe.wait_ge(S["const_loaded"], 32)

            def unit_gu(f, l):
                c, tb = divmod(l, f.nb)
                if tb == 0:
                    for kind in "gu":
                        pe.wait_ge(lo_ready[f.slot(kind, c)], f.uses(kind, c) + 1)
                if not isinstance(f.K, int) or f.count(l - 1) > 0:
                    pe.wait_ge(S["ft_lo_ready"], f.count(l - 1))
                s = f.slot("g", c)
                out = ps[:, f.bank(l), :].rearrange("p (g n) -> p g n", g=2)

                def moving(w, k):
                    return w[:, s * TILE:(s + 2) * TILE].rearrange("p (g k n) -> p g k n", g=2, k=KD)[:, :, k, :]
                for k in range(KD):
                    o = k * TOK + tb * P if f.nb > 1 else k * P
                    ins = product(pe, out, a_hi[:, o:o + P], a_lo[:, o:o + P], moving(w_hi, k), moving(w_lo, k),
                                  k == 0, k == KD - 1)
                ins.then_inc(S["gu_done"], 1)

            def unit_turn(f, l):
                pe.wait_ge(S["act_done"], f.count(l + 1))
                for i in range(2):
                    ins = pe.transpose(ps[:, f.bank(l), i * P:(i + 1) * P], act_b[:, i * P:(i + 1) * P], ident[:, :])
                ins.then_inc(S["turned"], 1)

            def unit_down(f, l, shift):
                c, tb = divmod(l, f.nb)
                if tb == 0:
                    pe.wait_ge(lo_ready[f.slot("d", c)], f.uses("d", c) + 1)
                pe.wait_ge(S["ft_lo_ready"], f.count(l + 1))
                s = f.slot("d", c)
                b = f.buf(l)
                step = (c + shift) % NF
                for i in range(2):
                    o = b * FT + i * P
                    for dh in range(2):
                        m = s * TILE + i * D + dh * 512
                        ins = product(pe, ps[:, 2 * tb + dh, :], ft_hi[:, o:o + P], ft_lo[:, o:o + P],
                                      w_hi[:, m:m + 512], w_lo[:, m:m + 512],
                                      step == 0 and i == 0, step == NF - 1 and i == 1)
                ins.then_inc(S["down_done"], 1)

            def pe_unit(f, l, shift, item):
                static = isinstance(f.step, int)
                true = l + shift if item is not None and static else None
                prev = item is not None and item.prev is not None
                if true == 0:
                    pe.wait_ge(S["xT_lo"], 2 * item.n + 2)
                unit_gu(f, l)
                if true == 0:
                    turn_one_hot(item)
                if prev and true in SCATTER:
                    scatter(item.prev[0], 1 - item.parity, SCATTER[true])
                if l > 0 or prev:
                    unit_turn(f, l - 1)
                if l > 1 or prev:
                    if true == 2 and prev:
                        pe.wait_ge(S["ye_lo_ready"], 2 * item.prev[0] + 2)
                    unit_down(f, l - 2, shift)
                if true == 9 and item.nxt is not None:
                    gather(item.nxt[0])

            def turn_one_hot(item):
                pe.wait_ge(S["x_added"], 6 * item.n + (12 if item.prev is not None else 18))
                for tb in range(NTB):
                    ins = pe.transpose(ps[:, 4, tb * P:(tb + 1) * P], onehot[:, tb * P:(tb + 1) * P], ident[:, :])
                ins.then_inc(S["pt_turned"], 1)

            def gather(n):
                pe.wait_ge(S["onehot_ready"], n + 1)
                for i in range(2):
                    for k in range(4 * i, 4 * i + 4):
                        for tb in range(NTB):
                            ins = pe.matmul(ps[:, 2 + i, (k % 4) * P:(k % 4 + 1) * P],
                                            h[:, tb * D + k * P:tb * D + (k + 1) * P],
                                            onehot[:, tb * P:(tb + 1) * P], start=tb == 0, stop=tb == NTB - 1)
                    ins.then_inc(S["gathered"], 1)

            def scatter(n, parity, pieces):
                for i in pieces:
                    tb, dh = divmod(i, 2)
                    if i >= 2:
                        pe.wait_ge(S["x_added"], 6 * n + 18 + i - 1)
                    pe.matmul(ps[:, 4 + i % 2, :], pt[parity][:, tb * P:(tb + 1) * P],
                              ye_hi[:, dh * 512:dh * 512 + 512], start=True, stop=False)
                    pe.matmul(ps[:, 4 + i % 2, :], pt[parity][:, tb * P:(tb + 1) * P],
                              ye_lo[:, dh * 512:dh * 512 + 512], start=False, stop=True).then_inc(S["scattered"], 1)

            for l in range(LAYERS):
                pe_hT(2 * l, range(NTB))
                if l == 0:
                    pe.wait_ge(S["prm_loaded_sp"], 16 * LAYERS)
                    pe.wait_ge(S["prm_loaded_act"], 16 * PRM_ACT)
                    pe.wait_ge(S["prm_loaded_pool"], 16 * (len(PRM_ROWS) - PRM_ACT))
                    pe.transpose(ps[:, 6, 0:C_CW], prm_rows[0:C_CW, 0:P], ident[0:C_CW, 0:C_CW])
                    for i in range(LAYERS):
                        n = TAPS * NCB
                        ins = pe.transpose(ps[:, 6, C_CW + i * n:C_CW + (i + 1) * n],
                                           prm_rows[0:n, (1 + i) * P:(2 + i) * P], ident[0:n, 0:n])
                    ins.then_inc(S["prm_turned"], 1)
                pe.wait_ge(S["hT_lo"], ht_count(2 * l, 2, 1))

                def states(i):
                    for c in range(NCB):
                        ins = pe.transpose(ps[0:state_rows(i), ST_BANK[i], c * P:(c + 1) * P], state_cols(i, c),
                                           ident[:, :])
                    ins.then_inc(S["st_turned"], 1)
                for j in range(12):
                    s, m = divmod(j, 2)
                    if m == 0:
                        pe.wait_ge(lo_ready[s], GEN_WIN[l][s] + 1)
                    if j in (4, 5):
                        pe.wait_ge(S["gated"], 4 * l + j - 3)
                    if j in (6, 7):
                        pe.wait_ge(S["sig_done"], 4 * l + j - 5)
                    if j >= 8:
                        pe.wait_ge(S["p_done"], 8 * l + 2 * (j - 8) + 2)
                    for k in range(KD):
                        o = s * TILE + k * 256 + m * P
                        ins = product(pe, ps[:, WIN_BANK[j], 0:TOK], w_hi[:, o:o + P], w_lo[:, o:o + P],
                                      blk(a_hi, k), blk(a_lo, k), k == 0, k == KD - 1)
                    ins.then_inc(S["blk_done"], 1)
                    if j == 1:
                        if l:
                            pe.wait_ge(S["x_added"], 12)
                        else:
                            pe.wait_ge(S["prm_ready"], 1)
                        pe.wait_ge(S["hist_loaded"], 32 * (l + 1))
                        for c in range(NCB):
                            for g in range(3):
                                rows = hist[0:120, g * CH + c * P:g * CH + (c + 1) * P]
                                ins = pe.transpose(ps[:, 2 + c, g * 120:(g + 1) * 120], rows, ident[0:120, 0:120])
                            ins.then_inc(S["hist_turned"], 1)
                    if j == 8:
                        pe.wait_ge(S["p_done"], 8 * (l + 1))
                        pe.wait_ge(S["hist_ready"], 2 * NCB * (l + 1))
                        states(0)
                        states(1)
                    if j == 9:
                        pe.wait_ge(S["st_copied"], NST * l + 1)
                        states(2)
                pe.wait_ge(S["st_copied"], NST * l + NPST)

                def conv(i, first, end):
                    c = PE_CONV[i]
                    pe.wait_ge(S["gated"], 4 * l + c + 1)
                    for j in range(first, end):
                        pe.wait_ge(S["diag_ready"], (2 * l + i) * TAPS + j + 1)
                        ins = pe.matmul(ps[:, 2 + c, 0:SEQ], diag[i][:, j * P:(j + 1) * P], cext(c)[:, j:j + SEQ],
                                        start=j == 0, stop=j == TAPS - 1)
                    if end == TAPS:
                        ins.then_inc(S["pe_conv_done"], 1)
                conv(0, 0, TAPS)
                pe.wait_ge(S["gated"], 4 * (l + 1))
                for n in range(NPST, NST):
                    states(n)
                conv(1, 0, 20)
                pe.wait_ge(S["poolw_loaded"], 16 * (l + 1))
                for g in range(NCB):
                    pe.wait_ge(S["st_copied"], NST * l + NPST + g + 1)
                    pe.wait_ge(S["z_in"], 4 * l + g + 1)
                    pe.matmul(ps[:, Z_BANK[g], 0:SEQ], pool_w[:, g * P:(g + 1) * P],
                              pext(g)[:, PHIST:PHIST + SEQ], start=True, stop=True)
                    pe.matmul(streams(ps[:, Z_BANK[g], SEQ:TOK]), pool_w[:, g * P:(g + 1) * P],
                              p_sample(g, PHIST, DSEQ), start=True, stop=True).then_inc(S["z_done"], 1)
                conv(1, 20, TAPS)

                def w_out(s, tb):
                    for i in range(2):
                        e = 2 * WOUT_TILES[s] + i
                        for dh in range(2):
                            o, m = e * TOK + tb * P, WOUT_SLOT[s] * TILE + i * D + dh * 512
                            ins = product(pe, ps[:, 2 * tb + dh, :], a_hi[:, o:o + P], a_lo[:, o:o + P],
                                          w_hi[:, m:m + 512], w_lo[:, m:m + 512], s == 0 and i == 0, s == 3 and i == 1)
                    return ins

                pe.wait_ge(S["mean_w_ready"], 2)
                pe.wait_ge(S["z_lo"], 4 * l + 1)
                for c in range(NCB):
                    pe.wait_ge(S["y_ready"], 4 * l + c + 1)
                    ins = pe.matmul(ps[:, 6, 0:TOK], mean_w[:, :], y_sb(c), start=c == 0, stop=c == NCB - 1)
                ins.then_inc(S["mean_done"], 1)
                pe.wait_ge(S["z_lo"], 4 * (l + 1))
                pe.wait_ge(lo_ready[WOUT_SLOT[0]], GEN_WOUT[l][0] + 1)
                for tb in range(NTB):
                    ins = w_out(0, tb)
                ins.then_inc(S["wout_used"], 1)
                pe.wait_ge(S["sq_done"], 4 * (l + 1))
                for c in range(NCB):
                    ins = pe.matmul(ps[:, 7, 0:TOK], mean_w[:, :], y_sq(c), start=c == 0, stop=c == NCB - 1)
                ins.then_inc(S["var_done"], 1)
                pe.wait_ge(lo_ready[WOUT_SLOT[1]], GEN_WOUT[l][1] + 1)
                for tb in range(NTB):
                    ins = w_out(1, tb)
                ins.then_inc(S["wout_used"], 1)
                pe.wait_ge(S["c_lo"], 4 * (l + 1))
                for s in (2, 3):
                    pe.wait_ge(lo_ready[WOUT_SLOT[s]], GEN_WOUT[l][s] + 1)
                for tb in range(NTB):
                    if tb == 2:
                        pe_hT(2 * l + 1, [0])
                    w_out(2, tb)
                    w_out(3, tb).then_inc(S["y_blk"], 1)
                pe.wait_ge(S["y_blk"], NTB * (l + 1))
                pe.sem_inc(S["wout_used"], 1)
                if l == 0:
                    pe_hT(1, [1])

                    def dense_unit(f, l, shift):
                        if l < NTB and shift == 0 and isinstance(f.step, int):
                            if l == 1:
                                pe_hT(1, [2])
                            if l == 2:
                                pe.wait_ge(S["x_added"], 6)
                            pe.wait_ge(S["hT_lo"], ht_count(1, l, 1))
                        pe_unit(f, l, shift, None)
                    units_loop(pe, dense, dense_unit)
                    unit_turn(dense, DENSE_UNITS - 1)
                    unit_down(dense, DENSE_UNITS - 2, 0)
                    unit_down(dense, DENSE_UNITS - 1, 0)
            pe_hT(3, [1, 2])
            pe.wait_ge(S["x_added"], 18)
            pe.wait_ge(S["hT_lo"], ht_count(3, 2, 1))
            pe.wait_ge(S["rw_lo_ready"], 1)
            for k in range(KD):
                ins = product(pe, ps[0:NE, 2, 0:TOK], rw_hi[:, k * NE:(k + 1) * NE], rw_lo[:, k * NE:(k + 1) * NE],
                              blk(a_hi, k), blk(a_lo, k), k == 0, k == KD - 1)
            ins.then_inc(S["logits_done"], 1)
            pe.wait_ge(S["lgt_ready"], 1)
            for tb in range(NTB):
                ins = pe.transpose(ps[:, 4, tb * NE:(tb + 1) * NE], lgt[0:NE, tb * P:(tb + 1) * P], ident[0:NE, 0:NE])
            ins.then_inc(S["lg_turned"], 1)
            pe.wait_ge(S["mask_ready"], 1)
            pe.wait_ge(S["tri_loaded"], 16)
            pe.matmul(ps[:, 3, 0:(NTB + 1) * NE], tri[:, :], mask[:, :], start=True, stop=False)
            for tb in range(NTB):
                ins = pe.matmul(ps[:, 3, (tb + 1) * NE:(NTB + 1) * NE], mean_w[:, :], mask[:, 0:(NTB - tb) * NE],
                                start=False, stop=tb == NTB - 1)
            ins.then_inc(S["pos_done"], 1)
            pe.wait_ge(S["cnt_ready"], 1)

            def start(p, spec):
                gather(spec[0])

            def finish(f, item):
                unit_turn(f, NF - 1)
                unit_down(f, NF - 2, 0)
                unit_down(f, NF - 1, 0)
                pe.wait_ge(S["ye_lo_ready"], 2 * item.n + 2)
                scatter(item.n, item.parity, range(6))
            mixture(pe, start, pe_unit, finish)

        @block.gpsimd
        def _(pool):
            chain = [0]

            def link(ins):
                chain[0] += 1
                ins.then_inc(S["pool_chain"], 1)
                pool.wait_ge(S["pool_chain"], chain[0])

            def rsqrt(out, src, width, ready, n, done):
                pool.wait_ge(S[ready], n)
                pool.tensor_tensor(out, src, mhalf[:, 0:1].to_broadcast([P, width]), ALU.pow).then_inc(S[done], 1)

            pool.dma_start(gbc, GAINS[0].to_broadcast([P, D])).then_inc(S["gbc_loaded"], 16)
            for r, rows in PRM_ROWS[PRM_ACT:]:
                pool.dma_start(prm_rows[r:r + rows.shape[0], 0:P], rows).then_inc(S["prm_loaded_pool"], 16)

            def scales(n, first=0):
                for tb in range(first, NTB):
                    rsqrt(stat[:, 6 + tb:7 + tb], stat[:, 3 + tb:4 + tb], 1, "ms_ready", NTB * n + tb + 1, "rstd_ready")

            def load_gain(n):
                pool.dma_start(gbc, GAINS[n].to_broadcast([P, D])).then_inc(S["gbc_loaded"], 16)

            def load_history(l):
                pool.dma_start(hist[0:120, 0:2 * CH].rearrange("p (g c) -> p g c", g=2),
                               a["state_conv"][l].rearrange("(g s) t c -> (s t) g c", g=2))\
                    .then_inc(S["hist_loaded"], 16)
                pool.dma_start(hist[0:120, 2 * CH:3 * CH], a["state_pool"][l].rearrange("s t c -> (s t) c"))\
                    .then_inc(S["hist_loaded"], 16)

            pool.wait_ge(S["mhalf_ready"], 1)
            for l in range(LAYERS):
                if l == 0:
                    rsqrt(stat[:, 6:7], stat[:, 3:4], 1, "ms_ready", 1, "rstd_ready")
                    load_history(0)
                    scales(0, 1)
                else:
                    scales(2)
                    pool.wait_ge(S["down_done"], DENSE_UNITS)
                    load_history(1)
                pool.wait_ge(S["ht_done"], ht_count(2 * l, 2, 1))
                pool.memset(ext[:, 0:NCB * CEXT].rearrange("p (c t) -> p c t", t=CEXT)[:, :, 0:CHIST], 0.0)\
                    .then_inc(S["ext_zeroed"], 1)
                pool.memset(ext[:, NCB * CEXT:].rearrange("p (c t) -> p c t", t=PEXT)[:, :, 0:PHIST], 0.0)\
                    .then_inc(S["ext_zeroed"], 1)
                pool.wait_ge(S["ext_zeroed"], 2 * l + 2)
                pool.wait_ge(S["p_done"], 8 * (l + 1))
                pool.wait_ge(S["hist_ready"], 2 * NCB * (l + 1))
                pool.wait_ge(S["const_loaded"], 32)
                pool.wait_ge(S["st_turned"], NST * l + NPST)
                pool.wait_ge(S["stp_stored0"], 16 * (l + 1) * pst_stores(0))
                for g in range(NCB):
                    w = 2 << g
                    for prompt in (True, False):
                        if prompt:
                            e = pext(g)[:, 0:PHIST + SEQ]
                            bufs = [win_a[:, 0:271], win_b[:, 0:271]]
                            sl = lambda ap, lo, hi: ap[:, lo:hi]
                            n = PHIST + SEQ
                        else:
                            e = pext(g)[:, PHIST + SEQ:].rearrange("p (s t) -> p s t", t=PSEG)
                            bufs = [b[:, 0:NSEQ * PSEG].rearrange("p (s t) -> p s t", t=PSEG) for b in (win_a, win_b)]
                            sl = lambda ap, lo, hi: ap[:, :, lo:hi]
                            n = PSEG
                        src, k = e, 1
                        for step in range(g + 1):
                            dst = bufs[step % 2]
                            link(pool.tensor_tensor(sl(dst, 2 * k - 1, n), sl(src, 2 * k - 1, n),
                                                    sl(src, k - 1, n - k), ALU.add))
                            src, k = dst, 2 * k
                        m = bufs[(g + 1) % 2]
                        link(pool.tensor_scalar(sl(m, PHIST, n), sl(src, PHIST, n), 1.0 / w, None, ALU.mult))
                        if prompt:
                            link(pool.tensor_tensor(m[:, PHIST:PHIST + w - 1], src[:, PHIST:PHIST + w - 1],
                                                    cinv[:, 0:w - 1], ALU.mult))
                        ins = pool.tensor_tensor(sl(e, PHIST, n), sl(m, PHIST, n), sl(e, PHIST, n), ALU.subtract)
                        if prompt:
                            link(ins)
                        else:
                            ins.then_inc(S["z_in"], 1)
                            pool.wait_ge(S["z_in"], 4 * l + g + 1)
                pool.wait_ge(S["var_done"], l + 1)
                load_gain(2 * l + 1)
                if l == LAYERS - 1:
                    pool.dma_start(iota, a["c_iota"]).then_inc(S["iota_loaded"], 16)
                    pool.wait_ge(S["c_lo"], 4 * LAYERS)
                    pool.dma_start(rw_raw[:, :].rearrange("p (k e) -> p k e", k=KD),
                                  a["router_w"][0].rearrange("(k p) e -> p k e", p=P)).then_inc(S["rw_loaded"], 16)
                    pool.dma_start(tri[:, :], a["c_tri"]).then_inc(S["tri_loaded"], 16)
                    pool.dma_start(low[:, :], a["c_low"]).then_inc(S["low_loaded"], 16)
                    pool.dma_start(rb[:, :], a["router_b"].to_broadcast([P, NE])).then_inc(S["rb_loaded"], 16)
                scales(2 * l + 1)
                pool.wait_ge(S["h_ready"], NTB * (2 * l + 2))
                load_gain(2 * l + 2)
            scales(4)


_INS = ["x_prompt", "x_sample", "state_conv", "state_pool", "norm_mix", "w_in", "conv_w", "conv_b", "conv_ln_g",
        "conv_ln_b", "pool_w", "pool_scale", "w_out", "norm_ffn", "dense_w_gate", "dense_w_up", "dense_w_down",
        "router_w", "router_b", "moe_w_gate", "moe_w_up", "moe_w_down", "norm_final"]
_OUTS = [("y_prompt", (1, SEQ, D)), ("y_sample", (NSEQ, DSEQ, D)), ("new_conv_prompt", (LAYERS, 1, CHIST, CH)),
         ("new_pool_prompt", (LAYERS, 1, PHIST, CH)), ("new_conv_sample", (LAYERS, NSEQ, CHIST, CH)),
         ("new_pool_sample", (LAYERS, NSEQ, PHIST, CH))]


def constants():
    i = np.arange(P)
    e = np.arange(NE)
    return {
        "c_ident": np.eye(P, dtype=np.float32),
        "c_tri": ((i[:, None] < i[None, :]) / float(CH)).astype(np.float32),
        "c_iota": np.broadcast_to(i, (P, P)).astype(np.float32),
        "c_inv": np.broadcast_to(1.0 / (np.arange(16) + 1.0), (P, 16)).astype(np.float32),
        "c_low": np.broadcast_to((e[None, :] < e[:, None]).reshape(1, -1), (P, NE * NE)).astype(np.float32),
    }


def kernel(**inputs):
    import numpy as _np
    import concourse.bacc as _bacc
    from concourse import mybir as _mybir
    from concourse.bass_utils import run_bass_kernel_spmd as _run

    nc = _bacc.Bacc("TRN2", target_bir_lowering=False, num_devices=1)
    arrays, args = {}, {}
    for name, value in list((n, inputs[n]) for n in _INS) + list(constants().items()):
        v = _np.ascontiguousarray(value)
        arrays[f"in_{name}"] = v
        args[name] = nc.dram_tensor(f"in_{name}", v.shape, _mybir.dt.from_np(v.dtype), kind="ExternalInput").ap()
    for name, shape in _OUTS:
        args[name] = nc.dram_tensor(f"out_{name}", shape, _mybir.dt.float32, kind="ExternalOutput").ap()
    build(nc, args)
    r = _run(nc, [arrays], core_ids=[0])
    return tuple(r.results[0][f"out_{name}"] for name, _ in _OUTS)
```
